# Optimizing a Trainium2 kernel written in Bass

```python
import jax, jax.numpy as jnp
from jax import lax
import numpy as np
import math

D_MODEL = 1024
BATCH = 1
SEQ = 512
DEPTH = 1

MEM_LEN = 256
N_HEADS_MLA = 8
QK_NOPE_DIM = 64
QK_ROPE_DIM = 32
QK_HEAD_DIM = QK_NOPE_DIM + QK_ROPE_DIM
V_HEAD_DIM = 64
Q_LORA_RANK = 3 * D_MODEL // 8
KV_LORA_RANK = D_MODEL // 4
MLA_WIDTH = N_HEADS_MLA * V_HEAD_DIM
CONV_WIDTH = D_MODEL // 2
CONV_K = 3
N_HEADS_MEM = 4
MEM_HEAD_DIM = 128
MEM_WIDTH = N_HEADS_MEM * MEM_HEAD_DIM

N_BRANCH = 3
ROPE_BASE = 10000.0
Q_BLOCK = 128
EPS = 1e-6

IN_SIZES = (Q_LORA_RANK, KV_LORA_RANK, QK_ROPE_DIM,
            CONV_WIDTH, CONV_WIDTH, CONV_WIDTH,
            MEM_WIDTH,
            MLA_WIDTH, CONV_WIDTH, MEM_WIDTH,
            N_BRANCH * D_MODEL)
IN_WIDTH = sum(IN_SIZES)


def rmsnorm(t, g):
    tf = t.astype(jnp.float32)
    tf = tf * lax.rsqrt(jnp.mean(tf * tf, axis=-1, keepdims=True) + EPS)
    return tf.astype(t.dtype) * g

def split_cols(t, sizes):
    return jnp.split(t, np.cumsum(sizes)[:-1].tolist(), axis=-1)

def rope_tables(positions, dtype):
    inv_freq = ROPE_BASE ** (-jnp.arange(0, QK_ROPE_DIM, 2, dtype=jnp.float32) / QK_ROPE_DIM)
    ang = positions.astype(jnp.float32)[..., None] * inv_freq
    return (jnp.cos(ang)[:, :, None, :].astype(dtype),
            jnp.sin(ang)[:, :, None, :].astype(dtype))

def rope_tail(t, cos, sin):
    t_nope, t1, t2 = split_cols(t, (QK_NOPE_DIM, QK_ROPE_DIM // 2, QK_ROPE_DIM // 2))
    return jnp.concatenate([t_nope, t1 * cos - t2 * sin, t2 * cos + t1 * sin], axis=-1)

def blocked_bidirectional_attention(q, k, v):
    B, S, H, Dh = q.shape
    nblk = S // Q_BLOCK
    qb = q.reshape(B, nblk, Q_BLOCK, H, Dh).transpose(1, 0, 2, 3, 4)
    scale = Dh ** -0.5

    def one_block(q_blk):
        s = jnp.einsum('bqhd,bkhd->bhqk', q_blk, k).astype(jnp.float32) * scale
        p = jax.nn.softmax(s, axis=-1).astype(v.dtype)
        return jnp.einsum('bhqk,bkhd->bqhd', p, v)

    out = lax.map(one_block, qb)
    return out.transpose(1, 0, 2, 3, 4).reshape(B, S, H * v.shape[-1])

def centred_short_conv(z, w, b):
    out = lax.conv_general_dilated(
        z, w[:, None, :], window_strides=(1,),
        padding=((CONV_K // 2, CONV_K // 2),),
        dimension_numbers=('NWC', 'WIO', 'NWC'),
        feature_group_count=z.shape[-1])
    return out + b

def hybrid_layer(x, mem, cos, sin, norm_g, w_in, b_gate, q_norm_g, w_uq, kv_norm_g, w_ukv,
                 q_head_g, k_head_g, conv_w, conv_b, mem_norm_g, w_mkv, mem_q_g, mem_k_g,
                 w_br_attn, w_br_conv, w_br_mem, w_out):
    B, S, _ = x.shape
    M = mem.shape[1]
    h = rmsnorm(x, norm_g)
    proj = h @ w_in
    (q_lat, kv_lat, k_pe, c_b, c_c, c_u, q_mem,
     g_attn, g_conv, g_mem, r) = split_cols(proj, IN_SIZES)

    q = (rmsnorm(q_lat, q_norm_g) @ w_uq).reshape(B, S, N_HEADS_MLA, QK_HEAD_DIM)
    kv = (rmsnorm(kv_lat, kv_norm_g) @ w_ukv).reshape(B, S, N_HEADS_MLA, QK_NOPE_DIM + V_HEAD_DIM)
    k_nope, v = split_cols(kv, (QK_NOPE_DIM, V_HEAD_DIM))
    k_rope = jnp.broadcast_to(k_pe[:, :, None, :], (B, S, N_HEADS_MLA, QK_ROPE_DIM))
    k = jnp.concatenate([k_nope, k_rope], axis=-1)
    q = rope_tail(rmsnorm(q, q_head_g), cos, sin)
    k = rope_tail(rmsnorm(k, k_head_g), cos, sin)
    o_attn = blocked_bidirectional_attention(q, k, v) * jax.nn.silu(g_attn)

    o_conv = c_b * centred_short_conv(c_c * c_u, conv_w, conv_b) * jax.nn.silu(g_conv)

    mkv = (rmsnorm(mem, mem_norm_g) @ w_mkv).reshape(B, M, N_HEADS_MEM, 2 * MEM_HEAD_DIM)
    m_k, m_v = split_cols(mkv, (MEM_HEAD_DIM, MEM_HEAD_DIM))
    mq = rmsnorm(q_mem.reshape(B, S, N_HEADS_MEM, MEM_HEAD_DIM), mem_q_g)
    m_k = rmsnorm(m_k, mem_k_g)
    s = jnp.einsum('bshd,bmhd->bhsm', mq, m_k).astype(jnp.float32) * (MEM_HEAD_DIM ** -0.5)
    p = jax.nn.softmax(s, axis=-1).astype(m_v.dtype)
    o_mem = jnp.einsum('bhsm,bmhd->bshd', p, m_v).reshape(B, S, MEM_WIDTH) * jax.nn.silu(g_mem)

    r_attn, r_conv, r_mem = split_cols(jax.nn.sigmoid(r + b_gate), (D_MODEL, D_MODEL, D_MODEL))
    y = r_attn * (o_attn @ w_br_attn) + r_conv * (o_conv @ w_br_conv) + r_mem * (o_mem @ w_br_mem)
    return x + y @ w_out

def first_inputs(seed: int = 0) -> dict:
    key = jax.random.key(seed)
    ks = jax.random.split(key, 24)

    def nrm(k, shape, scale):
        return jax.random.normal(k, shape, jnp.float32) * scale

    def gain(k, shape):
        return 1.0 + 0.1 * jax.random.normal(k, shape, jnp.float32)

    x = nrm(ks[0], (BATCH, SEQ, D_MODEL), 1.0)
    mem = nrm(ks[1], (BATCH, MEM_LEN, D_MODEL), 1.0)
    offset = jax.random.randint(ks[2], (BATCH, 1), 0, 1024, dtype=jnp.int32)
    positions = jnp.arange(SEQ, dtype=jnp.int32)[None, :] + offset
    return {
        'x': x,
        'mem': mem,
        'positions': positions,
        'norm_g': gain(ks[3], (DEPTH, D_MODEL)),
        'w_in': nrm(ks[4], (DEPTH, D_MODEL, IN_WIDTH), D_MODEL ** -0.5),
        'b_gate': nrm(ks[5], (DEPTH, N_BRANCH * D_MODEL), 0.1),
        'q_norm_g': gain(ks[6], (DEPTH, Q_LORA_RANK)),
        'w_uq': nrm(ks[7], (DEPTH, Q_LORA_RANK, N_HEADS_MLA * QK_HEAD_DIM), Q_LORA_RANK ** -0.5),
        'kv_norm_g': gain(ks[8], (DEPTH, KV_LORA_RANK)),
        'w_ukv': nrm(ks[9], (DEPTH, KV_LORA_RANK, N_HEADS_MLA * (QK_NOPE_DIM + V_HEAD_DIM)), KV_LORA_RANK ** -0.5),
        'q_head_g': gain(ks[10], (DEPTH, QK_HEAD_DIM)),
        'k_head_g': gain(ks[11], (DEPTH, QK_HEAD_DIM)),
        'conv_w': nrm(ks[12], (DEPTH, CONV_K, CONV_WIDTH), CONV_K ** -0.5),
        'conv_b': nrm(ks[13], (DEPTH, CONV_WIDTH), 0.1),
        'mem_norm_g': gain(ks[14], (DEPTH, D_MODEL)),
        'w_mkv': nrm(ks[15], (DEPTH, D_MODEL, 2 * MEM_WIDTH), D_MODEL ** -0.5),
        'mem_q_g': gain(ks[16], (DEPTH, MEM_HEAD_DIM)),
        'mem_k_g': gain(ks[17], (DEPTH, MEM_HEAD_DIM)),
        'w_br_attn': nrm(ks[18], (DEPTH, MLA_WIDTH, D_MODEL), MLA_WIDTH ** -0.5),
        'w_br_conv': nrm(ks[19], (DEPTH, CONV_WIDTH, D_MODEL), CONV_WIDTH ** -0.5),
        'w_br_mem': nrm(ks[20], (DEPTH, MEM_WIDTH, D_MODEL), MEM_WIDTH ** -0.5),
        'w_out': nrm(ks[21], (DEPTH, D_MODEL, D_MODEL), D_MODEL ** -0.5),
    }

def first_block(x, mem, positions, norm_g, w_in, b_gate, q_norm_g, w_uq, kv_norm_g, w_ukv,
              q_head_g, k_head_g, conv_w, conv_b, mem_norm_g, w_mkv, mem_q_g, mem_k_g,
              w_br_attn, w_br_conv, w_br_mem, w_out):
    cos, sin = rope_tables(positions, x.dtype)
    for i in range(DEPTH):
        x = hybrid_layer(x, mem, cos, sin, norm_g[i], w_in[i], b_gate[i], q_norm_g[i], w_uq[i],
                         kv_norm_g[i], w_ukv[i], q_head_g[i], k_head_g[i], conv_w[i], conv_b[i],
                         mem_norm_g[i], w_mkv[i], mem_q_g[i], mem_k_g[i],
                         w_br_attn[i], w_br_conv[i], w_br_mem[i], w_out[i])
    return x


DEPTH_2 = 2

N_MIXERS = 2
SB_HEADS = 16
SB_HEAD_DIM = D_MODEL // SB_HEADS
HG_EXPAND = 128
HG_HEADS = D_MODEL // HG_EXPAND
HG_KEY_DIM = HG_EXPAND
HG_VAL_DIM = D_MODEL // HG_HEADS
HG_CHUNK = 64
D_FF = 4 * D_MODEL
N_SB = (DEPTH_2 + N_MIXERS - 1) // N_MIXERS
N_HG = DEPTH_2 // N_MIXERS


def rmsnorm_2(x, gain):
    xf = x.astype(jnp.float32)
    y = xf * lax.rsqrt(jnp.mean(xf * xf, axis=-1, keepdims=True) + EPS)
    return (y * gain.astype(jnp.float32)).astype(x.dtype)

def stick_breaking_attention(q, k, v):
    seq = q.shape[2]
    scale = 1.0 / math.sqrt(q.shape[-1])
    outs = []
    for t0 in range(0, seq, Q_BLOCK):
        t1 = t0 + Q_BLOCK
        z = jnp.einsum('bhqd,bhkd->bhqk', q[:, :, t0:t1], k[:, :, :t1]).astype(jnp.float32) * scale
        causal = jnp.arange(t1)[None, :] < (t0 + jnp.arange(Q_BLOCK))[:, None]
        log_stay = jnp.where(causal, jax.nn.log_sigmoid(-z), 0.0)
        log_between = lax.cumsum(log_stay, axis=3, reverse=True) - log_stay
        weights = jnp.where(causal, jnp.exp(jax.nn.log_sigmoid(z) + log_between), 0.0)
        outs.append(jnp.einsum('bhqk,bhkd->bhqd', weights.astype(v.dtype), v[:, :, :t1]))
    return jnp.concatenate(outs, axis=2)

def stick_breaking_mixer(h, w_qkv, q_gain, k_gain, w_o):
    bsz, seq, _ = h.shape
    qkv = h @ w_qkv
    q, k, v = jnp.split(qkv, 3, axis=-1)
    q = rmsnorm_2(q.reshape(bsz, seq, SB_HEADS, SB_HEAD_DIM), q_gain)
    k = rmsnorm_2(k.reshape(bsz, seq, SB_HEADS, SB_HEAD_DIM), k_gain)
    v = v.reshape(bsz, seq, SB_HEADS, SB_HEAD_DIM)
    q, k, v = (jnp.transpose(a, (0, 2, 1, 3)) for a in (q, k, v))
    o = stick_breaking_attention(q, k, v)
    o = jnp.transpose(o, (0, 2, 1, 3)).reshape(bsz, seq, D_MODEL)
    return o @ w_o

def hgrn2_chunk_scan(q, k, v, log_f):
    bsz, nh, seq, dk = q.shape
    dv = v.shape[-1]
    n_chunks = seq // HG_CHUNK

    def to_chunks(a):
        return jnp.moveaxis(a.astype(jnp.float32).reshape(bsz, nh, n_chunks, HG_CHUNK, a.shape[-1]), 2, 0)

    incl = jnp.tril(jnp.ones((HG_CHUNK, HG_CHUNK), dtype=bool))

    def step(state, inp):
        qc, kc, vc, lfc = inp
        b = jnp.cumsum(lfc, axis=2)
        inter = jnp.einsum('bhck,bhkv->bhcv', qc * jnp.exp(b), state)
        diff = b[:, :, :, None, :] - b[:, :, None, :, :]
        decay = jnp.where(incl[:, :, None], jnp.exp(jnp.minimum(diff, 0.0)), 0.0)
        scores = jnp.einsum('bhtk,bhsk,bhtsk->bhts', qc, kc, decay)
        intra = jnp.einsum('bhts,bhsv->bhtv', scores, vc)
        b_last = b[:, :, -1:, :]
        new_state = (jnp.exp(b_last[:, :, 0, :])[..., None] * state
                     + jnp.einsum('bhsk,bhsv->bhkv', kc * jnp.exp(b_last - b), vc))
        return new_state, inter + intra

    init = jnp.zeros((bsz, nh, dk, dv), jnp.float32)
    _, ys = lax.scan(step, init, (to_chunks(q), to_chunks(k), to_chunks(v), to_chunks(log_f)))
    return jnp.moveaxis(ys, 0, 2).reshape(bsz, nh, seq, dv)

def hgrn2_mixer(h, w_in, lower_bound, norm_gain, w_o):
    bsz, seq, _ = h.shape
    proj = h @ w_in
    q, f, i, g = jnp.split(proj, 4, axis=-1)
    q = jax.nn.silu(q)
    lb = lower_bound.astype(jnp.float32)
    forget = lb + (1.0 - lb) * jax.nn.sigmoid(f.astype(jnp.float32))
    log_f = jnp.log(forget)
    k = -jnp.expm1(log_f)

    def heads(a, d):
        return jnp.transpose(a.reshape(bsz, seq, HG_HEADS, d), (0, 2, 1, 3))

    o = hgrn2_chunk_scan(heads(q, HG_KEY_DIM), heads(k, HG_KEY_DIM),
                         heads(i, HG_VAL_DIM), heads(log_f, HG_KEY_DIM))
    o = jnp.transpose(o, (0, 2, 1, 3)).astype(h.dtype)
    o = rmsnorm_2(o, norm_gain).reshape(bsz, seq, D_MODEL)
    o = o * jax.nn.sigmoid(g)
    return o @ w_o

def squared_relu_mlp(h, w1, w2):
    a = jax.nn.relu(h @ w1)
    return (a * a) @ w2

def second_inputs(seed: int = 0) -> dict:
    key = jax.random.key(seed)
    ks = jax.random.split(key, 12)
    d_in = D_MODEL ** -0.5
    res = (2 * DEPTH_2) ** -0.5
    nrm = jax.random.normal
    return {
        "x": nrm(ks[0], (BATCH, SEQ, D_MODEL), jnp.float32),
        "norm_gains": 1.0 + 0.02 * nrm(ks[1], (DEPTH_2, 2, D_MODEL), jnp.float32),
        "sb_w_qkv": nrm(ks[2], (N_SB, D_MODEL, 3 * D_MODEL), jnp.float32) * d_in,
        "sb_q_gain": 1.0 + 0.02 * nrm(ks[3], (N_SB, SB_HEAD_DIM), jnp.float32),
        "sb_k_gain": 1.0 + 0.02 * nrm(ks[4], (N_SB, SB_HEAD_DIM), jnp.float32),
        "sb_w_o": nrm(ks[5], (N_SB, D_MODEL, D_MODEL), jnp.float32) * d_in * res,
        "hg_w_in": nrm(ks[6], (N_HG, D_MODEL, 4 * D_MODEL), jnp.float32) * d_in,
        "hg_lb_logits": 0.5 * nrm(ks[7], (N_HG, D_MODEL), jnp.float32),
        "hg_norm_gain": 1.0 + 0.02 * nrm(ks[8], (N_HG, HG_VAL_DIM), jnp.float32),
        "hg_w_o": nrm(ks[9], (N_HG, D_MODEL, D_MODEL), jnp.float32) * d_in * res,
        "mlp_w1": nrm(ks[10], (DEPTH_2, D_MODEL, D_FF), jnp.float32) * d_in,
        "mlp_w2": nrm(ks[11], (DEPTH_2, D_FF, D_MODEL), jnp.float32) * (D_FF ** -0.5) * res,
    }

def second_block(x, norm_gains, sb_w_qkv, sb_q_gain, sb_k_gain, sb_w_o,
              hg_w_in, hg_lb_logits, hg_norm_gain, hg_w_o, mlp_w1, mlp_w2):
    p = jax.nn.softmax(hg_lb_logits.astype(jnp.float32), axis=0)
    lower_bounds = jnp.cumsum(p, axis=0) - p[0:1]
    for layer in range(DEPTH_2):
        j = layer // N_MIXERS
        h = rmsnorm_2(x, norm_gains[layer, 0])
        if layer % N_MIXERS == 0:
            x = x + stick_breaking_mixer(h, sb_w_qkv[j], sb_q_gain[j], sb_k_gain[j], sb_w_o[j])
        else:
            x = x + hgrn2_mixer(h, hg_w_in[j], lower_bounds[j], hg_norm_gain[j], hg_w_o[j])
        h = rmsnorm_2(x, norm_gains[layer, 1])
        x = x + squared_relu_mlp(h, mlp_w1[layer], mlp_w2[layer])
    return x


def setup_inputs(seed=0):
    out = dict(first_inputs(seed))
    for name, value in second_inputs(seed + 1).items():
        if name != "x":
            out[name + "_2"] = value
    return out


def reference(
    x, mem, positions, norm_g, w_in, b_gate, q_norm_g, w_uq, kv_norm_g, w_ukv, q_head_g,
    k_head_g, conv_w, conv_b, mem_norm_g, w_mkv, mem_q_g, mem_k_g, w_br_attn, w_br_conv,
    w_br_mem, w_out, norm_gains_2, sb_w_qkv_2, sb_q_gain_2, sb_k_gain_2, sb_w_o_2, hg_w_in_2,
    hg_lb_logits_2, hg_norm_gain_2, hg_w_o_2, mlp_w1_2, mlp_w2_2,
):
    x = first_block(
        x, mem, positions, norm_g, w_in, b_gate, q_norm_g, w_uq, kv_norm_g, w_ukv, q_head_g,
        k_head_g, conv_w, conv_b, mem_norm_g, w_mkv, mem_q_g, mem_k_g, w_br_attn, w_br_conv,
        w_br_mem, w_out,
    )
    return second_block(
        x, norm_gains_2, sb_w_qkv_2, sb_q_gain_2, sb_k_gain_2, sb_w_o_2, hg_w_in_2,
        hg_lb_logits_2, hg_norm_gain_2, hg_w_o_2, mlp_w1_2, mlp_w2_2,
    )


_drawn_inputs = setup_inputs


def setup_inputs(seed=0):
    import zlib

    import numpy as np

    out = dict(_drawn_inputs(seed))
    spreads = {}
    factors = {'b_gate': 4.455,
     'q_norm_g': 8.0,
     'kv_norm_g': 8.0,
     'q_head_g': 8.0,
     'k_head_g': 8.0,
     'mem_norm_g': 8.0,
     'mem_q_g': 8.0,
     'mem_k_g': 8.0,
     'norm_gains_2': 3.165,
     'sb_q_gain_2': 8.0,
     'sb_k_gain_2': 8.0,
     'hg_norm_gain_2': 8.0}
    for name, (base, spread) in spreads.items():
        noise = np.random.default_rng([zlib.crc32(name.encode()), seed]).standard_normal(out[name].shape)
        drawn = base * np.exp(spread * noise) if base else spread * noise
        out[name] = __import__('jax').numpy.asarray(drawn.astype(out[name].dtype))
    for name, factor in factors.items():
        out[name] = (out[name] * factor).astype(out[name].dtype)
    return out
```

```python
from contextlib import ExitStack
from math import lcm

import concourse.bass as bass
import numpy as np
from concourse import mybir

ALU = mybir.AluOpType
ACT = mybir.ActivationFunctionType
F32 = mybir.dt.float32
F32R = mybir.dt.float32r
I32 = mybir.dt.int32
AX = mybir.AxisListType

P = 128
T = 512
NT = T // P
D = 1024
ND = D // P
M = 256
NM = M // P
EPS = 1e-6
HEADS, NOPE, ROPE, QK, DV = 8, 64, 32, 96, 64
Q_RANK, KV_RANK = 384, 256
CONV = 512
MEM_HEADS = 4
SB_HEADS, SB_DIM = 16, 64
HG_HEADS = 8
D_FF = 4096

C_QLAT, C_KVLAT, C_KPE = 0, 384, 640
C_B, C_C, C_U = 672, 1184, 1696
C_QMEM, C_GATTN, C_GCONV, C_GMEM, C_R = 2208, 2720, 3232, 3744, 4256

K_EYE, K_ONE, K_CAUSAL = 0, 128, 256
K_HALVES = 384
K_INVF, K_SIGN, K_EPS = 386, 387, 388
K_LEVEL = 392
LEVELS = 7
K_DIAG = K_EYE
K_COLS = K_LEVEL + LEVELS * P

VEC_ROWS = [("norm_g", 8), ("b_gate", 24), ("q_norm_g", 3), ("kv_norm_g", 2), ("conv_w", 12),
            ("conv_b", 4), ("mem_norm_g", 8), ("mem_q_g", 1), ("mem_k_g", 1), ("norm_gains_2", 32),
            ("hg_lb_logits_2", 8), ("hg_norm_gain_2", 1),
            ("q_head_g", 1), ("k_head_g", 1), ("sb_q_gain_2", 1), ("sb_k_gain_2", 1)]
VEC = {}
_at = 0
for _name, _n in VEC_ROWS:
    VEC[_name] = _at
    _at += _n
VEC_N = _at


def shape_constants():
    c = np.zeros((P, K_COLS), np.float32)
    c[:, K_EYE:K_EYE + P] = np.eye(P)
    c[:, K_ONE:K_ONE + P] = 1.0
    q = np.arange(P)[:, None]
    s = np.arange(P)[None, :]
    c[:, K_CAUSAL:K_CAUSAL + P] = np.where(s < q, 0.0, -1e30)
    c[:64, K_HALVES] = 1.0
    c[64:, K_HALVES + 1] = 1.0
    freq = np.float32(10000.0) ** (-np.arange(0, ROPE, 2, dtype=np.float32) / np.float32(ROPE))
    c[NOPE:QK, K_INVF] = np.concatenate([freq, freq])
    c[NOPE:QK, K_SIGN] = np.concatenate([-np.ones(16), np.ones(16)])
    c[:, K_EPS] = EPS
    src, dst = np.arange(P)[:, None], np.arange(P)[None, :]
    for level in range(LEVELS):
        h = 1 << level
        same = src // (2 * h) == dst // (2 * h)
        c[:, K_LEVEL + level * P:K_LEVEL + (level + 1) * P] = same & (src // h % 2 == 0) & (dst // h % 2 == 1)
    return c


def wait(eng, sem, value):
    if isinstance(value, int) and value <= 0:
        return
    eng.wait_ge(sem, value)


def rounds(eng, n):
    yield 0
    if n > 1:
        with eng.Fori(1, n) as i:
            yield i


def at(i, size):
    return bass.ds(i * size, size) if not isinstance(i, int) else slice(i * size, (i + 1) * size)


RING = 4
UNIT = ND * P


class Weights:

    def __init__(self, nc, sb, sem, w):
        self.stage = [sb(f"weight_stage{i}", [P, UNIT], F32) for i in range(RING)]
        self.hi = [sb(f"weight_hi{i}", [P, UNIT], F32R) for i in range(RING)]
        self.lo = [sb(f"weight_lo{i}", [P, UNIT], F32R) for i in range(RING)]
        self.loaded = [sem(f"weight_loaded{i}") for i in range(RING)]
        self.one, self.one_set = sb("weight_one", [P, 1], F32), sem("weight_one_set")
        self.hi_done = sem("weight_hi_done")
        self.split_done = sem("weight_split_done")
        self.used = sem("weight_used")
        self.runs, self.n = [], 0
        self.first = {}

        def cols(name, lead, base):
            def view(f):
                full = w[name][lead].rearrange("(k p) n -> p k n", p=P)
                return full[:, :, bass.ds(f * P + base, P) if not isinstance(f, int) else slice(base + f * P, base + f * P + P)]
            return view

        def add(name, count, period, load, size=lambda r: UNIT):
            self.first[name] = self.n
            self.runs.append((self.n, count, period, load, size))
            self.n += count

        win = [cols("w_in", 0, c) for c in (C_QLAT,)][0]
        add("latent", 5, 1, lambda f, r: win(f))
        add("kpe", 1, 1, lambda f, r: w["w_in"][0].rearrange("(k p) n -> p k n", p=P)[:, :, C_KPE - 64:C_KPE + ROPE],
            lambda r: ND * QK)
        add("uq", 3, 1, lambda f, r: w["w_uq"][0, f * P:(f + 1) * P, :].rearrange("p (k n) -> p k n", k=1),
            lambda r: HEADS * QK)
        add("ukv", 2, 1, lambda f, r: w["w_ukv"][0, f * P:(f + 1) * P, :].rearrange("p (k n) -> p k n", k=1))
        qmem = cols("w_in", 0, C_QMEM)
        add("qmem", 4, 1, lambda f, r: qmem(f))
        mkv = cols("w_mkv", 0, 0)
        add("mkv", 8, 1, lambda f, r: mkv(f))
        conv = [cols("w_in", 0, c) for c in (C_C, C_U, C_B, C_GCONV)]
        add("conv", 16, 4, lambda f, r: conv[r](f))
        gates = [cols("w_in", 0, c) for c in (C_GATTN, C_GMEM)]
        add("gates", 8, 8, lambda f, r: gates[r // 4](r % 4))
        mix = [cols("w_in", 0, C_R), cols("w_br_attn", 0, 0), cols("w_in", 0, C_R + D), cols("w_br_conv", 0, 0),
               cols("w_in", 0, C_R + 2 * D), cols("w_br_mem", 0, 0)]
        add("mix", 48, 6, lambda f, r: mix[r](f), lambda r: UNIT // 2 if r % 2 else UNIT)
        for name, source, count in (("out", "w_out", 8), ("qkv", "sb_w_qkv_2", 24), ("sbo", "sb_w_o_2", 8)):
            add(name, count, 1, lambda f, r, v=cols(source, 0, 0): v(f))
        self.mlp_runs(add, w, 0, cols)
        for name, source, count in (("hgin", "hg_w_in_2", 32), ("hgo", "hg_w_o_2", 8)):
            add(name, count, 1, lambda f, r, v=cols(source, 0, 0): v(f))
        self.mlp_runs(add, w, 1, cols)

    def mlp_runs(self, add, w, layer, cols):
        one = cols("mlp_w1_2", layer, 0)
        w2 = w["mlp_w2_2"][layer].rearrange("(g k p) n -> g p k n", k=4, p=P)

        def two(g, r):
            group = w2[g] if isinstance(g, int) else w2[bass.ds(g, 1)].rearrange("a p k n -> p (a k) n")
            return group[:, :, r * 256:(r + 1) * 256]

        def body(f, r):
            which, r = divmod(r, 4)
            if which % 2 == 0:
                return one(f * 8 + (4 if which == 0 else 8) + r)
            return two(f * 2 + (0 if which == 1 else 1), r)

        def tail(f, r):
            return one(28 + r) if r < 4 else two(6 if r < 8 else 7, r % 4)

        add(f"mlp{layer}head", 4, 1, lambda f, r: one(f))
        add(f"mlp{layer}", 48, 16, body)
        add(f"mlp{layer}tail", 12, 12, tail)

    def steps(self, eng, lo, hi, straight=()):
        for start, count, period, load, size in self.runs:
            a, b = max(lo, start), min(hi, start + count)
            if a >= b:
                continue
            body = lcm(RING, period)
            times = (b - a) // body if b - a >= 2 * body and start not in straight else 0

            def one(i, j):
                q, r = divmod(a - start + j, period)
                return (i * body + a + j, (a + j) % RING, i * (body // RING) + (a + j) // RING + 1,
                        lambda: load(i * (body // period) + q, r), size(r))
            if times:
                with eng.Fori(0, times) as i:
                    for j in range(body):
                        yield one(i, j)
            for j in range(times * body, b - a):
                yield one(0, j)

    def load(self, sp, lo, hi):
        for u, slot, fills, source, size in self.steps(sp, min(lo, self.n), min(hi, self.n),
                                                       (self.first["mix"],)):
            wait(sp, self.split_done, u - RING + 1)
            src = source()
            k = src.shape[1]
            sp.dma_start(self.stage[slot][:, 0:size].rearrange("p (k n) -> p k n", k=k),
                         src).then_inc(self.loaded[slot], 16)

    def split(self, pool, lo, hi):
        for u, slot, fills, _, size in self.steps(pool, min(lo, self.n), min(hi, self.n)):
            stage, whi, wlo = (x[slot][:, 0:size] for x in (self.stage, self.hi, self.lo))
            wait(pool, self.used, u - RING + 1)
            pool.wait_ge(self.loaded[slot], fills * 16)
            pool.tensor_tensor(whi, stage, self.one[:, :].to_broadcast([P, size]), ALU.mult).then_inc(self.hi_done, 1)
            pool.wait_ge(self.hi_done, u + 1)
            pool.tensor_tensor(wlo, stage, whi.bitcast(F32), ALU.subtract).then_inc(self.split_done, 1)

    def tile(self, u, k, a=0, n=P, width=P):
        s = u % RING
        return self.hi[s][:, k * width + a:k * width + a + n], self.lo[s][:, k * width + a:k * width + a + n]


def products(pe, out, pairs):
    pairs = list(pairs)
    n = 0
    for (whi, wlo), (ahi, alo) in pairs:
        for l, r in ((wlo, ahi), (whi, alo), (whi, ahi)):
            last = pe.matmul(out, l, r, start=n == 0, stop=n == 3 * len(pairs) - 1)
            n += 1
    return last


class Norm:

    def __init__(self, S, name, groups, width, tokens=NT, halves=False):
        self.S, self.groups, self.width, self.tokens, self.halves = S, groups, width, tokens, halves
        self.cols = groups * tokens * (2 if halves else 1)
        self.signals = {}
        for event in ("squared", "summed", "rooted", "inverted", "spread", "applied"):
            sem, count = S.shared(f"norm_{event}")
            self.signals[event] = (sem, count)
        self.root = S.columns(self.cols)
        self.rstd = S.columns(self.cols)

    def sem(self, event):
        return self.signals[event][0]

    def wait(self, eng, event, n):
        if n > 0:
            sem, before = self.signals[event]
            eng.wait_ge(sem, before + n)

    def end(self, squares, applied):
        counts = {"squared": squares, "summed": 1, "rooted": 1, "inverted": 1, "spread": self.groups,
                  "applied": applied}
        for event, n in counts.items():
            self.S.advance(f"norm_{event}", n)

    def square(self, act, out, src):
        act.activation(out, src, ACT.Square).then_inc(self.sem("squared"), 1)

    def sums(self, pe, bank, parts, squares=1):
        self.wait(pe, "squared", squares)
        w = 2 if self.halves else 1
        for g in range(self.groups):
            for i in range(self.tokens):
                c = (g * self.tokens + i) * w
                todo = parts(g)
                for n, (sq, ones) in enumerate(todo):
                    last = pe.matmul(bank[:, c:c + w], sq[:, i * P:(i + 1) * P], ones,
                                     start=n == 0, stop=n == len(todo) - 1)
        last.then_inc(self.sem("summed"), 1)

    def roots(self, act, bank):
        self.wait(act, "summed", 1)
        act.activation(self.root, bank[:, 0:self.cols], ACT.Sqrt, bias=self.S.const[:, K_EPS:K_EPS + 1],
                       scale=1.0 / self.width).then_inc(self.sem("rooted"), 1)

    def invert(self, dve):
        self.wait(dve, "rooted", 1)
        dve.reciprocal(self.rstd, self.root).then_inc(self.sem("inverted"), 1)

    def spread_group(self, pe, bank, g, rows=P, free_at=0):
        if g == 0:
            self.wait(pe, "inverted", 1)
        self.wait(pe, "applied", free_at)
        for i in range(self.tokens):
            c = g * self.tokens + i
            cols = bank[:, i * P:(i + 1) * P]
            if self.halves:
                for half in range(2):
                    lhs = self.rstd[:, 2 * c + half:2 * c + half + 1].to_broadcast([P, 64])
                    last = pe.matmul(cols[half * 64:(half + 1) * 64, :], lhs, self.S.eye, start=True, stop=True)
            else:
                lhs = self.rstd[:, c:c + 1].to_broadcast([P, rows])
                last = pe.matmul(cols[0:rows, :], lhs, self.S.eye, start=True, stop=True)
        last.then_inc(self.sem("spread"), 1)


class State:
    pass


def model_norm(S, name, src, gain, hi, lo, scratch, tokens=NT, load=None, width=D):
    nc = S.nc
    tiles = width // P
    n = Norm(S, name, 1, width, tokens)
    (hi_done, hi0), (lo_done, _) = S.shared("split_hi"), S.shared("split_lo")
    tk = tokens * P
    with nc.Block() as block:
        @block.scalar
        def _(act):
            n.square(act, scratch[:, 0:tiles, 0:tk], src[:, 0:tiles, 0:tk])
            n.roots(act, S.ps[0])
            for t in range(tiles):
                n.wait(act, "applied", t + 1)
                act.activation(hi[:, t, 0:tk], scratch[:, t, 0:tk], ACT.Copy).then_inc(hi_done, 1)

        @block.tensor
        def _(pe):
            n.sums(pe, S.ps[0], lambda g: [(scratch[:, t, 0:tk], S.ones[:, 0:1]) for t in range(tiles)])
            n.spread_group(pe, S.ps[1], 0)

        @block.vector
        def _(dve):
            n.invert(dve)
            n.wait(dve, "spread", 1)
            for t in range(tiles):
                dve.scalar_tensor_tensor(out=scratch[:, t, 0:tk], in0=src[:, t, 0:tk],
                                         scalar=S.vec[:, gain + t:gain + t + 1], in1=S.ps[1][:, 0:tk],
                                         op0=ALU.mult, op1=ALU.mult).then_inc(n.sem("applied"), 1)
            for t in range(tiles):
                dve.wait_ge(hi_done, hi0 + t + 1)
                n.wait(dve, "applied", t + 1)
                dve.tensor_tensor(lo[:, t, 0:tk], scratch[:, t, 0:tk], hi[:, t, 0:tk].bitcast(F32),
                                  ALU.subtract).then_inc(lo_done, 1)
    n.end(1, tiles)
    S.advance("split_hi", tiles)
    S.advance("split_lo", tiles)


def setup(S, w, consts):
    nc, W = S.nc, S.W
    loaded, vec_loaded, zeroed = S.sem("setup_loaded"), S.sem("vec_loaded"), S.sem("rows_zeroed")
    turned, copied = S.sem("x_turned"), S.sem("x_copied")
    vec_turned, vec_copied = S.sem("vec_turned"), S.sem("vec_copied")
    pos_f, spread, angle = S.sem("pos_float"), S.sem("pos_spread"), S.sem("angle_steps")
    x_loaded = S.sem("x_loaded")
    with ExitStack() as scope:
        def sb(name, shape, dt):
            return scope.enter_context(nc.sbuf_tensor(name, shape, dt))
        x_tok = sb("x_tok", [P, NT, D], F32)
        rows = sb("vec_rows", [P, P], F32)
        pos_i = sb("pos_i", [1, T], I32)
        pos = sb("pos", [1, T], F32)
        ang = sb("ang", [P, 5, T], F32)
        whole = sb("whole", [P, T], I32)
        block = scope.enter_context(nc.Block())

        @block.sync
        def _(sp):
            sp.dma_start(x_tok[:, :, :], w["x"][0].rearrange("(i p) d -> p i d", p=P)).then_inc(x_loaded, 16)
            sp.dma_start(S.const[:, :], consts).then_inc(loaded, 16)
            sp.dma_start(pos_i[:, :], w["positions"]).then_inc(loaded, 16)
            sp.wait_ge(zeroed, 1)
            n = 0
            for name, k in VEC_ROWS:
                r, src = VEC[name], w[name]
                if name == "conv_w":
                    views = [(rows[r:r + k, :], src[0].rearrange("t (c p) -> (t c) p", p=P))]
                elif name == "norm_gains_2":
                    views = [(rows[r:r + k, :], src.rearrange("l s (c p) -> (l s c) p", p=P))]
                elif name in ("sb_q_gain_2", "sb_k_gain_2"):
                    views = [(rows[r:r + 1, 0:64], src), (rows[r:r + 1, 64:128], src)]
                elif name in ("q_head_g", "k_head_g"):
                    views = [(rows[r:r + 1, 0:QK], src)]
                else:
                    views = [(rows[r:r + k, :], src[0].rearrange("(c p) -> c p", p=P))]
                for dst, view in views:
                    sp.dma_start(dst, view).then_inc(vec_loaded, 16)
                    n += 1
            S.n_vec = n
            W.load(sp, 0, 2 * RING)

        @block.gpsimd
        def _(pool):
            pool.memset(rows[:, :], 0.0).then_inc(zeroed, 1)
            pool.memset(W.one[:, :], 1.0).then_inc(W.one_set, 1)
            pool.wait_ge(W.one_set, 1)
            W.split(pool, 0, RING)

        @block.tensor
        def _(pe):
            pe.wait_ge(loaded, 32)
            pe.wait_ge(x_loaded, 16)
            for c in range(ND):
                if c >= 4:
                    pe.wait_ge(copied, c - 3)
                for i in range(NT):
                    last = pe.transpose(S.ps[c % 4][:, i * P:(i + 1) * P], x_tok[:, i, c * P:(c + 1) * P], S.eye)
                last.then_inc(turned, 1)
            pe.wait_ge(vec_loaded, 16 * S.n_vec)
            pe.transpose(S.ps[4][:, 0:P], rows[:, :], S.eye).then_inc(vec_turned, 1)
            pe.wait_ge(pos_f, 1)
            pe.matmul(S.ps[5][0:QK, :], S.ones[0:1, 0:QK], pos[:, :], start=True, stop=True).then_inc(spread, 1)

        @block.scalar
        def _(act):
            for c in range(ND):
                act.wait_ge(turned, c + 1)
                act.activation(S.x[:, c, :], S.ps[c % 4][:, :], ACT.Copy).then_inc(copied, 1)
            act.wait_ge(angle, 15)
            act.activation(S.cos[NOPE:QK, :], ang[NOPE:QK, 4, :], ACT.Sin).then_inc(angle, 1)
            act.activation(ang[NOPE:QK, 1, :], ang[NOPE:QK, 3, :], ACT.Sin).then_inc(angle, 1)

        @block.vector
        def _(dve):
            dve.wait_ge(loaded, 32)
            dve.tensor_copy(pos[:, :], pos_i[:, :]).then_inc(pos_f, 1)
            dve.wait_ge(vec_turned, 1)
            dve.tensor_copy(S.vec[:, :], S.ps[4][:, 0:P]).then_inc(vec_copied, 1)
            dve.wait_ge(vec_copied, 1)
            dve.tensor_scalar(S.q_gain[:, :], S.vec[:, VEC["q_head_g"]:VEC["q_head_g"] + 1], QK ** -0.5, None,
                              ALU.mult).then_inc(vec_copied, 1)
            dve.tensor_scalar(S.mq_gain[:, :], S.vec[:, VEC["mem_q_g"]:VEC["mem_q_g"] + 1], P ** -0.5, None,
                              ALU.mult).then_inc(vec_copied, 1)
            lg = S.vec[:, VEC["hg_lb_logits_2"]:VEC["hg_lb_logits_2"] + 8]
            dve.tensor_tensor(S.lb[:, :], lg, lg, ALU.subtract).then_inc(vec_copied, 1)
            r = slice(NOPE, QK)
            steps = 0

            def step(ins):
                nonlocal steps
                ins.then_inc(angle, 1)
                steps += 1
                dve.wait_ge(angle, steps)
            dve.wait_ge(spread, 1)
            step(dve.tensor_scalar(ang[r, 0, :], S.ps[5][r, :], S.const[r, K_INVF:K_INVF + 1], None, ALU.mult))
            for quarter, dst in ((0.25, 4), (0.0, 3)):
                step(dve.tensor_scalar(ang[r, 1, :], ang[r, 0, :], 1.0 / (2 * np.pi), quarter, ALU.mult, ALU.add))
                step(dve.tensor_copy(whole[r, :], ang[r, 1, :]))
                step(dve.tensor_copy(ang[r, 2, :], whole[r, :]))
                for k, part in enumerate(TWO_PI):
                    step(dve.scalar_tensor_tensor(out=ang[r, dst, :], in0=ang[r, 2, :], scalar=-part,
                                                  in1=ang[r, 0 if k == 0 else dst, :], op0=ALU.mult, op1=ALU.add))
                if quarter:
                    step(dve.tensor_scalar(ang[r, dst, :], ang[r, dst, :], float(np.pi / 2), None, ALU.add))
            assert steps == 14
            dve.tensor_scalar(ang[r, 3:5, :], ang[r, 3:5, :], PI_DOWN, -PI_DOWN, ALU.min, ALU.max).then_inc(angle, 1)
            dve.wait_ge(angle, 17)
            dve.tensor_scalar(S.sin[r, :], ang[r, 1, :], S.const[r, K_SIGN:K_SIGN + 1], None,
                              ALU.mult).then_inc(vec_copied, 1)


PI_DOWN = 3.1415925
_A = 6.28125
_B = float(np.float32(np.floor((2 * np.pi - _A) * 2 ** 21) / 2 ** 21))
TWO_PI = (_A, _B, 2 * np.pi - _A - _B)
SWAP = [(i + 16) % 32 for i in range(32)]


def project(S, name, dests, u0, act_side, funcs=None):
    nc, W = S.nc, S.W
    out_done, before = S.shared("projected")
    ahi, alo, tokens = act_side
    with nc.Block() as block:
        n_units = len(dests)

        @block.sync
        def _(sp):
            W.load(sp, u0 + 2 * RING, u0 + n_units + 2 * RING)

        @block.gpsimd
        def _(pool):
            W.split(pool, u0 + RING, u0 + n_units + RING)

        @block.tensor
        def _(pe):
            for n, (dst, rows, _) in enumerate(dests):
                u = u0 + n
                pe.wait_ge(W.split_done, u + 1)
                if n >= 4:
                    pe.wait_ge(out_done, before + n - 3)
                products(pe, S.ps[n % 4][0:rows, 0:tokens],
                         ((W.tile(u, k, 0, rows, rows), (ahi[:, k, 0:tokens], alo[:, k, 0:tokens]))
                          for k in range(ND))).then_inc(W.used, 1)

        @block.scalar
        def _(act):
            for n, (dst, rows, func) in enumerate(dests):
                act.wait_ge(W.used, u0 + n + 1)
                act.activation(dst, S.ps[n % 4][0:rows, 0:tokens], func).then_inc(out_done, 1)
    S.advance("projected", len(dests))


def project_loop(S, name, u0, groups, ahi, alo):
    nc, W = S.nc, S.W
    out_done, before = S.shared("projected")
    total = sum(n for _, _, n in groups)
    with nc.Block() as block:
        @block.sync
        def _(sp):
            W.load(sp, u0 + 2 * RING, u0 + total + 2 * RING)

        @block.gpsimd
        def _(pool):
            W.split(pool, u0 + RING, u0 + total + RING)

        @block.tensor
        def _(pe):
            for i in rounds(pe, total // 4):
                for j in range(4):
                    pe.wait_ge(W.split_done, i * 4 + (u0 + j + 1))
                    if not isinstance(i, int):
                        pe.wait_ge(out_done, i * 4 + (before + j - 3))
                    products(pe, S.ps[j][:, :], ((W.tile(u0 + j, k), (ahi[:, k, :], alo[:, k, :]))
                                                 for k in range(ND))).then_inc(W.used, 1)

        @block.scalar
        def _(act):
            base = 0
            for dst, func, n in groups:
                with act.Fori(0, n // 4) as i:
                    for j in range(4):
                        act.wait_ge(W.used, i * 4 + (u0 + base + j + 1))
                        act.activation(dst[:, bass.ds(i * 4 + j, 1), :].rearrange("p a t -> p (a t)"),
                                       S.ps[j][:, :], func).then_inc(out_done, 1)
                base += n
    S.advance("projected", total)


def add_to_x(S, name, u0, ahi, alo):
    nc, W = S.nc, S.W
    added, before = S.shared("x_added")
    with nc.Block() as block:
        @block.sync
        def _(sp):
            W.load(sp, u0 + 2 * RING, u0 + ND + 2 * RING)

        @block.gpsimd
        def _(pool):
            W.split(pool, u0 + RING, u0 + ND + RING)

        @block.tensor
        def _(pe):
            for n in range(ND):
                pe.wait_ge(W.split_done, u0 + n + 1)
                if n >= 4:
                    pe.wait_ge(added, before + n - 3)
                products(pe, S.ps[n % 4][:, :], ((W.tile(u0 + n, k), (ahi[:, k, :], alo[:, k, :]))
                                                 for k in range(ND))).then_inc(W.used, 1)

        @block.vector
        def _(dve):
            for n in range(ND):
                dve.wait_ge(W.used, u0 + n + 1)
                dve.tensor_tensor(S.x[:, n, :], S.x[:, n, :], S.ps[n % 4][:, :], ALU.add).then_inc(added, 1)
    S.advance("x_added", ND)


def softmax_attention(S, name, heads, q, k, v, key_tiles, dv, out, pt, prob):
    nc = S.nc
    keys = key_tiles * P
    per = P // dv
    scored, maxed, exped = S.sem(f"{name}_scored"), S.sem(f"{name}_maxed"), S.sem(f"{name}_exped")
    inverted, scaled = S.sem(f"{name}_inverted"), S.sem(f"{name}_scaled")
    turned, kept = S.sem(f"{name}_turned"), S.sem(f"{name}_kept")
    summed, out_done = S.sem(f"{name}_summed"), S.sem(f"{name}_out_done")
    items = [(h, i) for h in range(heads) for i in range(NT)]
    nmax = S.columns(len(items))
    total = S.columns(len(items))
    inv = S.columns(len(items))
    score_banks, turn_banks, out_banks = S.ps[0:3], S.ps[3:5], S.ps[5:7]
    with nc.Block() as block:
        @block.tensor
        def _(pe):
            def score(n):
                h, i = items[n]
                wait(pe, exped, n - 2)
                pe.matmul(score_banks[n % 3][:, 0:keys], q(h)[:, i * P:(i + 1) * P], k(h), start=True,
                          stop=True).then_inc(scored, 1)

            def turn(n):
                wait(pe, kept, n - 1)
                pe.wait_ge(scaled, n + 1)
                for b in range(key_tiles):
                    last = pe.transpose(turn_banks[n % 2][:, b * P:(b + 1) * P],
                                        prob[n % 3][:, b * P:(b + 1) * P], S.eye)
                last.then_inc(turned, 1)

            def weigh(h):
                o = h // per
                wait(pe, out_done, o - 1)
                pe.wait_ge(kept, NT * (h + 1))
                r = h % per * dv
                for b in range(key_tiles):
                    last = pe.matmul(out_banks[o % 2][r:r + dv, :], v(h, b), pt[h % 2][:, b, :],
                                     start=b == 0, stop=b == key_tiles - 1)
                last.then_inc(summed, 1)

            for n in range(len(items) + 2):
                if n == 0:
                    score(0)
                    score(1)
                if n + 2 < len(items):
                    score(n + 2)
                if n < len(items):
                    turn(n)
                if n >= 5 and (n - 5) % NT == 0:
                    weigh((n - 5) // NT)

        @block.vector
        def _(dve):
            def normalise(n):
                dve.wait_ge(exped, n + 1)
                dve.reciprocal(inv[:, n:n + 1], total[:, n:n + 1]).then_inc(inverted, 1)
                dve.wait_ge(inverted, n + 1)
                dve.tensor_scalar(prob[n % 3][:, 0:keys], prob[n % 3][:, 0:keys], inv[:, n:n + 1], None,
                                  ALU.mult).then_inc(scaled, 1)
            for n in range(len(items)):
                dve.wait_ge(scored, n + 1)
                dve.tensor_reduce(nmax[:, n:n + 1], score_banks[n % 3][:, 0:keys], AX.X, ALU.max,
                                  negate=True).then_inc(maxed, 1)
                if n >= 1:
                    normalise(n - 1)
            normalise(len(items) - 1)

        @block.scalar
        def _(act):
            def keep(n):
                h, i = items[n]
                act.wait_ge(turned, n + 1)
                wait(act, summed, h - 1)
                act.activation(pt[h % 2][:, 0:key_tiles, i * P:(i + 1) * P],
                               turn_banks[n % 2][:, 0:keys].rearrange("p (b t) -> p b t", b=key_tiles),
                               ACT.Copy).then_inc(kept, 1)

            def put(o):
                act.wait_ge(summed, per * (o + 1))
                act.activation(out[:, o, :], out_banks[o % 2][:, :], ACT.Copy).then_inc(out_done, 1)
            for n in range(len(items)):
                act.wait_ge(maxed, n + 1)
                wait(act, turned, n - 2)
                act.activation(prob[n % 3][:, 0:keys], score_banks[n % 3][:, 0:keys], ACT.Exp,
                               bias=nmax[:, n:n + 1], accum_out=total[:, n:n + 1]).then_inc(exped, 1)
                if n >= 2:
                    keep(n - 2)
                if n >= 8 and (n - 8) % (NT * per) == NT * per - 1:
                    put((n - 8) // (NT * per))
            keep(len(items) - 2)
            keep(len(items) - 1)
            done = len([n for n in range(8, len(items)) if (n - 8) % (NT * per) == NT * per - 1])
            for o in range(done, heads // per):
                put(o)


def head_norm(S, name, groups, width, src, rows, sq, parts, gain, tokens=NT, halves=False, extra=None,
              square=None, squares=1):
    nc = S.nc
    n = Norm(S, name, groups, width, tokens, halves)
    tk = tokens * P
    with nc.Block() as block:
        @block.scalar
        def _(act):
            square(act, n)
            n.roots(act, S.ps[0])

        @block.tensor
        def _(pe):
            n.sums(pe, S.ps[0], parts, squares)
            for g in range(groups):
                n.spread_group(pe, S.ps[1 + g % 3], g, rows, free_at=g - 2)

        @block.vector
        def _(dve):
            n.invert(dve)
            for g in range(groups):
                n.wait(dve, "spread", g + 1)
                bank = S.ps[1 + g % 3]
                if extra is not None:
                    extra(dve, g, bank, n)
                s = src(g)
                r = s.shape[0]
                dve.scalar_tensor_tensor(out=s, in0=s, scalar=gain[0:r, :], in1=bank[0:r, 0:tk],
                                         op0=ALU.mult, op1=ALU.mult).then_inc(n.sem("applied"), 1)
    n.end(squares, groups)


def first_block(S, w):
    nc, W = S.nc, S.W
    f = W.first
    model_norm(S, "norm1", S.x, VEC["norm_g"], S.ahi, S.alo, S.scratch)
    outer = ExitStack()
    with outer:
        def sbo(name, shape, dt=F32):
            return outer.enter_context(nc.sbuf_tensor(name, shape, dt))
        o_attn = sbo("o_attn", [P, 4, T])
        with ExitStack() as mla:
            def sb(name, shape, dt=F32):
                return mla.enter_context(nc.sbuf_tensor(name, shape, dt))
            qh = sb("q_heads", [QK, HEADS, T])
            kv = sb("kv_heads", [P, HEADS, T])
            v_tok = sb("v_tok", [P, NT, HEADS, DV])
            kpe = sb("k_rope", [QK, 3, T])
            lat = kv
            with ExitStack() as lat_scope:
                lhi = lat_scope.enter_context(nc.sbuf_tensor("latent_hi", [P, 5, T], F32R))
                llo = lat_scope.enter_context(nc.sbuf_tensor("latent_lo", [P, 5, T], F32R))
                project(S, "latent", [(lat[:, n, :], P, ACT.Copy) for n in range(5)] +
                        [(kpe[:, 0, :], QK, ACT.Copy)], f["latent"], (S.ahi, S.alo, T))
                model_norm(S, "q_latent", lat, VEC["q_norm_g"], lhi, llo, S.scratch, width=Q_RANK)
                model_norm(S, "kv_latent", lat[:, 3:5, :], VEC["kv_norm_g"], lhi[:, 3:5, :], llo[:, 3:5, :],
                           S.scratch, width=KV_RANK)
                up_project(S, qh, kv, lhi, llo)
            turn_values_and_rope(S, qh, kv, v_tok, kpe)
            p_scope = ExitStack()
            with p_scope:
                prob = [p_scope.enter_context(nc.sbuf_tensor(f"attn_prob{i}", [P, T], F32)) for i in range(3)]
                pt = [S.scratch[:, 0:4, :], S.scratch[:, 4:8, :]]
                softmax_attention(S, "mla", HEADS, lambda h: qh[:, h, :], lambda h: kv[0:QK, h, :],
                                  lambda h, b: v_tok[:, b, h, :], NT, DV, o_attn, pt, prob)
        o_mem = sbo("o_mem", [P, 4, T])
        memory_branch(S, w, o_mem)
        mix_branches(S, w, o_attn, o_mem)


def up_project(S, qh, kv, lhi, llo):
    nc, W = S.nc, S.W
    out_done, head_done = S.sem("up_out_done"), S.sem("up_head_done")
    uq, ukv = W.first["uq"], W.first["ukv"]
    n_units = 5
    with nc.Block() as block:
        @block.sync
        def _(sp):
            W.load(sp, uq + 2 * RING, uq + n_units + 2 * RING)

        @block.gpsimd
        def _(pool):
            W.split(pool, uq + RING, uq + n_units + RING)

        @block.tensor
        def _(pe):
            pe.wait_ge(W.split_done, uq + 3)
            for h in range(HEADS):
                wait(pe, out_done, h - 3)
                last = products(pe, S.ps[h % 4][0:QK, :], ((W.tile(uq + k, 0, h * QK, QK), (lhi[:, k, :], llo[:, k, :]))
                                                          for k in range(3)))
                last.then_inc(head_done, 1)
                if h == HEADS - 1:
                    pass
            pe.wait_ge(head_done, HEADS)
            pe.sem_inc(W.used, 3)
            pe.wait_ge(W.split_done, ukv + 2)
            for h in range(HEADS):
                wait(pe, out_done, HEADS + h - 3)
                products(pe, S.ps[h % 4][:, :], ((W.tile(ukv + k, 0, h * P, P), (lhi[:, 3 + k, :], llo[:, 3 + k, :]))
                                                 for k in range(2))).then_inc(head_done, 1)
            pe.wait_ge(head_done, 2 * HEADS)
            pe.sem_inc(W.used, 2)

        @block.scalar
        def _(act):
            for n in range(2 * HEADS):
                act.wait_ge(head_done, n + 1)
                h = n % HEADS
                dst, rows = (qh[:, h, :], QK) if n < HEADS else (kv[:, h, :], P)
                act.activation(dst, S.ps[n % 4][0:rows, :], ACT.Copy).then_inc(out_done, 1)


def turn_values_and_rope(S, qh, kv, v_tok, kpe):
    nc = S.nc
    turned, kept = S.sem("v_turned"), S.sem("v_kept")
    with nc.Block() as block:
        @block.tensor
        def _(pe):
            for h in range(HEADS):
                wait(pe, kept, h - 3)
                for i in range(NT):
                    last = pe.transpose(S.ps[h % 4][:, i * P:(i + 1) * P], kv[:, h, i * P:(i + 1) * P], S.eye)
                last.then_inc(turned, 1)

        @block.scalar
        def _(act):
            for h in range(HEADS):
                act.wait_ge(turned, h + 1)
                act.activation(v_tok[:, :, h, :], S.ps[h % 4][:, :].rearrange("p (i c) -> p i c", i=NT)[:, :, NOPE:P],
                               ACT.Copy).then_inc(kept, 1)

    sq = S.scratch

    def square_q(act, n):
        n.square(act, sq[0:QK, :, :], qh[:, :, :])
    head_norm(S, "q_head", HEADS, QK, lambda g: qh[:, g, :], QK, sq,
              lambda g: [(sq[0:QK, g, :], S.ones[0:QK, 0:1])], S.q_gain[:, 0:1], square=square_q)

    kg = S.vec[:, VEC["k_head_g"]:VEC["k_head_g"] + 1]
    r = slice(NOPE, QK)
    rope = S.sem("k_rope_steps")

    def square_k(act, n):
        n.square(act, sq[0:NOPE, :, :], kv[0:NOPE, :, :])
        act.wait_ge(rope, 1)
        act.activation(S.kpe_sq[r, :], kpe[r, 0, :], ACT.Square).then_inc(n.sem("squared"), 1)

    def rotate(dve, g, bank, n):
        if g == 0:
            n.wait(dve, "squared", 2)
            done = 1

            def step(ins):
                nonlocal done
                ins.then_inc(rope, 1)
                done += 1
                dve.wait_ge(rope, done)
            step(dve.tensor_scalar(kpe[r, 0, :], kpe[r, 0, :], kg[r, :], None, ALU.mult))
            step(dve.stream_shuffle(kpe[r, 1, :], kpe[r, 0, :], SWAP))
            step(dve.tensor_tensor(kpe[r, 0, :], kpe[r, 0, :], S.cos[r, :], ALU.mult))
            step(dve.tensor_tensor(kpe[r, 1, :], kpe[r, 1, :], S.sin[r, :], ALU.mult))
            step(dve.tensor_tensor(kpe[r, 2, :], kpe[r, 0, :], kpe[r, 1, :], ALU.add))
        dve.tensor_tensor(kv[r, g, :], kpe[r, 2, :], bank[r, :], ALU.mult).then_inc(rope, 1)

    q_rope = S.sem("q_rope_steps")
    with nc.Block() as block:
        @block.vector
        def _(dve):
            done = 0

            def step(ins):
                nonlocal done
                ins.then_inc(q_rope, 1)
                done += 1
                dve.wait_ge(q_rope, done)
            part = qh[r, :, :]
            swapped = S.scratch[r, :, :]
            step(dve.stream_shuffle(swapped.rearrange("p h t -> p (h t)"), part.rearrange("p h t -> p (h t)"), SWAP))
            cos = S.cos[r, :].unsqueeze(1).to_broadcast([ROPE, HEADS, T])
            sin = S.sin[r, :].unsqueeze(1).to_broadcast([ROPE, HEADS, T])
            step(dve.tensor_tensor(swapped, swapped, sin, ALU.mult))
            step(dve.tensor_tensor(part, part, cos, ALU.mult))
            step(dve.tensor_tensor(part, part, swapped, ALU.add))
            dve.sem_inc(rope, 1)

    head_norm(S, "k_head", HEADS, QK, lambda g: kv[0:NOPE, g, :], QK, sq,
              lambda g: [(sq[0:NOPE, g, :], S.ones[0:NOPE, 0:1]), (S.kpe_sq[r, :], S.ones[r, 0:1])],
              kg, extra=rotate, square=square_k, squares=2)


def memory_branch(S, w, o_mem):
    nc, W = S.nc, S.W
    with ExitStack() as scope:
        def sb(name, shape, dt=F32):
            return scope.enter_context(nc.sbuf_tensor(name, shape, dt))
        qm = sb("mem_q", [P, MEM_HEADS, T])
        memT = sb("mem_t", [P, ND, M])
        mkv = sb("mem_kv", [P, 2 * MEM_HEADS, M])
        mv = sb("mem_v", [P, NM, MEM_HEADS, P])
        mhi, mlo = sb("mem_hi", [P, ND, M], F32R), sb("mem_lo", [P, ND, M], F32R)
        prob = [sb(f"mem_prob{i}", [P, M]) for i in range(3)]
        mem_loaded, turned, copied = S.sem("memory_loaded"), S.sem("memory_turned"), S.sem("memory_copied")
        tok = S.scratch[:, 0:4, :].rearrange("p a t -> p (a t)").rearrange("p (i d) -> p i d", i=NM)
        with nc.Block() as block:
            @block.sync
            def _(sp):
                sp.dma_start(tok, w["mem"][0].rearrange("(i p) d -> p i d", p=P)).then_inc(mem_loaded, 16)

            @block.tensor
            def _(pe):
                pe.wait_ge(mem_loaded, 16)
                for c in range(ND):
                    wait(pe, copied, c - 3)
                    for i in range(NM):
                        last = pe.transpose(S.ps[c % 4][:, i * P:(i + 1) * P], tok[:, i, c * P:(c + 1) * P], S.eye)
                    last.then_inc(turned, 1)

            @block.scalar
            def _(act):
                for c in range(ND):
                    act.wait_ge(turned, c + 1)
                    act.activation(memT[:, c, :], S.ps[c % 4][:, 0:M], ACT.Copy).then_inc(copied, 1)
        model_norm(S, "mem_norm", memT, VEC["mem_norm_g"], mhi, mlo, S.scratch, tokens=NM)
        project(S, "qmem", [(qm[:, n, :], P, ACT.Copy) for n in range(MEM_HEADS)], W.first["qmem"],
                (S.ahi, S.alo, T))
        project(S, "mkv", [(mkv[:, n, :], P, ACT.Copy) for n in range(2 * MEM_HEADS)], W.first["mkv"],
                (mhi, mlo, M))
        v_turned, v_kept = S.sem("mem_v_turned"), S.sem("mem_v_kept")
        with nc.Block() as block:
            @block.tensor
            def _(pe):
                for h in range(MEM_HEADS):
                    for i in range(NM):
                        last = pe.transpose(S.ps[h][:, i * P:(i + 1) * P], mkv[:, 2 * h + 1, i * P:(i + 1) * P], S.eye)
                    last.then_inc(v_turned, 1)

            @block.scalar
            def _(act):
                for h in range(MEM_HEADS):
                    act.wait_ge(v_turned, h + 1)
                    act.activation(mv[:, :, h, :], S.ps[h][:, 0:M].rearrange("p (i c) -> p i c", i=NM),
                                   ACT.Copy).then_inc(v_kept, 1)
        sq = S.scratch
        head_norm(S, "mem_q_norm", MEM_HEADS, P, lambda g: qm[:, g, :], P, sq,
                  lambda g: [(sq[:, g, :], S.ones[:, 0:1])], S.mq_gain[:, 0:1],
                  square=lambda act, n: n.square(act, sq[:, 0:4, :], qm[:, :, :]))
        head_norm(S, "mem_k_norm", MEM_HEADS, P, lambda g: mkv[:, 2 * g, :], P, sq,
                  lambda g: [(sq[:, g, 0:M], S.ones[:, 0:1])], S.vec[:, VEC["mem_k_g"]:VEC["mem_k_g"] + 1],
                  tokens=NM, square=lambda act, n: n.square(act, sq[:, 0:4, 0:M], mkv[:, 0:8:2, :]))
        softmax_attention(S, "mem", MEM_HEADS, lambda h: qm[:, h, :], lambda h: mkv[:, 2 * h, :],
                          lambda h, b: mv[:, b, h, :], NM, P, o_mem,
                          [S.scratch[:, 0:4, :], S.scratch[:, 4:8, :]], prob)


def mix_branches(S, w, o_attn, o_mem):
    nc, W = S.nc, S.W
    with ExitStack() as scope:
        def sb(name, shape, dt=F32):
            return scope.enter_context(nc.sbuf_tensor(name, shape, dt))
        ohi, olo = sb("o_hi", [P, 12, T], F32R), sb("o_lo", [P, 12, T], F32R)
        with ExitStack() as conv_scope:
            def sbc(name, shape, dt=F32):
                return conv_scope.enter_context(nc.sbuf_tensor(name, shape, dt))
            cc, z = sbc("conv_c", [P, T]), sbc("conv_z", [P, T + 2])
            gate, acc = sbc("conv_gate", [P, T]), sbc("conv_acc", [P, T])
            c_kept, gated, hi_done = S.sem("conv_c_kept"), S.sem("conv_gate_done"), S.sem("conv_hi_done")
            steps, tile_done, padded = S.sem("conv_steps"), S.sem("conv_tile_done"), S.sem("conv_padded")
            u0 = W.first["conv"]
            with nc.Block() as block:
                @block.sync
                def _(sp):
                    W.load(sp, u0 + 2 * RING, u0 + 16 + 2 * RING)

                @block.gpsimd
                def _(pool):
                    W.split(pool, u0 + RING, u0 + 16 + RING)

                @block.tensor
                def _(pe):
                    for t in range(4):
                        wait(pe, tile_done, t - 1)
                        for j in range(4):
                            u = u0 + 4 * t + j
                            pe.wait_ge(W.split_done, u + 1)
                            products(pe, S.ps[t % 2 * 4 + j][:, :], ((W.tile(u, k), (S.ahi[:, k, :], S.alo[:, k, :]))
                                                                     for k in range(ND))).then_inc(W.used, 1)

                @block.scalar
                def _(act):
                    for t in range(4):
                        b = S.ps[t % 2 * 4:t % 2 * 4 + 4]
                        act.wait_ge(W.used, u0 + 4 * t + 1)
                        wait(act, steps, 6 * (t - 1) + 1)
                        act.activation(cc[:, :], b[0][:, :], ACT.Copy).then_inc(c_kept, 1)
                        act.wait_ge(W.used, u0 + 4 * t + 4)
                        wait(act, tile_done, t)
                        act.activation(gate[:, :], b[3][:, :], ACT.Silu).then_inc(gated, 1)
                        act.wait_ge(steps, 6 * t + 6)
                        act.activation(ohi[:, 4 + t, :], acc[:, :], ACT.Copy).then_inc(hi_done, 1)

                @block.vector
                def _(dve):
                    dve.memset(z[:, 0:1], 0.0).then_inc(padded, 1)
                    dve.memset(z[:, T + 1:T + 2], 0.0).then_inc(padded, 1)
                    dve.wait_ge(padded, 2)
                    n = 0

                    def step(ins):
                        nonlocal n
                        ins.then_inc(steps, 1)
                        n += 1
                        dve.wait_ge(steps, n)
                    for t in range(4):
                        b = S.ps[t % 2 * 4:t % 2 * 4 + 4]

                        def tap(k):
                            c = VEC["conv_w"] + 4 * k + t
                            return S.vec[:, c:c + 1]
                        c = VEC["conv_b"] + t
                        dve.wait_ge(c_kept, t + 1)
                        dve.wait_ge(W.used, u0 + 4 * t + 3)
                        step(dve.tensor_tensor(z[:, 1:T + 1], cc[:, :], b[1][:, :], ALU.mult))
                        step(dve.tensor_scalar(acc[:, :], z[:, 0:T], tap(0), S.vec[:, c:c + 1], ALU.mult, ALU.add))
                        for k in (1, 2):
                            step(dve.scalar_tensor_tensor(out=acc[:, :], in0=z[:, k:T + k], scalar=tap(k),
                                                          in1=acc[:, :], op0=ALU.mult, op1=ALU.add))
                        step(dve.tensor_tensor(acc[:, :], acc[:, :], b[2][:, :], ALU.mult))
                        dve.wait_ge(gated, t + 1)
                        step(dve.tensor_tensor(acc[:, :], acc[:, :], gate[:, :], ALU.mult))
                        dve.wait_ge(hi_done, t + 1)
                        dve.tensor_tensor(olo[:, 4 + t, :], acc[:, :], ohi[:, 4 + t, :].bitcast(F32),
                                          ALU.subtract).then_inc(tile_done, 1)
                        dve.wait_ge(tile_done, t + 1)
        u0 = W.first["gates"]
        silu = [sb(f"branch_gate{i}", [P, T]) for i in range(2)]
        silu_done, prod, hi2, lo2 = S.sem("gate_silu"), S.sem("gate_product"), S.sem("gate_hi"), S.sem("gate_lo")
        with nc.Block() as block:
            @block.sync
            def _(sp):
                W.load(sp, u0 + 2 * RING, u0 + 8 + 2 * RING)

            @block.gpsimd
            def _(pool):
                W.split(pool, u0 + RING, u0 + 8 + RING)

            @block.tensor
            def _(pe):
                for n in range(8):
                    pe.wait_ge(W.split_done, u0 + n + 1)
                    wait(pe, silu_done, n - 3)
                    products(pe, S.ps[n % 4][:, :], ((W.tile(u0 + n, k), (S.ahi[:, k, :], S.alo[:, k, :]))
                                                     for k in range(ND))).then_inc(W.used, 1)

            @block.scalar
            def _(act):
                for n in range(9):
                    if n < 8:
                        act.wait_ge(W.used, u0 + n + 1)
                        wait(act, prod, n - 1)
                        act.activation(silu[n % 2][:, :], S.ps[n % 4][:, :], ACT.Silu).then_inc(silu_done, 1)
                    if n >= 1:
                        o = o_attn if n <= 4 else o_mem
                        t = (n - 1) % 4
                        act.wait_ge(prod, n)
                        act.activation(ohi[:, (0 if n <= 4 else 8) + t, :], o[:, t, :], ACT.Copy).then_inc(hi2, 1)

            @block.vector
            def _(dve):
                for n in range(9):
                    if n < 8:
                        o, t = (o_attn if n < 4 else o_mem), n % 4
                        dve.wait_ge(silu_done, n + 1)
                        dve.tensor_tensor(o[:, t, :], o[:, t, :], silu[n % 2][:, :], ALU.mult).then_inc(prod, 1)
                    if n >= 1:
                        o, t = (o_attn if n <= 4 else o_mem), (n - 1) % 4
                        dve.wait_ge(hi2, n)
                        dve.wait_ge(prod, n)
                        c = (0 if n <= 4 else 8) + t
                        dve.tensor_tensor(olo[:, c, :], o[:, t, :], ohi[:, c, :].bitcast(F32),
                                          ALU.subtract).then_inc(lo2, 1)
        u0 = W.first["mix"]
        rt = [sb(f"mix_r{i}", [P, T]) for i in range(2)]
        tmp = sb("mix_term", [P, T])
        r_done, gated, summed = S.sem("mix_r_done"), S.sem("mix_gated"), S.sem("mix_summed")
        with nc.Block() as block:
            @block.sync
            def _(sp):
                W.load(sp, u0 + 2 * RING, u0 + 48 + 2 * RING)

            @block.gpsimd
            def _(pool):
                W.split(pool, u0 + RING, u0 + 48 + RING)

            @block.tensor
            def _(pe):
                for i in rounds(pe, 4):
                    for j in range(12):
                        m, kind = divmod(j, 6)
                        branch = kind // 2
                        pe.wait_ge(W.split_done, i * 12 + (u0 + j + 1))
                        if kind % 2 == 0:
                            wait(pe, r_done, i * 6 + (3 * m + branch - 2))
                            pairs = ((W.tile(u0 + j, k), (S.ahi[:, k, :], S.alo[:, k, :])) for k in range(ND))
                        else:
                            wait(pe, gated, i * 6 + (3 * m + branch - 2))
                            pairs = ((W.tile(u0 + j, k), (ohi[:, 4 * branch + k, :], olo[:, 4 * branch + k, :]))
                                     for k in range(4))
                        products(pe, S.ps[kind][:, :], pairs).then_inc(W.used, 1)

            @block.scalar
            def _(act):
                for i in rounds(act, 8):
                    for b in range(3):
                        act.wait_ge(W.used, i * 6 + (u0 + 2 * b + 1))
                        wait(act, gated, i * 3 + (b - 1))
                        c = S.vec[:, VEC["b_gate"] + 8 * b + i:VEC["b_gate"] + 8 * b + i + 1] if isinstance(i, int) \
                            else S.vec[:, bass.ds(i + (VEC["b_gate"] + 8 * b), 1)]
                        act.activation(S.mix_r[b][:, :], S.ps[2 * b][:, :], ACT.Sigmoid, bias=c).then_inc(r_done, 1)

            @block.vector
            def _(dve):
                for i in rounds(dve, 8):
                    y = S.scratch[:, i, :] if isinstance(i, int) else \
                        S.scratch[:, bass.ds(i, 1), :].rearrange("p a t -> p (a t)")
                    for b in range(3):
                        dve.wait_ge(W.used, i * 6 + (u0 + 2 * b + 2))
                        dve.wait_ge(r_done, i * 3 + (b + 1))
                        wait(dve, summed, i * 2 + (b - 1))
                        dst = y if b == 0 else tmp[:, :]
                        dve.tensor_tensor(dst, S.mix_r[b][:, :], S.ps[2 * b + 1][:, :], ALU.mult).then_inc(gated, 1)
                        if b:
                            dve.wait_ge(gated, i * 3 + (b + 1))
                            dve.tensor_tensor(y, y, tmp[:, :], ALU.add).then_inc(summed, 1)
    hi3, lo3 = S.sem("y_hi"), S.sem("y_lo")
    split_tiles(S, S.scratch, S.ahi, S.alo, hi3, lo3)
    add_to_x(S, "first_out", W.first["out"], S.ahi, S.alo)


def split_tiles(S, src, hi, lo, hi_done, lo_done):
    with S.nc.Block() as block:
        @block.scalar
        def _(act):
            for t in range(ND):
                act.activation(hi[:, t, :], src[:, t, :], ACT.Copy).then_inc(hi_done, 1)

        @block.vector
        def _(dve):
            for t in range(ND):
                dve.wait_ge(hi_done, t + 1)
                dve.tensor_tensor(lo[:, t, :], src[:, t, :], hi[:, t, :].bitcast(F32), ALU.subtract).then_inc(lo_done, 1)


def stick_breaking(S):
    nc, W = S.nc, S.W
    model_norm(S, "norm2", S.x, VEC["norm_gains_2"], S.ahi, S.alo, S.scratch)
    with ExitStack() as scope:
        def sb(name, shape, dt=F32):
            return scope.enter_context(nc.sbuf_tensor(name, shape, dt))
        qkv = sb("sb_qkv", [P, 24, T])
        v_tok = sb("sb_v_tok", [P, NT, D])
        stay = [sb(f"sb_stay{i}", [P, T]) for i in range(2)]
        beta = [sb(f"sb_beta{i}", [P, T]) for i in range(2)]
        left = [sb(f"sb_left{i}", [P, T + 1]) for i in range(2)]
        zeros = sb("sb_zeros", [P, T])
        project_loop(S, "qkv", W.first["qkv"], [(qkv, ACT.Copy, 24)], S.ahi, S.alo)
        turned, kept, zeroed = S.sem("sb_v_turned"), S.sem("sb_v_kept"), S.sem("sb_zeroed")
        with nc.Block() as block:
            @block.gpsimd
            def _(pool):
                pool.memset(zeros[:, :], 0.0).then_inc(zeroed, 1)
                for l in left:
                    pool.memset(l[:, T:T + 1], 1.0).then_inc(zeroed, 1)

            @block.tensor
            def _(pe):
                for c in range(ND):
                    wait(pe, kept, c - 3)
                    for i in range(NT):
                        last = pe.transpose(S.ps[c % 4][:, i * P:(i + 1) * P], qkv[:, 16 + c, i * P:(i + 1) * P], S.eye)
                    last.then_inc(turned, 1)

            @block.scalar
            def _(act):
                for c in range(ND):
                    act.wait_ge(turned, c + 1)
                    act.activation(v_tok[:, :, c * P:(c + 1) * P], S.ps[c % 4][:, :].rearrange("p (i c) -> p i c", i=NT),
                                   ACT.Copy).then_inc(kept, 1)
        sq = S.scratch
        for name, first in (("sb_q", 0), ("sb_k", 8)):
            g = VEC[f"{name}_gain_2"]
            head_norm(S, f"{name}_norm", 8, SB_DIM, lambda t: qkv[:, first + t, :], P, sq,
                      lambda t: [(sq[:, t, :], S.const[:, K_HALVES:K_HALVES + 2])], S.vec[:, g:g + 1], halves=True,
                      square=lambda act, n: n.square(act, sq[:, :, :], qkv[:, first:first + 8, :]))
        items = [(h, i) for h in range(SB_HEADS) for i in range(NT)]
        pt = [S.scratch[:, 0:4, :], S.scratch[:, 4:8, :]]
        names = ("scored", "masked", "sigmoids", "scanned", "weighted", "turned2", "kept2", "summed", "out_hi", "out_lo")
        scored, masked, sig, scanned, weighted, turned2, kept2, summed, out_hi, out_lo = (S.sem(f"sb_{x}") for x in names)
        score_banks, turn_banks, out_banks = S.ps[0:3], S.ps[3:5], S.ps[5:7]
        scale = SB_DIM ** -0.5
        N = len(items)
        with nc.Block() as block:
            @block.tensor
            def _(pe):
                def score(n):
                    h, i = items[n]
                    r = slice(h % 2 * 64, h % 2 * 64 + 64)
                    wait(pe, sig, n - 2)
                    pe.matmul(score_banks[n % 3][:, 0:(i + 1) * P], qkv[r, h // 2, i * P:(i + 1) * P],
                              qkv[r, 8 + h // 2, 0:(i + 1) * P], start=True, stop=True).then_inc(scored, 1)

                def turn(n):
                    h, i = items[n]
                    wait(pe, kept2, n - 1)
                    pe.wait_ge(weighted, n + 1)
                    a = T - (i + 1) * P
                    for b in range(i + 1):
                        last = pe.transpose(turn_banks[n % 2][:, b * P:(b + 1) * P],
                                            beta[n % 2][:, a + b * P:a + (b + 1) * P], S.eye)
                    last.then_inc(turned2, 1)

                def weigh(h):
                    o = h // 2
                    wait(pe, out_lo, o - 1)
                    pe.wait_ge(kept2, NT * (h + 1))
                    r = h % 2 * 64
                    for b in range(NT):
                        last = pe.matmul(out_banks[o % 2][r:r + 64, b * P:T], v_tok[:, b, h * 64:(h + 1) * 64],
                                         pt[h % 2][:, b, b * P:T], start=b == 0, stop=b == NT - 1)
                    last.then_inc(summed, 1)
                score(0)
                score(1)
                for n in range(N):
                    if n + 2 < N:
                        score(n + 2)
                    turn(n)
                    if n >= 5 and (n - 5) % NT == 0:
                        weigh((n - 5) // NT)
                weigh(SB_HEADS - 1)

            @block.vector
            def _(dve):
                def mask(n):
                    h, i = items[n]
                    dve.wait_ge(scored, n + 1)
                    diag = score_banks[n % 3][:, i * P:(i + 1) * P]
                    dve.tensor_tensor(diag, diag, S.const[:, K_CAUSAL:K_CAUSAL + P], ALU.add).then_inc(masked, 1)

                def weigh(n):
                    h, i = items[n]
                    a = T - (i + 1) * P
                    dve.wait_ge(sig, n + 1)
                    wait(dve, weighted, n - 1)
                    rev = slice(None, None, -1)
                    dve.tensor_tensor_scan(left[n % 2][:, a:T][:, rev], stay[n % 2][:, a:T][:, rev], zeros[:, a:T],
                                           1.0, ALU.mult, ALU.add).then_inc(scanned, 1)
                    dve.wait_ge(scanned, n + 1)
                    dve.tensor_tensor(beta[n % 2][:, a:T], beta[n % 2][:, a:T], left[n % 2][:, a + 1:T + 1],
                                      ALU.mult).then_inc(weighted, 1)

                def lower(o):
                    dve.wait_ge(out_hi, o + 1)
                    dve.tensor_tensor(S.alo[:, o, :], out_banks[o % 2][:, :], S.ahi[:, o, :].bitcast(F32),
                                      ALU.subtract).then_inc(out_lo, 1)
                mask(0)
                for n in range(N):
                    if n + 1 < N:
                        mask(n + 1)
                    weigh(n)
                    if n >= 8 and (n - 8) % 8 == 7:
                        lower((n - 8) // 8)
                lower(SB_HEADS // 2 - 1)

            @block.scalar
            def _(act):
                def keep(n):
                    h, i = items[n]
                    act.wait_ge(turned2, n + 1)
                    wait(act, summed, h - 1)
                    act.activation(pt[h % 2][:, 0:i + 1, i * P:(i + 1) * P],
                                   turn_banks[n % 2][:, 0:(i + 1) * P].rearrange("p (b t) -> p b t", b=i + 1),
                                   ACT.Copy).then_inc(kept2, 1)

                def put(o):
                    act.wait_ge(summed, 2 * (o + 1))
                    act.activation(S.ahi[:, o, :], out_banks[o % 2][:, :], ACT.Copy).then_inc(out_hi, 1)
                for n in range(N):
                    h, i = items[n]
                    a = T - (i + 1) * P
                    src = score_banks[n % 3][:, 0:(i + 1) * P]
                    act.wait_ge(masked, n + 1)
                    wait(act, turned2, n - 1)
                    act.activation(stay[n % 2][:, a:T], src, ACT.Sigmoid, scale=-scale)
                    act.activation(beta[n % 2][:, a:T], src, ACT.Sigmoid, scale=scale).then_inc(sig, 1)
                    if n >= 1:
                        keep(n - 1)
                    if n >= 7 and (n - 7) % 8 == 7:
                        put((n - 7) // 8)
                keep(N - 1)
                put(SB_HEADS // 2 - 1)
        add_to_x(S, "sb_out", W.first["sbo"], S.ahi, S.alo)


def mlp(S, layer):
    nc, W = S.nc, S.W
    model_norm(S, f"mlp_norm{layer}", S.x, VEC["norm_gains_2"] + 16 * layer + 8, S.ahi, S.alo, S.scratch)
    with ExitStack() as scope:
        def sb(name, shape, dt=F32):
            return scope.enter_context(nc.sbuf_tensor(f"{name}{layer}", shape, dt))
        hhi = [sb(f"hidden_hi{i}_", [P, 4, T], F32R) for i in range(2)]
        hlo = [sb(f"hidden_lo{i}_", [P, 4, T], F32R) for i in range(2)]
        relu = [sb(f"hidden_relu{i}_", [P, T]) for i in range(4)]
        squ = [sb(f"hidden_square{i}_", [P, T]) for i in range(4)]
        names = ("relu_done", "hi_done", "square_done", "lo_done", "added")
        relu_done, hi_done, square_done, lo_done, added = (S.shared(f"mlp_{x}")[0] for x in names)
        tiles0, sums0 = 32 * layer, 64 * layer
        u0 = W.first[f"mlp{layer}head"]
        GROUPS = 8

        def order(eng, up, down):
            up(0, 0, u0, 0)
            for i in eng_rounds(eng, 3):
                b = u0 + 4
                up(i, 1, b, 1)
                down(i, 0, b + 4, 0)
                up(i, 2, b + 8, 0)
                down(i, 1, b + 12, 1)
            b = u0 + 52
            up(0, 7, b, 1)
            down(0, 6, b + 4, 0)
            down(0, 7, b + 8, 1)

        eng_rounds = rounds

        with nc.Block() as block:
            @block.sync
            def _(sp):
                W.load(sp, u0 + 2 * RING, u0 + 64 + 2 * RING)

            @block.gpsimd
            def _(pool):
                W.split(pool, u0 + RING, u0 + 64 + RING)

            @block.tensor
            def _(pe):
                def up(i, c, b, half):
                    for r in range(4):
                        pe.wait_ge(W.split_done, i * 16 + (b + r + 1))
                        wait(pe, relu_done, i * 8 + (tiles0 + 4 * c + r - 3))
                        products(pe, S.ps[r][:, :], ((W.tile(b + r, k), (S.ahi[:, k, :], S.alo[:, k, :]))
                                                     for k in range(ND))).then_inc(W.used, 1)

                def down(i, c, b, half):
                    wait(pe, lo_done, i * 8 + (tiles0 + 4 * c + 4))
                    for r in range(4):
                        pe.wait_ge(W.split_done, i * 16 + (b + r + 1))
                        wait(pe, added, i * 16 + (sums0 + 8 * c + 2 * r - 2))
                        for m in range(2):
                            last = products(pe, S.ps[4 + r % 2 * 2 + m][:, :],
                                            ((W.tile(b + r, k, m * P, P, 256), (hhi[half][:, k, :], hlo[half][:, k, :]))
                                             for k in range(4)))
                        last.then_inc(W.used, 1)
                order(pe, up, down)

            @block.scalar
            def _(act):
                def up(i, c, b, half):
                    for r in range(4):
                        act.wait_ge(W.used, i * 16 + (b + r + 1))
                        wait(act, lo_done, i * 8 + (tiles0 + 4 * c + r - 3))
                        act.activation(relu[r][:, :], S.ps[r][:, :], ACT.Relu).then_inc(relu_done, 1)
                        act.wait_ge(relu_done, i * 8 + (tiles0 + 4 * c + r + 1))
                        act.activation(hhi[half][:, r, :], relu[r][:, :], ACT.Square).then_inc(hi_done, 1)
                order(act, up, lambda *a: None)

            @block.vector
            def _(dve):
                def up(i, c, b, half):
                    for r in range(4):
                        dve.wait_ge(relu_done, i * 8 + (tiles0 + 4 * c + r + 1))
                        wait(dve, lo_done, i * 8 + (tiles0 + 4 * c + r - 3))
                        dve.tensor_tensor(squ[r][:, :], relu[r][:, :], relu[r][:, :], ALU.mult).then_inc(square_done, 1)
                        dve.wait_ge(hi_done, i * 8 + (tiles0 + 4 * c + r + 1))
                        dve.wait_ge(square_done, i * 8 + (tiles0 + 4 * c + r + 1))
                        dve.tensor_tensor(hlo[half][:, r, :], squ[r][:, :], hhi[half][:, r, :].bitcast(F32),
                                          ALU.subtract).then_inc(lo_done, 1)

                def down(i, c, b, half):
                    for r in range(4):
                        dve.wait_ge(W.used, i * 16 + (b + r + 1))
                        for m in range(2):
                            t = 2 * r + m
                            wait(dve, added, i * 16 + (sums0 + 8 * c + t - 7))
                            dve.tensor_tensor(S.x[:, t, :], S.x[:, t, :], S.ps[4 + r % 2 * 2 + m][:, :],
                                              ALU.add).then_inc(added, 1)
                order(dve, up, down)


def hgrn(S):
    nc, W = S.nc, S.W
    model_norm(S, "hg_norm_in", S.x, VEC["norm_gains_2"] + 16, S.ahi, S.alo, S.scratch)
    with ExitStack() as scope:
        def sb(name, shape, dt=F32):
            return scope.enter_context(nc.sbuf_tensor(name, shape, dt))
        qs, fs, vs, gs = (sb(f"hg_{x}", [P, ND, T]) for x in ("q", "f", "v", "g"))
        kk = [sb(f"hg_k{i}", [P, T]) for i in range(2)]
        st = [sb(f"hg_scores{i}", [P, NT, P]) for i in range(2)]
        project_loop(S, "hgin", W.first["hgin"], [(qs, ACT.Silu, 8), (fs, ACT.Sigmoid, 8), (vs, ACT.Copy, 8),
                                                  (gs, ACT.Sigmoid, 8)], S.ahi, S.alo)
        turned, kept, forget = S.sem("hg_v_turned"), S.sem("hg_v_kept"), S.sem("hg_forget")
        with nc.Block() as block:
            @block.vector
            def _(dve):
                dve.tensor_scalar(S.lb1[:, :], S.lb[:, :], -1.0, 1.0, ALU.mult, ALU.add).then_inc(forget, 1)
                dve.wait_ge(forget, 1)
                for h in range(HG_HEADS):
                    dve.tensor_scalar(fs[:, h, :], fs[:, h, :], S.lb1[:, h:h + 1], S.lb[:, h:h + 1], ALU.mult,
                                      ALU.add).then_inc(forget, 1)

            @block.tensor
            def _(pe):
                for h in range(HG_HEADS):
                    wait(pe, kept, h - 3)
                    for c in range(NT):
                        last = pe.transpose(S.ps[h % 4][:, c * P:(c + 1) * P], vs[:, h, c * P:(c + 1) * P], S.eye)
                    last.then_inc(turned, 1)

            @block.scalar
            def _(act):
                for h in range(HG_HEADS):
                    act.wait_ge(turned, h + 1)
                    act.activation(vs[:, h, :], S.ps[h % 4][:, :], ACT.Copy).then_inc(kept, 1)
        pre, suf = S.scratch[:, 0, :], S.scratch[:, 1, :]
        ql, kl = [S.scratch[:, 2, :], S.scratch[:, 3, :]], [S.scratch[:, 4, :], S.scratch[:, 5, :]]
        k_tok, state = S.scratch[:, 6, :], S.scratch[:, 7, 0:3 * P].rearrange("p (c v) -> p c v", c=3)
        names = ("zeroed", "key", "suffix", "prefix", "q_ready", "k_ready", "scored", "picked", "k_turned", "k_kept",
                 "update", "stated", "out", "out_kept")
        (zeroed, key, suffix, prefix, q_ready, k_ready, scored, picked, k_turned, k_kept, update, stated, out,
         out_kept) = (S.sem(f"hg_{x}") for x in names)
        H = HG_HEADS
        LV = LEVELS + 1
        with nc.Block() as block:
            def halves(ap, level):
                v = ap.rearrange("p (b s h) -> p b s h", s=2, h=1 << level)
                return v[:, :, 0, :], v[:, :, 1, :]

            @block.gpsimd
            def _(pool):
                for b in (*ql, *kl):
                    pool.memset(b, 0.0).then_inc(zeroed, 1)
                pool.wait_ge(zeroed, 4)
                for h in range(H):
                    for level in range(LEVELS):
                        n = h * (LEVELS + 1) + level
                        _, qr = halves(qs[:, h, :], level)
                        kleft, _ = halves(kk[h % 2][:, :], level)
                        _, pr = halves(pre, level)
                        ul, _ = halves(suf, level)
                        pool.wait_ge(prefix, h * (LEVELS + 1) + level + 1)
                        wait(pool, scored, h * LV + level)
                        pool.tensor_tensor(halves(ql[n % 2], level)[1], qr, pr, ALU.mult).then_inc(q_ready, 1)
                        pool.tensor_tensor(halves(kl[n % 2], level)[0], kleft, ul, ALU.mult).then_inc(k_ready, 1)
                    n = h * (LEVELS + 1) + LEVELS
                    pool.wait_ge(prefix, (h + 1) * (LEVELS + 1))
                    pool.wait_ge(scored, h * LV + LEVELS)
                    pool.tensor_tensor(ql[n % 2], qs[:, h, :], pre, ALU.mult).then_inc(q_ready, 1)
                    pool.tensor_tensor(kl[n % 2], kk[h % 2][:, :], suf, ALU.mult).then_inc(k_ready, 1)

            @block.vector
            def _(dve):
                def start(h):
                    wait(dve, k_ready, h * (LEVELS + 1))
                    wait(dve, stated, 3 * h)
                    dve.tensor_scalar(kk[h % 2][:, :], fs[:, h, :], -1.0, 1.0, ALU.mult, ALU.add).then_inc(key, 1)
                    dve.memset(suf, 1.0).then_inc(suffix, 1)
                    dve.tensor_copy(pre, fs[:, h, :]).then_inc(prefix, 1)

                def grow(h, level):
                    d = 1 << level
                    n = h * (LEVELS + 1) + level + 1
                    dve.wait_ge(k_ready, n)
                    dve.wait_ge(q_ready, n)
                    dve.wait_ge(prefix, n)
                    dve.wait_ge(suffix, n)
                    ul, _ = halves(suf, level)
                    pl, pr = halves(pre, level)
                    total = pr[:, :, d - 1:d].to_broadcast([P, T // (2 * d), d])
                    dve.tensor_tensor(ul, ul, total, ALU.mult).then_inc(suffix, 1)
                    dve.wait_ge(suffix, n + 1)
                    ltotal = pl[:, :, d - 1:d].to_broadcast([P, T // (2 * d), d])
                    dve.tensor_tensor(pr, pr, ltotal, ALU.mult).then_inc(prefix, 1)

                def pick(h, level):
                    n = h * LV + level
                    dve.wait_ge(scored, n + 1)
                    bank = S.ps[n % 3][:, :].rearrange("p (c t) -> p c t", c=NT)
                    if level == 0:
                        wait(dve, out, h - 1)
                        m = S.const[:, K_EYE:K_EYE + P].unsqueeze(1).to_broadcast([P, NT, P])
                        dve.tensor_tensor(st[h % 2][:, :, :], bank, m, ALU.mult).then_inc(picked, 1)
                    else:
                        dve.wait_ge(picked, n)
                        a = K_LEVEL + (level - 1) * P
                        m = S.const[:, a:a + P].bitcast(I32).unsqueeze(1).to_broadcast([P, NT, P])
                        dve.copy_predicated(st[h % 2][:, :, :], m, bank).then_inc(picked, 1)

                def states(h):
                    dve.wait_ge(update, h + 1)
                    wait(dve, out, h)
                    dve.wait_ge(prefix, (h + 1) * (LEVELS + 1))
                    dve.tensor_copy(state[:, 0, :], S.ps[3][:, 0:P]).then_inc(stated, 1)
                    for c in (1, 2):
                        dve.wait_ge(stated, 3 * h + c)
                        dve.scalar_tensor_tensor(out=state[:, c, :], in0=state[:, c - 1, :],
                                                 scalar=pre[:, (c + 1) * P - 1:(c + 1) * P],
                                                 in1=S.ps[3][:, c * P:(c + 1) * P], op0=ALU.mult,
                                                 op1=ALU.add).then_inc(stated, 1)
                for h in range(H):
                    start(h)
                    for level in range(LEVELS):
                        if level >= 1:
                            pick(h, level - 1)
                        grow(h, level)
                    pick(h, LEVELS - 1)
                    pick(h, LEVELS)
                    states(h)

            @block.tensor
            def _(pe):
                def score(h, level):
                    n = h * LV + level
                    wait(pe, picked, n - 2)
                    if level == 0:
                        pe.wait_ge(key, h + 1)
                        q, k = qs[:, h, :], kk[h % 2][:, :]
                    else:
                        m = h * (LEVELS + 1) + level - 1
                        pe.wait_ge(q_ready, m + 1)
                        pe.wait_ge(k_ready, m + 1)
                        q, k = ql[m % 2], kl[m % 2]
                    for c in range(NT):
                        last = pe.matmul(S.ps[n % 3][:, c * P:(c + 1) * P], k[:, c * P:(c + 1) * P],
                                         q[:, c * P:(c + 1) * P], start=True, stop=True)
                    last.then_inc(scored, 1)
                for h in range(H):
                    for level in range(LV):
                        score(h, level)
                    m = h * (LEVELS + 1) + LEVELS
                    pe.wait_ge(k_ready, m + 1)
                    for c in range(NT):
                        last = pe.transpose(S.ps[4][:, c * P:(c + 1) * P], kl[m % 2][:, c * P:(c + 1) * P], S.eye)
                    last.then_inc(k_turned, 1)
                    pe.wait_ge(k_kept, h + 1)
                    wait(pe, stated, 3 * h)
                    for c in range(NT - 1):
                        last = pe.matmul(S.ps[3][:, c * P:(c + 1) * P], k_tok[:, c * P:(c + 1) * P],
                                         vs[:, h, c * P:(c + 1) * P], start=True, stop=True)
                    last.then_inc(update, 1)
                    wait(pe, out_kept, h - 1)
                    pe.wait_ge(picked, LV * (h + 1))
                    pe.wait_ge(q_ready, m + 1)
                    bank = S.ps[5 + h % 2]
                    for c in range(NT):
                        if c:
                            pe.wait_ge(stated, 3 * h + c)
                        cols = bank[:, c * P:(c + 1) * P]
                        last = pe.matmul(cols, vs[:, h, c * P:(c + 1) * P], st[h % 2][:, c, :], start=True, stop=c == 0)
                        if c:
                            last = pe.matmul(cols, state[:, c - 1, :], ql[m % 2][:, c * P:(c + 1) * P], start=False,
                                             stop=True)
                    last.then_inc(out, 1)

            @block.scalar
            def _(act):
                for h in range(H):
                    act.wait_ge(k_turned, h + 1)
                    wait(act, update, h)
                    act.activation(k_tok, S.ps[4][:, :], ACT.Copy).then_inc(k_kept, 1)
                    act.wait_ge(out, h + 1)
                    act.activation(qs[:, h, :], S.ps[5 + h % 2][:, :], ACT.Copy).then_inc(out_kept, 1)
        sq = S.scratch
        head_norm(S, "hg_out_norm", ND, P, lambda g: qs[:, g, :], P, sq,
                  lambda g: [(sq[:, g, :], S.ones[:, 0:1])],
                  S.vec[:, VEC["hg_norm_gain_2"]:VEC["hg_norm_gain_2"] + 1],
                  square=lambda act, n: n.square(act, sq[:, :, :], qs[:, :, :]))
        prod, hi_done, lo_done = S.sem("hg_gated"), S.sem("hg_gated_hi"), S.sem("hg_gated_lo")
        with nc.Block() as block:
            @block.gpsimd
            def _(pool):
                for t in range(ND):
                    pool.tensor_tensor(qs[:, t, :], qs[:, t, :], gs[:, t, :], ALU.mult).then_inc(prod, 1)

            @block.scalar
            def _(act):
                for t in range(ND):
                    act.wait_ge(prod, t + 1)
                    act.activation(S.ahi[:, t, :], qs[:, t, :], ACT.Copy).then_inc(hi_done, 1)

            @block.vector
            def _(dve):
                for t in range(ND):
                    dve.wait_ge(hi_done, t + 1)
                    dve.tensor_tensor(S.alo[:, t, :], qs[:, t, :], S.ahi[:, t, :].bitcast(F32),
                                      ALU.subtract).then_inc(lo_done, 1)
        add_to_x(S, "hg_out", W.first["hgo"], S.ahi, S.alo)


def store(S, out):
    nc = S.nc
    turned, copied, stored = S.sem("out_turned"), S.sem("out_copied"), S.sem("out_stored")
    with nc.Block() as block:
        tok = S.scratch[:, :, :].rearrange("p a t -> p (a t)").rearrange("p (i d) -> p i d", i=NT)

        @block.tensor
        def _(pe):
            for n in range(2 * NT):
                i, half = divmod(n, 2)
                wait(pe, copied, n - 3)
                for c in range(4):
                    last = pe.transpose(S.ps[n % 4][:, c * P:(c + 1) * P], S.x[:, half * 4 + c, i * P:(i + 1) * P], S.eye)
                last.then_inc(turned, 1)

        @block.scalar
        def _(act):
            for n in range(2 * NT):
                i, half = divmod(n, 2)
                act.wait_ge(turned, n + 1)
                act.activation(tok[:, i, half * T:(half + 1) * T], S.ps[n % 4][:, :], ACT.Copy).then_inc(copied, 1)

        @block.sync
        def _(sp):
            for i in range(NT):
                sp.wait_ge(copied, 2 * (i + 1))
                sp.dma_start(out[0, i * P:(i + 1) * P, :], tok[:, i, :]).then_inc(stored, 16)
            sp.wait_ge(stored, 16 * NT)


def build(nc, w, consts, out):
    with ExitStack() as ctx:
        S = State()
        S.nc = nc
        S.sb = lambda name, shape, dt: ctx.enter_context(nc.sbuf_tensor(name, shape, dt))
        S.sem = lambda name: ctx.enter_context(nc.semaphore(name))
        S.W = Weights(nc, S.sb, S.sem, w)
        S.ps = [ctx.enter_context(nc.psum_tensor(f"bank{i}", [P, T], F32)) for i in range(8)]
        S.x = S.sb("x_t", [P, ND, T], F32)
        S.ahi, S.alo = S.sb("a_hi", [P, ND, T], F32R), S.sb("a_lo", [P, ND, T], F32R)
        S.scratch = S.sb("scratch", [P, ND, T], F32)
        S.const = S.sb("const", [P, K_COLS], F32)
        S.vec = S.sb("vec", [P, P], F32)
        S.q_gain, S.mq_gain = S.sb("q_gain", [P, 1], F32), S.sb("mq_gain", [P, 1], F32)
        S.lb, S.lb1 = S.sb("lower_bound", [P, ND], F32), S.sb("one_less_bound", [P, ND], F32)
        S.cos, S.sin = S.sb("cos", [P, T], F32), S.sb("sin", [P, T], F32)
        S.kpe_sq = S.sb("kpe_sq", [P, T], F32)
        S.mix_r = [S.cos, S.sin, S.kpe_sq]
        S.eye, S.ones = S.const[:, K_EYE:K_EYE + P], S.const[:, K_ONE:K_ONE + P]
        shared = {}

        def share(name):
            if name not in shared:
                shared[name] = [S.sem(name), 0]
            return tuple(shared[name])

        def advance(name, n):
            shared[name][1] += n
        S.shared, S.advance = share, advance
        small = S.sb("small_columns", [P, 1100], F32)
        S.used_columns = 0

        def columns(n):
            S.used_columns += n
            assert S.used_columns <= 1100
            return small[:, S.used_columns - n:S.used_columns]
        S.columns = columns
        setup(S, w, consts)
        first_block(S, w)
        stick_breaking(S)
        mlp(S, 0)
        hgrn(S)
        mlp(S, 1)
        store(S, out)


_INS = ["x", "mem", "positions", "norm_g", "w_in", "b_gate", "q_norm_g", "w_uq", "kv_norm_g", "w_ukv", "q_head_g",
        "k_head_g", "conv_w", "conv_b", "mem_norm_g", "w_mkv", "mem_q_g", "mem_k_g", "w_br_attn", "w_br_conv",
        "w_br_mem", "w_out", "norm_gains_2", "sb_w_qkv_2", "sb_q_gain_2", "sb_k_gain_2", "sb_w_o_2", "hg_w_in_2",
        "hg_lb_logits_2", "hg_norm_gain_2", "hg_w_o_2", "mlp_w1_2", "mlp_w2_2"]


def kernel(**inputs):
    import numpy as _np
    import concourse.bacc as _bacc
    from concourse import mybir as _mybir
    from concourse.bass_utils import run_bass_kernel_spmd as _run

    nc = _bacc.Bacc("TRN2", target_bir_lowering=False, num_devices=1)
    arrays, w = {}, {}
    for name in _INS:
        a = _np.ascontiguousarray(inputs[name])
        arrays[f"in_{name}"] = a
        w[name] = nc.dram_tensor(f"in_{name}", a.shape, _mybir.dt.from_np(a.dtype), kind="ExternalInput").ap()
    c = shape_constants()
    arrays["in_consts"] = c
    consts = nc.dram_tensor("in_consts", c.shape, _mybir.dt.float32, kind="ExternalInput").ap()
    out = nc.dram_tensor("out_0", (1, T, D), _mybir.dt.float32, kind="ExternalOutput").ap()
    build(nc, w, consts, out)
    r = _run(nc, [arrays], core_ids=[0])
    return r.results[0]["out_0"]
```

```python
from contextlib import ExitStack
from math import lcm

import concourse.bass as bass
import numpy as np
from concourse import mybir

ALU = mybir.AluOpType
ACT = mybir.ActivationFunctionType
F32 = mybir.dt.float32
F32R = mybir.dt.float32r
I32 = mybir.dt.int32
AX = mybir.AxisListType

P = 128
T = 512
NT = T // P
D = 1024
ND = D // P
M = 256
NM = M // P
EPS = 1e-6
HEADS, NOPE, ROPE, QK, DV = 8, 64, 32, 96, 64
Q_RANK, KV_RANK = 384, 256
CONV = 512
MEM_HEADS = 4
SB_HEADS, SB_DIM = 16, 64
HG_HEADS = 8
D_FF = 4096

C_QLAT, C_KVLAT, C_KPE = 0, 384, 640
C_B, C_C, C_U = 672, 1184, 1696
C_QMEM, C_GATTN, C_GCONV, C_GMEM, C_R = 2208, 2720, 3232, 3744, 4256

K_EYE, K_ONE, K_CAUSAL = 0, 128, 256
K_HALVES = 384
K_INVF, K_SIGN, K_EPS = 386, 387, 388
K_LEVEL = 392
LEVELS = 7
K_DIAG = K_EYE
K_COLS = K_LEVEL + LEVELS * P

VEC_ROWS = [("norm_g", 8), ("b_gate", 24), ("q_norm_g", 3), ("kv_norm_g", 2), ("conv_w", 12),
            ("conv_b", 4), ("mem_norm_g", 8), ("mem_q_g", 1), ("mem_k_g", 1), ("norm_gains_2", 32),
            ("hg_lb_logits_2", 8), ("hg_norm_gain_2", 1),
            ("q_head_g", 1), ("k_head_g", 1), ("sb_q_gain_2", 1), ("sb_k_gain_2", 1)]
VEC = {}
_at = 0
for _name, _n in VEC_ROWS:
    VEC[_name] = _at
    _at += _n
VEC_N = _at


def shape_constants():
    c = np.zeros((P, K_COLS), np.float32)
    c[:, K_EYE:K_EYE + P] = np.eye(P)
    c[:, K_ONE:K_ONE + P] = 1.0
    q = np.arange(P)[:, None]
    s = np.arange(P)[None, :]
    c[:, K_CAUSAL:K_CAUSAL + P] = np.where(s < q, 0.0, -1e30)
    c[:64, K_HALVES] = 1.0
    c[64:, K_HALVES + 1] = 1.0
    freq = np.float32(10000.0) ** (-np.arange(0, ROPE, 2, dtype=np.float32) / np.float32(ROPE))
    c[NOPE:QK, K_INVF] = np.concatenate([freq, freq])
    c[NOPE:QK, K_SIGN] = np.concatenate([-np.ones(16), np.ones(16)])
    c[:, K_EPS] = EPS
    src, dst = np.arange(P)[:, None], np.arange(P)[None, :]
    for level in range(LEVELS):
        h = 1 << level
        same = src // (2 * h) == dst // (2 * h)
        c[:, K_LEVEL + level * P:K_LEVEL + (level + 1) * P] = same & (src // h % 2 == 0) & (dst // h % 2 == 1)
    return c


def wait(eng, sem, value):
    if isinstance(value, int) and value <= 0:
        return
    eng.wait_ge(sem, value)


def rounds(eng, n):
    yield 0
    if n > 1:
        with eng.Fori(1, n) as i:
            yield i


def at(i, size):
    return bass.ds(i * size, size) if not isinstance(i, int) else slice(i * size, (i + 1) * size)


RING = 4
UNIT = ND * P


class Weights:

    def __init__(self, nc, sb, sem, w):
        self.stage = [sb(f"weight_stage{i}", [P, UNIT], F32) for i in range(RING)]
        self.hi = [sb(f"weight_hi{i}", [P, UNIT], F32R) for i in range(RING)]
        self.lo = [sb(f"weight_lo{i}", [P, UNIT], F32R) for i in range(RING)]
        self.loaded = [sem(f"weight_loaded{i}") for i in range(RING)]
        self.hi_done = sem("weight_hi_done")
        self.split_done = sem("weight_split_done")
        self.used = sem("weight_used")
        self.runs, self.n = [], 0
        self.first = {}

        def cols(name, lead, base):
            def view(f):
                full = w[name][lead].rearrange("(k p) n -> p k n", p=P)
                return full[:, :, bass.ds(f * P + base, P) if not isinstance(f, int) else slice(base + f * P, base + f * P + P)]
            return view

        def add(name, count, period, load, size=lambda r: UNIT):
            self.first[name] = self.n
            self.runs.append((self.n, count, period, load, size))
            self.n += count

        win = [cols("w_in", 0, c) for c in (C_QLAT,)][0]
        add("latent", 5, 1, lambda f, r: win(f))
        add("kpe", 1, 1, lambda f, r: w["w_in"][0].rearrange("(k p) n -> p k n", p=P)[:, :, C_KPE - 64:C_KPE + ROPE],
            lambda r: ND * QK)
        add("uq", 3, 1, lambda f, r: w["w_uq"][0, f * P:(f + 1) * P, :].rearrange("p (k n) -> p k n", k=1),
            lambda r: HEADS * QK)
        add("ukv", 2, 1, lambda f, r: w["w_ukv"][0, f * P:(f + 1) * P, :].rearrange("p (k n) -> p k n", k=1))
        qmem = cols("w_in", 0, C_QMEM)
        add("qmem", 4, 1, lambda f, r: qmem(f))
        mkv = cols("w_mkv", 0, 0)
        add("mkv", 8, 1, lambda f, r: mkv(f))
        conv = [cols("w_in", 0, c) for c in (C_C, C_U, C_B, C_GCONV)]
        add("conv", 16, 4, lambda f, r: conv[r](f))
        gates = [cols("w_in", 0, c) for c in (C_GATTN, C_GMEM)]
        add("gates", 8, 8, lambda f, r: gates[r // 4](r % 4))
        mix = [cols("w_in", 0, C_R), cols("w_br_attn", 0, 0), cols("w_in", 0, C_R + D), cols("w_br_conv", 0, 0),
               cols("w_in", 0, C_R + 2 * D), cols("w_br_mem", 0, 0)]
        add("mix", 48, 6, lambda f, r: mix[r](f), lambda r: UNIT // 2 if r % 2 else UNIT)
        for name, source, count in (("out", "w_out", 8), ("qkv", "sb_w_qkv_2", 24), ("sbo", "sb_w_o_2", 8)):
            add(name, count, 1, lambda f, r, v=cols(source, 0, 0): v(f))
        self.mlp_runs(add, w, 0, cols)
        for name, source, count in (("hgin", "hg_w_in_2", 32), ("hgo", "hg_w_o_2", 8)):
            add(name, count, 1, lambda f, r, v=cols(source, 0, 0): v(f))
        self.mlp_runs(add, w, 1, cols)

    def mlp_runs(self, add, w, layer, cols):
        one = cols("mlp_w1_2", layer, 0)
        w2 = w["mlp_w2_2"][layer].rearrange("(g k p) n -> g p k n", k=4, p=P)

        def two(g, r):
            group = w2[g] if isinstance(g, int) else w2[bass.ds(g, 1)].rearrange("a p k n -> p (a k) n")
            return group[:, :, r * 256:(r + 1) * 256]

        def body(f, r):
            which, r = divmod(r, 4)
            if which % 2 == 0:
                return one(f * 8 + (4 if which == 0 else 8) + r)
            return two(f * 2 + (0 if which == 1 else 1), r)

        def tail(f, r):
            return one(28 + r) if r < 4 else two(6 if r < 8 else 7, r % 4)

        add(f"mlp{layer}head", 4, 1, lambda f, r: one(f))
        add(f"mlp{layer}", 48, 16, body)
        add(f"mlp{layer}tail", 12, 12, tail)

    def steps(self, eng, lo, hi, straight=()):
        for start, count, period, load, size in self.runs:
            a, b = max(lo, start), min(hi, start + count)
            if a >= b:
                continue
            body = lcm(RING, period)
            times = (b - a) // body if b - a >= 2 * body and start not in straight else 0

            def one(i, j):
                q, r = divmod(a - start + j, period)
                return (i * body + a + j, (a + j) % RING, i * (body // RING) + (a + j) // RING + 1,
                        lambda: load(i * (body // period) + q, r), size(r))
            if times:
                with eng.Fori(0, times) as i:
                    for j in range(body):
                        yield one(i, j)
            for j in range(times * body, b - a):
                yield one(0, j)

    def load(self, sp, lo, hi):
        for u, slot, fills, source, size in self.steps(sp, min(lo, self.n), min(hi, self.n),
                                                       (self.first["mix"],)):
            wait(sp, self.split_done, u - RING + 1)
            src = source()
            k = src.shape[1]
            sp.dma_start(self.stage[slot][:, 0:size].rearrange("p (k n) -> p k n", k=k),
                         src).then_inc(self.loaded[slot], 16)

    def high(self, act, c, i=0, per=0):
        if c >= self.n:
            return
        slot = c % RING
        act.wait_ge(self.loaded[slot], i * (16 * per // RING) + 16 * (c // RING + 1))
        wait(act, self.used, i * per + (c - RING + 1))
        act.activation(self.hi[slot][:, :], self.stage[slot][:, :], ACT.Copy).then_inc(self.hi_done, 1)

    def low(self, pool, lo, hi):
        for u, slot, fills, _, size in self.steps(pool, min(lo, self.n), min(hi, self.n)):
            pool.wait_ge(self.hi_done, u + 1)
            pool.tensor_tensor(self.lo[slot][:, :], self.stage[slot][:, :], self.hi[slot][:, :].bitcast(F32),
                               ALU.subtract).then_inc(self.split_done, 1)

    def tile(self, u, k, a=0, n=P, width=P):
        s = u % RING
        return self.hi[s][:, k * width + a:k * width + a + n], self.lo[s][:, k * width + a:k * width + a + n]


def products(pe, out, pairs, before=None):
    pairs = list(pairs)
    n = 0
    for k, ((whi, wlo), (ahi, alo)) in enumerate(pairs):
        if before is not None:
            before(k)
        for l, r in ((wlo, ahi), (whi, alo), (whi, ahi)):
            last = pe.matmul(out, l, r, start=n == 0, stop=n == 3 * len(pairs) - 1)
            n += 1
    return last


class Norm:

    def __init__(self, S, name, groups, width, tokens=NT, halves=False, squares=1, applied=None):
        self.S, self.groups, self.width, self.tokens, self.halves = S, groups, width, tokens, halves
        self.cols = groups * tokens * (2 if halves else 1)
        self.signals = {}
        counts = {"squared": squares, "summed": 1, "rooted": 1, "inverted": 1, "spread": groups,
                  "applied": groups if applied is None else applied}
        for event, n in counts.items():
            self.signals[event] = S.shared(f"norm_{event}")
            S.advance(f"norm_{event}", n)
        self.root = S.columns(self.cols)
        self.rstd = S.columns(self.cols)

    def sem(self, event):
        return self.signals[event][0]

    def wait(self, eng, event, n):
        if n > 0:
            sem, before = self.signals[event]
            eng.wait_ge(sem, before + n)

    def square(self, act, out, src):
        act.activation(out, src, ACT.Square).then_inc(self.sem("squared"), 1)

    def sums(self, pe, bank, parts, squares=1):
        self.wait(pe, "squared", squares)
        w = 2 if self.halves else 1
        for g in range(self.groups):
            for i in range(self.tokens):
                c = (g * self.tokens + i) * w
                todo = parts(g)
                for n, (sq, ones) in enumerate(todo):
                    last = pe.matmul(bank[:, c:c + w], sq[:, i * P:(i + 1) * P], ones,
                                     start=n == 0, stop=n == len(todo) - 1)
        last.then_inc(self.sem("summed"), 1)

    def roots(self, act, bank):
        self.wait(act, "summed", 1)
        act.activation(self.root, bank[:, 0:self.cols], ACT.Sqrt, bias=self.S.const[:, K_EPS:K_EPS + 1],
                       scale=1.0 / self.width).then_inc(self.sem("rooted"), 1)

    def invert(self, dve):
        self.wait(dve, "rooted", 1)
        dve.reciprocal(self.rstd, self.root).then_inc(self.sem("inverted"), 1)

    def spread_group(self, pe, bank, g, rows=P, free_at=0):
        if g == 0:
            self.wait(pe, "inverted", 1)
        self.wait(pe, "applied", free_at)
        for i in range(self.tokens):
            c = g * self.tokens + i
            cols = bank[:, i * P:(i + 1) * P]
            if self.halves:
                for half in range(2):
                    lhs = self.rstd[:, 2 * c + half:2 * c + half + 1].to_broadcast([P, 64])
                    last = pe.matmul(cols[half * 64:(half + 1) * 64, :], lhs, self.S.eye, start=True, stop=True)
            else:
                lhs = self.rstd[:, c:c + 1].to_broadcast([P, rows])
                last = pe.matmul(cols[0:rows, :], lhs, self.S.eye, start=True, stop=True)
        last.then_inc(self.sem("spread"), 1)


class State:
    pass


class ModelNorm(Norm):

    def __init__(self, S, src, gain, hi, lo, tokens=NT, width=D, sum_bank=7, spread_bank=7, work=0):
        self.tiles = width // P
        super().__init__(S, "model", 1, width, tokens, squares=self.tiles, applied=self.tiles)
        self.src, self.gain, self.hi, self.lo, self.tk = src, gain, hi, lo, tokens * P
        self.scratch = S.scratch[:, work:, :]
        self.sum_bank, self.spread_bank = S.ps[sum_bank], S.ps[spread_bank]
        self.hi_done, self.hi0 = S.shared("split_hi")
        self.lo_done, self.lo0 = S.shared("split_lo")
        S.advance("split_hi", self.tiles)
        S.advance("split_lo", self.tiles)

    def square_tile(self, act, t):
        self.square(act, self.scratch[:, t, 0:self.tk], self.src[:, t, 0:self.tk])

    def sum_tile(self, pe, t):
        self.wait(pe, "squared", t + 1)
        for i in range(self.tokens):
            last = pe.matmul(self.sum_bank[:, i:i + 1], self.scratch[:, t, i * P:(i + 1) * P], self.S.ones[:, 0:1],
                             start=t == 0 and i == 0, stop=t == self.tiles - 1, skip_group_check=True)
        if t == self.tiles - 1:
            last.then_inc(self.sem("summed"), 1)

    def act_root(self, act):
        self.roots(act, self.sum_bank)

    def act_high(self, act):
        for t in range(self.tiles):
            self.wait(act, "applied", t + 1)
            act.activation(self.hi[:, t, 0:self.tk], self.scratch[:, t, 0:self.tk],
                           ACT.Copy).then_inc(self.hi_done, 1)

    def pe_spread(self, pe):
        self.spread_group(pe, self.spread_bank, 0)

    def dve_apply(self, dve):
        self.invert(dve)
        self.wait(dve, "spread", 1)

        def low(t):
            dve.wait_ge(self.hi_done, self.hi0 + t + 1)
            dve.tensor_tensor(self.lo[:, t, 0:self.tk], self.scratch[:, t, 0:self.tk],
                              self.hi[:, t, 0:self.tk].bitcast(F32), ALU.subtract).then_inc(self.lo_done, 1)
        for t in range(self.tiles):
            dve.scalar_tensor_tensor(out=self.scratch[:, t, 0:self.tk], in0=self.src[:, t, 0:self.tk],
                                     scalar=self.S.vec[:, self.gain + t:self.gain + t + 1],
                                     in1=self.spread_bank[:, 0:self.tk], op0=ALU.mult,
                                     op1=ALU.mult).then_inc(self.sem("applied"), 1)
            if t >= 2:
                low(t - 2)
        low(self.tiles - 2)
        low(self.tiles - 1)

    def ready(self, pe):
        return lambda k: pe.wait_ge(self.lo_done, self.lo0 + k + 1)


def setup(S, w, consts, norm):
    nc, W = S.nc, S.W
    loaded, vec_loaded, zeroed = S.sem("setup_loaded"), S.sem("vec_loaded"), S.sem("rows_zeroed")
    turned, copied = S.sem("x_turned"), S.sem("x_copied")
    vec_turned, vec_copied = S.sem("vec_turned"), S.sem("vec_copied")
    pos_f, spread, angle = S.sem("pos_float"), S.sem("pos_spread"), S.sem("angle_steps")
    x_loaded = S.sem("x_loaded")
    with ExitStack() as scope:
        def sb(name, shape, dt):
            return scope.enter_context(nc.sbuf_tensor(name, shape, dt))
        x_tok = sb("x_tok", [P, NT, D], F32)
        rows = sb("vec_rows", [P, P], F32)
        pos_i = sb("pos_i", [1, T], I32)
        pos = sb("pos", [1, T], F32)
        ang = sb("ang", [P, 5, T], F32)
        whole = sb("whole", [P, T], I32)
        block = scope.enter_context(nc.Block())

        @block.sync
        def _(sp):
            sp.dma_start(x_tok[:, :, :], w["x"][0].rearrange("(i p) d -> p i d", p=P)).then_inc(x_loaded, 16)
            sp.dma_start(S.const[:, :], consts).then_inc(loaded, 16)
            sp.dma_start(pos_i[:, :], w["positions"]).then_inc(loaded, 16)
            sp.wait_ge(zeroed, 1)
            n = 0
            for name, k in VEC_ROWS:
                r, src = VEC[name], w[name]
                if name == "conv_w":
                    views = [(rows[r:r + k, :], src[0].rearrange("t (c p) -> (t c) p", p=P))]
                elif name == "norm_gains_2":
                    views = [(rows[r:r + k, :], src.rearrange("l s (c p) -> (l s c) p", p=P))]
                elif name in ("sb_q_gain_2", "sb_k_gain_2"):
                    views = [(rows[r:r + 1, 0:64], src), (rows[r:r + 1, 64:128], src)]
                elif name in ("q_head_g", "k_head_g"):
                    views = [(rows[r:r + 1, 0:QK], src)]
                else:
                    views = [(rows[r:r + k, :], src[0].rearrange("(c p) -> c p", p=P))]
                for dst, view in views:
                    sp.dma_start(dst, view).then_inc(vec_loaded, 16)
                    n += 1
            S.n_vec = n
            W.load(sp, 0, 2 * RING)

        @block.gpsimd
        def _(pool):
            pool.memset(rows[:, :], 0.0).then_inc(zeroed, 1)
            W.low(pool, 0, RING)

        @block.tensor
        def _(pe):
            pe.wait_ge(loaded, 32)
            pe.wait_ge(x_loaded, 16)
            for c in range(ND):
                if c >= 4:
                    pe.wait_ge(copied, c - 3)
                for i in range(NT):
                    last = pe.transpose(S.ps[c % 4][:, i * P:(i + 1) * P], x_tok[:, i, c * P:(c + 1) * P], S.eye)
                last.then_inc(turned, 1)
                if c >= 2:
                    norm.sum_tile(pe, c - 2)
            norm.sum_tile(pe, ND - 2)
            norm.sum_tile(pe, ND - 1)
            pe.wait_ge(vec_loaded, 16 * S.n_vec)
            pe.transpose(S.ps[4][:, 0:P], rows[:, :], S.eye).then_inc(vec_turned, 1)
            pe.wait_ge(pos_f, 1)
            pe.matmul(S.ps[5][0:QK, :], S.ones[0:1, 0:QK], pos[:, :], start=True, stop=True).then_inc(spread, 1)

        @block.scalar
        def _(act):
            for c in range(ND):
                act.wait_ge(turned, c + 1)
                act.activation(S.x[:, c, :], S.ps[c % 4][:, :], ACT.Copy).then_inc(copied, 1)
                act.wait_ge(copied, c + 1)
                norm.square_tile(act, c)
            for u in range(RING):
                W.high(act, u)
            act.wait_ge(angle, 15)
            act.activation(S.cos[NOPE:QK, :], ang[NOPE:QK, 4, :], ACT.Sin).then_inc(angle, 1)
            act.activation(ang[NOPE:QK, 1, :], ang[NOPE:QK, 3, :], ACT.Sin).then_inc(angle, 1)

        @block.vector
        def _(dve):
            dve.wait_ge(loaded, 32)
            dve.tensor_copy(pos[:, :], pos_i[:, :]).then_inc(pos_f, 1)
            dve.wait_ge(vec_turned, 1)
            dve.tensor_copy(S.vec[:, :], S.ps[4][:, 0:P]).then_inc(vec_copied, 1)
            dve.wait_ge(vec_copied, 1)
            dve.tensor_scalar(S.q_gain[:, :], S.vec[:, VEC["q_head_g"]:VEC["q_head_g"] + 1], QK ** -0.5, None,
                              ALU.mult).then_inc(vec_copied, 1)
            dve.tensor_scalar(S.mq_gain[:, :], S.vec[:, VEC["mem_q_g"]:VEC["mem_q_g"] + 1], P ** -0.5, None,
                              ALU.mult).then_inc(vec_copied, 1)
            lg = S.vec[:, VEC["hg_lb_logits_2"]:VEC["hg_lb_logits_2"] + 8]
            dve.tensor_tensor(S.lb[:, :], lg, lg, ALU.subtract).then_inc(vec_copied, 1)
            r = slice(NOPE, QK)
            steps = 0

            def step(ins):
                nonlocal steps
                ins.then_inc(angle, 1)
                steps += 1
                dve.wait_ge(angle, steps)
            dve.wait_ge(spread, 1)
            step(dve.tensor_scalar(ang[r, 0, :], S.ps[5][r, :], S.const[r, K_INVF:K_INVF + 1], None, ALU.mult))
            for quarter, dst in ((0.25, 4), (0.0, 3)):
                step(dve.tensor_scalar(ang[r, 1, :], ang[r, 0, :], 1.0 / (2 * np.pi), quarter, ALU.mult, ALU.add))
                step(dve.tensor_copy(whole[r, :], ang[r, 1, :]))
                step(dve.tensor_copy(ang[r, 2, :], whole[r, :]))
                for k, part in enumerate(TWO_PI):
                    step(dve.scalar_tensor_tensor(out=ang[r, dst, :], in0=ang[r, 2, :], scalar=-part,
                                                  in1=ang[r, 0 if k == 0 else dst, :], op0=ALU.mult, op1=ALU.add))
                if quarter:
                    step(dve.tensor_scalar(ang[r, dst, :], ang[r, dst, :], float(np.pi / 2), None, ALU.add))
            assert steps == 14
            dve.tensor_scalar(ang[r, 3:5, :], ang[r, 3:5, :], PI_DOWN, -PI_DOWN, ALU.min, ALU.max).then_inc(angle, 1)
            dve.wait_ge(angle, 17)
            dve.tensor_scalar(S.sin[r, :], ang[r, 1, :], S.const[r, K_SIGN:K_SIGN + 1], None,
                              ALU.mult).then_inc(vec_copied, 1)


PI_DOWN = 3.1415925
_A = 6.28125
_B = float(np.float32(np.floor((2 * np.pi - _A) * 2 ** 21) / 2 ** 21))
TWO_PI = (_A, _B, 2 * np.pi - _A - _B)
SWAP = [(i + 16) % 32 for i in range(32)]


def project(S, dests, u0, act_side, norm=None, after=()):
    nc, W = S.nc, S.W
    out_done, before = S.shared("projected")
    ahi, alo, tokens = act_side
    n_units = len(dests)
    with nc.Block() as block:
        @block.sync
        def _(sp):
            W.load(sp, u0 + 2 * RING, u0 + n_units + 2 * RING)

        @block.gpsimd
        def _(pool):
            W.low(pool, u0 + RING, u0 + n_units + RING)

        @block.tensor
        def _(pe):
            if norm is not None:
                norm.pe_spread(pe)
            for n, (dst, rows, _) in enumerate(dests):
                u = u0 + n
                pe.wait_ge(W.split_done, u + 1)
                if n >= 4:
                    pe.wait_ge(out_done, before + n - 3)
                products(pe, S.ps[n % 4][0:rows, 0:tokens],
                         ((W.tile(u, k, 0, rows, rows), (ahi[:, k, 0:tokens], alo[:, k, 0:tokens]))
                          for k in range(ND)), norm.ready(pe) if norm is not None and n == 0 else None
                         ).then_inc(W.used, 1)
                for later, t, unit in after:
                    if unit == n - 1:
                        later.sum_tile(pe, t)
            for later, t, unit in after:
                if unit == n_units - 1:
                    later.sum_tile(pe, t)

        @block.scalar
        def _(act):
            if norm is not None:
                norm.act_root(act)
                norm.act_high(act)
            for n, (dst, rows, func) in enumerate(dests):
                act.wait_ge(W.used, u0 + n + 1)
                act.activation(dst, S.ps[n % 4][0:rows, 0:tokens], func).then_inc(out_done, 1)
                W.high(act, u0 + n + RING)
                for later, t, unit in after:
                    if unit == n:
                        act.wait_ge(out_done, before + n + 1)
                        later.square_tile(act, t)

        if norm is not None:
            @block.vector
            def _(dve):
                norm.dve_apply(dve)
    S.advance("projected", n_units)


def project_loop(S, u0, groups, ahi, alo, norm):
    nc, W = S.nc, S.W
    out_done, before = S.shared("projected")
    total = sum(n for _, _, n in groups)
    with nc.Block() as block:
        @block.sync
        def _(sp):
            W.load(sp, u0 + 2 * RING, u0 + total + 2 * RING)

        @block.gpsimd
        def _(pool):
            W.low(pool, u0 + RING, u0 + total + RING)

        @block.tensor
        def _(pe):
            norm.pe_spread(pe)
            for i in rounds(pe, total // 4):
                for j in range(4):
                    pe.wait_ge(W.split_done, i * 4 + (u0 + j + 1))
                    if not isinstance(i, int):
                        pe.wait_ge(out_done, i * 4 + (before + j - 3))
                    first = isinstance(i, int) and j == 0
                    products(pe, S.ps[j][:, :], ((W.tile(u0 + j, k), (ahi[:, k, :], alo[:, k, :]))
                                                 for k in range(ND)), norm.ready(pe) if first else None
                             ).then_inc(W.used, 1)

        @block.scalar
        def _(act):
            norm.act_root(act)
            norm.act_high(act)
            base = 0
            for dst, func, n in groups:
                with act.Fori(0, n // 4) as i:
                    for j in range(4):
                        act.wait_ge(W.used, i * 4 + (u0 + base + j + 1))
                        act.activation(dst[:, bass.ds(i * 4 + j, 1), :].rearrange("p a t -> p (a t)"),
                                       S.ps[j][:, :], func).then_inc(out_done, 1)
                        W.high(act, u0 + base + j + RING, i, 4)
                base += n

        @block.vector
        def _(dve):
            norm.dve_apply(dve)
    S.advance("projected", total)


def add_to_x(S, u0, ahi, alo, make_norm, split=None):
    nc, W = S.nc, S.W
    added, before = S.shared("x_added")
    (hi_done, hi0), (lo_done, lo0) = S.shared("split_hi"), S.shared("split_lo")
    if split is not None:
        S.advance("split_hi", ND)
        S.advance("split_lo", ND)
    later = make_norm()
    with nc.Block() as block:
        @block.sync
        def _(sp):
            W.load(sp, u0 + 2 * RING, u0 + ND + 2 * RING)

        @block.gpsimd
        def _(pool):
            W.low(pool, u0 + RING, u0 + ND + RING)

        @block.tensor
        def _(pe):
            for n in range(ND):
                pe.wait_ge(W.split_done, u0 + n + 1)
                if n >= 4:
                    pe.wait_ge(added, before + n - 3)
                ready = (lambda k: pe.wait_ge(lo_done, lo0 + k + 1)) if split is not None and n == 0 else None
                products(pe, S.ps[n % 4][:, :], ((W.tile(u0 + n, k), (ahi[:, k, :], alo[:, k, :]))
                                                 for k in range(ND)), ready).then_inc(W.used, 1)
                if n >= 1:
                    later.sum_tile(pe, n - 1)
            later.sum_tile(pe, ND - 1)

        @block.scalar
        def _(act):
            if split is not None:
                for t in range(ND):
                    act.activation(ahi[:, t, :], split[:, t, :], ACT.Copy).then_inc(hi_done, 1)
                act.wait_ge(lo_done, lo0 + ND)
            for n in range(ND):
                act.wait_ge(W.used, u0 + n + 1)
                W.high(act, u0 + n + RING)
                act.wait_ge(added, before + n + 1)
                later.square_tile(act, n)

        @block.vector
        def _(dve):
            if split is not None:
                for t in range(ND):
                    dve.wait_ge(hi_done, hi0 + t + 1)
                    dve.tensor_tensor(alo[:, t, :], split[:, t, :], ahi[:, t, :].bitcast(F32),
                                      ALU.subtract).then_inc(lo_done, 1)
            for n in range(ND):
                dve.wait_ge(W.used, u0 + n + 1)
                dve.tensor_tensor(S.x[:, n, :], S.x[:, n, :], S.ps[n % 4][:, :], ALU.add).then_inc(added, 1)
    S.advance("x_added", ND)
    return later


def softmax_attention(S, name, heads, q, k, v, key_tiles, dv, out, pt, prob):
    nc = S.nc
    keys = key_tiles * P
    per = P // dv
    scored, maxed, exped = S.sem(f"{name}_scored"), S.sem(f"{name}_maxed"), S.sem(f"{name}_exped")
    inverted, scaled = S.sem(f"{name}_inverted"), S.sem(f"{name}_scaled")
    turned, kept = S.sem(f"{name}_turned"), S.sem(f"{name}_kept")
    summed, out_done = S.sem(f"{name}_summed"), S.sem(f"{name}_out_done")
    items = [(h, i) for h in range(heads) for i in range(NT)]
    nmax = S.columns(len(items))
    total = S.columns(len(items))
    inv = S.columns(len(items))
    score_banks, turn_banks, out_banks = S.ps[0:3], S.ps[3:5], S.ps[5:7]
    with nc.Block() as block:
        @block.tensor
        def _(pe):
            def score(n):
                h, i = items[n]
                wait(pe, exped, n - 2)
                pe.matmul(score_banks[n % 3][:, 0:keys], q(h)[:, i * P:(i + 1) * P], k(h), start=True,
                          stop=True).then_inc(scored, 1)

            def turn(n):
                wait(pe, kept, n - 1)
                pe.wait_ge(scaled, n + 1)
                for b in range(key_tiles):
                    last = pe.transpose(turn_banks[n % 2][:, b * P:(b + 1) * P],
                                        prob[n % 3][:, b * P:(b + 1) * P], S.eye)
                last.then_inc(turned, 1)

            def weigh(h):
                o = h // per
                wait(pe, out_done, o - 1)
                pe.wait_ge(kept, NT * (h + 1))
                r = h % per * dv
                for b in range(key_tiles):
                    last = pe.matmul(out_banks[o % 2][r:r + dv, :], v(h, b), pt[h % 2][:, b, :],
                                     start=b == 0, stop=b == key_tiles - 1)
                last.then_inc(summed, 1)

            for n in range(len(items) + 2):
                if n == 0:
                    score(0)
                    score(1)
                if n + 2 < len(items):
                    score(n + 2)
                if n < len(items):
                    turn(n)
                if n >= 5 and (n - 5) % NT == 0:
                    weigh((n - 5) // NT)

        @block.vector
        def _(dve):
            def normalise(n):
                dve.wait_ge(exped, n + 1)
                dve.reciprocal(inv[:, n:n + 1], total[:, n:n + 1]).then_inc(inverted, 1)
                dve.wait_ge(inverted, n + 1)
                dve.tensor_scalar(prob[n % 3][:, 0:keys], prob[n % 3][:, 0:keys], inv[:, n:n + 1], None,
                                  ALU.mult).then_inc(scaled, 1)
            for n in range(len(items)):
                dve.wait_ge(scored, n + 1)
                dve.tensor_reduce(nmax[:, n:n + 1], score_banks[n % 3][:, 0:keys], AX.X, ALU.max,
                                  negate=True).then_inc(maxed, 1)
                if n >= 1:
                    normalise(n - 1)
            normalise(len(items) - 1)

        @block.scalar
        def _(act):
            def keep(n):
                h, i = items[n]
                act.wait_ge(turned, n + 1)
                wait(act, summed, h - 1)
                act.activation(pt[h % 2][:, 0:key_tiles, i * P:(i + 1) * P],
                               turn_banks[n % 2][:, 0:keys].rearrange("p (b t) -> p b t", b=key_tiles),
                               ACT.Copy).then_inc(kept, 1)

            def put(o):
                act.wait_ge(summed, per * (o + 1))
                act.activation(out[:, o, :], out_banks[o % 2][:, :], ACT.Copy).then_inc(out_done, 1)
            for n in range(len(items)):
                act.wait_ge(maxed, n + 1)
                wait(act, turned, n - 2)
                act.activation(prob[n % 3][:, 0:keys], score_banks[n % 3][:, 0:keys], ACT.Exp,
                               bias=nmax[:, n:n + 1], accum_out=total[:, n:n + 1]).then_inc(exped, 1)
                if n >= 2:
                    keep(n - 2)
                if n >= 8 and (n - 8) % (NT * per) == NT * per - 1:
                    put((n - 8) // (NT * per))
            keep(len(items) - 2)
            keep(len(items) - 1)
            done = len([n for n in range(8, len(items)) if (n - 8) % (NT * per) == NT * per - 1])
            for o in range(done, heads // per):
                put(o)


def head_norm(S, name, groups, width, src, rows, sq, parts, gain, tokens=NT, halves=False, extra=None,
              square=None, squares=1):
    nc = S.nc
    n = Norm(S, name, groups, width, tokens, halves, squares)
    tk = tokens * P
    with nc.Block() as block:
        @block.scalar
        def _(act):
            square(act, n)
            n.roots(act, S.ps[0])

        @block.tensor
        def _(pe):
            n.sums(pe, S.ps[0], parts, squares)
            for g in range(groups):
                n.spread_group(pe, S.ps[1 + g % 3], g, rows, free_at=g - 2)

        @block.vector
        def _(dve):
            n.invert(dve)
            for g in range(groups):
                n.wait(dve, "spread", g + 1)
                bank = S.ps[1 + g % 3]
                if extra is not None:
                    extra(dve, g, bank, n)
                s = src(g)
                r = s.shape[0]
                dve.scalar_tensor_tensor(out=s, in0=s, scalar=gain[0:r, :], in1=bank[0:r, 0:tk],
                                         op0=ALU.mult, op1=ALU.mult).then_inc(n.sem("applied"), 1)


def first_block(S, w, norm, norm2):
    nc, W = S.nc, S.W
    f = W.first
    outer = ExitStack()
    with outer:
        def sbo(name, shape, dt=F32):
            return outer.enter_context(nc.sbuf_tensor(name, shape, dt))
        o_attn = sbo("o_attn", [P, 4, T])
        with ExitStack() as mla:
            def sb(name, shape, dt=F32):
                return mla.enter_context(nc.sbuf_tensor(name, shape, dt))
            qh = sb("q_heads", [QK, HEADS, T])
            kv = sb("kv_heads", [P, HEADS, T])
            v_tok = sb("v_tok", [P, NT, HEADS, DV])
            kpe = sb("k_rope", [QK, 3, T])
            lat = kv
            with ExitStack() as lat_scope:
                lhi = lat_scope.enter_context(nc.sbuf_tensor("latent_hi", [P, 5, T], F32R))
                llo = lat_scope.enter_context(nc.sbuf_tensor("latent_lo", [P, 5, T], F32R))
                q_norm = ModelNorm(S, lat, VEC["q_norm_g"], lhi, llo, width=Q_RANK, sum_bank=6, spread_bank=6)
                kv_norm = ModelNorm(S, lat[:, 3:5, :], VEC["kv_norm_g"], lhi[:, 3:5, :], llo[:, 3:5, :],
                                    width=KV_RANK, sum_bank=5, spread_bank=5, work=3)
                project(S, [(lat[:, n, :], P, ACT.Copy) for n in range(5)] + [(kpe[:, 0, :], QK, ACT.Copy)],
                        f["latent"], (S.ahi, S.alo, T), norm,
                        [(q_norm, t, t) for t in range(3)] + [(kv_norm, t, 3 + t) for t in range(2)])
                up_project(S, qh, kv, lhi, llo, q_norm, kv_norm)
            turn_values_and_rope(S, qh, kv, v_tok, kpe)
            p_scope = ExitStack()
            with p_scope:
                prob = [p_scope.enter_context(nc.sbuf_tensor(f"attn_prob{i}", [P, T], F32)) for i in range(3)]
                pt = [S.scratch[:, 0:4, :], S.scratch[:, 4:8, :]]
                softmax_attention(S, "mla", HEADS, lambda h: qh[:, h, :], lambda h: kv[0:QK, h, :],
                                  lambda h, b: v_tok[:, b, h, :], NT, DV, o_attn, pt, prob)
        o_mem = sbo("o_mem", [P, 4, T])
        memory_branch(S, w, o_mem)
        return mix_branches(S, w, o_attn, o_mem, norm2)


def up_project(S, qh, kv, lhi, llo, q_norm, kv_norm):
    nc, W = S.nc, S.W
    out_done, head_done = S.sem("up_out_done"), S.sem("up_head_done")
    uq, ukv = W.first["uq"], W.first["ukv"]
    n_units = 5
    with nc.Block() as block:
        @block.sync
        def _(sp):
            W.load(sp, uq + 2 * RING, uq + n_units + 2 * RING)

        @block.gpsimd
        def _(pool):
            W.low(pool, uq + RING, uq + n_units + RING)

        @block.tensor
        def _(pe):
            q_norm.pe_spread(pe)
            kv_norm.pe_spread(pe)
            pe.wait_ge(W.split_done, uq + 3)
            for h in range(HEADS):
                wait(pe, out_done, h - 3)
                last = products(pe, S.ps[h % 4][0:QK, :], ((W.tile(uq + k, 0, h * QK, QK), (lhi[:, k, :], llo[:, k, :]))
                                                          for k in range(3)), q_norm.ready(pe) if h == 0 else None)
                last.then_inc(head_done, 1)
            pe.wait_ge(head_done, HEADS)
            pe.sem_inc(W.used, 3)
            pe.wait_ge(W.split_done, ukv + 2)
            for h in range(HEADS):
                wait(pe, out_done, HEADS + h - 3)
                products(pe, S.ps[h % 4][:, :], ((W.tile(ukv + k, 0, h * P, P), (lhi[:, 3 + k, :], llo[:, 3 + k, :]))
                                                 for k in range(2)),
                         kv_norm.ready(pe) if h == 0 else None).then_inc(head_done, 1)
            pe.wait_ge(head_done, 2 * HEADS)
            pe.sem_inc(W.used, 2)

        @block.scalar
        def _(act):
            q_norm.act_root(act)
            kv_norm.act_root(act)
            q_norm.act_high(act)
            kv_norm.act_high(act)
            for n in range(2 * HEADS):
                act.wait_ge(head_done, n + 1)
                h = n % HEADS
                dst, rows = (qh[:, h, :], QK) if n < HEADS else (kv[:, h, :], P)
                act.activation(dst, S.ps[n % 4][0:rows, :], ACT.Copy).then_inc(out_done, 1)
                if n == HEADS - 1:
                    for k in range(3):
                        W.high(act, uq + RING + k)
            for k in range(3, n_units):
                W.high(act, uq + RING + k)

        @block.vector
        def _(dve):
            q_norm.dve_apply(dve)
            kv_norm.dve_apply(dve)


def turn_values_and_rope(S, qh, kv, v_tok, kpe):
    nc = S.nc
    turned, kept = S.sem("v_turned"), S.sem("v_kept")
    with nc.Block() as block:
        @block.tensor
        def _(pe):
            for h in range(HEADS):
                wait(pe, kept, h - 3)
                for i in range(NT):
                    last = pe.transpose(S.ps[h % 4][:, i * P:(i + 1) * P], kv[:, h, i * P:(i + 1) * P], S.eye)
                last.then_inc(turned, 1)

        @block.scalar
        def _(act):
            for h in range(HEADS):
                act.wait_ge(turned, h + 1)
                act.activation(v_tok[:, :, h, :], S.ps[h % 4][:, :].rearrange("p (i c) -> p i c", i=NT)[:, :, NOPE:P],
                               ACT.Copy).then_inc(kept, 1)

    sq = S.scratch

    def square_q(act, n):
        n.square(act, sq[0:QK, :, :], qh[:, :, :])
    head_norm(S, "q_head", HEADS, QK, lambda g: qh[:, g, :], QK, sq,
              lambda g: [(sq[0:QK, g, :], S.ones[0:QK, 0:1])], S.q_gain[:, 0:1], square=square_q)

    kg = S.vec[:, VEC["k_head_g"]:VEC["k_head_g"] + 1]
    r = slice(NOPE, QK)
    rope = S.sem("k_rope_steps")

    def square_k(act, n):
        n.square(act, sq[0:NOPE, :, :], kv[0:NOPE, :, :])
        act.wait_ge(rope, 1)
        act.activation(S.kpe_sq[r, :], kpe[r, 0, :], ACT.Square).then_inc(n.sem("squared"), 1)

    def rotate(dve, g, bank, n):
        if g == 0:
            n.wait(dve, "squared", 2)
            done = 1

            def step(ins):
                nonlocal done
                ins.then_inc(rope, 1)
                done += 1
                dve.wait_ge(rope, done)
            step(dve.tensor_scalar(kpe[r, 0, :], kpe[r, 0, :], kg[r, :], None, ALU.mult))
            step(dve.stream_shuffle(kpe[r, 1, :], kpe[r, 0, :], SWAP))
            step(dve.tensor_tensor(kpe[r, 0, :], kpe[r, 0, :], S.cos[r, :], ALU.mult))
            step(dve.tensor_tensor(kpe[r, 1, :], kpe[r, 1, :], S.sin[r, :], ALU.mult))
            step(dve.tensor_tensor(kpe[r, 2, :], kpe[r, 0, :], kpe[r, 1, :], ALU.add))
        dve.tensor_tensor(kv[r, g, :], kpe[r, 2, :], bank[r, :], ALU.mult).then_inc(rope, 1)

    q_rope = S.sem("q_rope_steps")
    with nc.Block() as block:
        @block.vector
        def _(dve):
            done = 0

            def step(ins):
                nonlocal done
                ins.then_inc(q_rope, 1)
                done += 1
                dve.wait_ge(q_rope, done)
            part = qh[r, :, :]
            swapped = S.scratch[r, :, :]
            step(dve.stream_shuffle(swapped.rearrange("p h t -> p (h t)"), part.rearrange("p h t -> p (h t)"), SWAP))
            cos = S.cos[r, :].unsqueeze(1).to_broadcast([ROPE, HEADS, T])
            sin = S.sin[r, :].unsqueeze(1).to_broadcast([ROPE, HEADS, T])
            step(dve.tensor_tensor(swapped, swapped, sin, ALU.mult))
            step(dve.tensor_tensor(part, part, cos, ALU.mult))
            step(dve.tensor_tensor(part, part, swapped, ALU.add))
            dve.sem_inc(rope, 1)

    head_norm(S, "k_head", HEADS, QK, lambda g: kv[0:NOPE, g, :], QK, sq,
              lambda g: [(sq[0:NOPE, g, :], S.ones[0:NOPE, 0:1]), (S.kpe_sq[r, :], S.ones[r, 0:1])],
              kg, extra=rotate, square=square_k, squares=2)


def memory_branch(S, w, o_mem):
    nc, W = S.nc, S.W
    with ExitStack() as scope:
        def sb(name, shape, dt=F32):
            return scope.enter_context(nc.sbuf_tensor(name, shape, dt))
        qm = sb("mem_q", [P, MEM_HEADS, T])
        memT = sb("mem_t", [P, ND, M])
        mkv = sb("mem_kv", [P, 2 * MEM_HEADS, M])
        mv = sb("mem_v", [P, NM, MEM_HEADS, P])
        mhi, mlo = sb("mem_hi", [P, ND, M], F32R), sb("mem_lo", [P, ND, M], F32R)
        prob = [sb(f"mem_prob{i}", [P, M]) for i in range(3)]
        mem_loaded, turned, copied = S.sem("memory_loaded"), S.sem("memory_turned"), S.sem("memory_copied")
        tok = S.scratch[:, 0:4, :].rearrange("p a t -> p (a t)").rearrange("p (i d) -> p i d", i=NM)
        with nc.Block() as block:
            @block.sync
            def _(sp):
                sp.dma_start(tok, w["mem"][0].rearrange("(i p) d -> p i d", p=P)).then_inc(mem_loaded, 16)

            @block.tensor
            def _(pe):
                pe.wait_ge(mem_loaded, 16)
                for c in range(ND):
                    wait(pe, copied, c - 3)
                    for i in range(NM):
                        last = pe.transpose(S.ps[c % 4][:, i * P:(i + 1) * P], tok[:, i, c * P:(c + 1) * P], S.eye)
                    last.then_inc(turned, 1)

            @block.scalar
            def _(act):
                for c in range(ND):
                    act.wait_ge(turned, c + 1)
                    act.activation(memT[:, c, :], S.ps[c % 4][:, 0:M], ACT.Copy).then_inc(copied, 1)
        mem_norm = ModelNorm(S, memT, VEC["mem_norm_g"], mhi, mlo, tokens=NM)
        project(S, [(qm[:, n, :], P, ACT.Copy) for n in range(MEM_HEADS)], W.first["qmem"],
                (S.ahi, S.alo, T), None, [(mem_norm, t, t // 2) for t in range(ND)])
        project(S, [(mkv[:, n, :], P, ACT.Copy) for n in range(2 * MEM_HEADS)], W.first["mkv"],
                (mhi, mlo, M), mem_norm)
        v_turned, v_kept = S.sem("mem_v_turned"), S.sem("mem_v_kept")
        with nc.Block() as block:
            @block.tensor
            def _(pe):
                for h in range(MEM_HEADS):
                    for i in range(NM):
                        last = pe.transpose(S.ps[h][:, i * P:(i + 1) * P], mkv[:, 2 * h + 1, i * P:(i + 1) * P], S.eye)
                    last.then_inc(v_turned, 1)

            @block.scalar
            def _(act):
                for h in range(MEM_HEADS):
                    act.wait_ge(v_turned, h + 1)
                    act.activation(mv[:, :, h, :], S.ps[h][:, 0:M].rearrange("p (i c) -> p i c", i=NM),
                                   ACT.Copy).then_inc(v_kept, 1)
        sq = S.scratch
        head_norm(S, "mem_q_norm", MEM_HEADS, P, lambda g: qm[:, g, :], P, sq,
                  lambda g: [(sq[:, g, :], S.ones[:, 0:1])], S.mq_gain[:, 0:1],
                  square=lambda act, n: n.square(act, sq[:, 0:4, :], qm[:, :, :]))
        head_norm(S, "mem_k_norm", MEM_HEADS, P, lambda g: mkv[:, 2 * g, :], P, sq,
                  lambda g: [(sq[:, g, 0:M], S.ones[:, 0:1])], S.vec[:, VEC["mem_k_g"]:VEC["mem_k_g"] + 1],
                  tokens=NM, square=lambda act, n: n.square(act, sq[:, 0:4, 0:M], mkv[:, 0:8:2, :]))
        softmax_attention(S, "mem", MEM_HEADS, lambda h: qm[:, h, :], lambda h: mkv[:, 2 * h, :],
                          lambda h, b: mv[:, b, h, :], NM, P, o_mem,
                          [S.scratch[:, 0:4, :], S.scratch[:, 4:8, :]], prob)


def mix_branches(S, w, o_attn, o_mem, norm2):
    nc, W = S.nc, S.W
    with ExitStack() as scope:
        def sb(name, shape, dt=F32):
            return scope.enter_context(nc.sbuf_tensor(name, shape, dt))
        ohi, olo = sb("o_hi", [P, 12, T], F32R), sb("o_lo", [P, 12, T], F32R)
        with ExitStack() as conv_scope:
            def sbc(name, shape, dt=F32):
                return conv_scope.enter_context(nc.sbuf_tensor(name, shape, dt))
            cc, z = sbc("conv_c", [P, T]), sbc("conv_z", [P, T + 2])
            gate, acc = sbc("conv_gate", [P, T]), sbc("conv_acc", [P, T])
            c_kept, gated, hi_done = S.sem("conv_c_kept"), S.sem("conv_gate_done"), S.sem("conv_hi_done")
            steps, tile_done, padded = S.sem("conv_steps"), S.sem("conv_tile_done"), S.sem("conv_padded")
            u0 = W.first["conv"]
            with nc.Block() as block:
                @block.sync
                def _(sp):
                    W.load(sp, u0 + 2 * RING, u0 + 16 + 2 * RING)

                @block.gpsimd
                def _(pool):
                    W.low(pool, u0 + RING, u0 + 16 + RING)

                @block.tensor
                def _(pe):
                    for t in range(4):
                        wait(pe, tile_done, t - 1)
                        for j in range(4):
                            u = u0 + 4 * t + j
                            pe.wait_ge(W.split_done, u + 1)
                            products(pe, S.ps[t % 2 * 4 + j][:, :], ((W.tile(u, k), (S.ahi[:, k, :], S.alo[:, k, :]))
                                                                     for k in range(ND))).then_inc(W.used, 1)

                @block.scalar
                def _(act):
                    for t in range(4):
                        b = S.ps[t % 2 * 4:t % 2 * 4 + 4]
                        act.wait_ge(W.used, u0 + 4 * t + 1)
                        wait(act, steps, 6 * (t - 1) + 1)
                        act.activation(cc[:, :], b[0][:, :], ACT.Copy).then_inc(c_kept, 1)
                        for j in range(3):
                            W.high(act, u0 + 4 * t + RING + j)
                        act.wait_ge(W.used, u0 + 4 * t + 4)
                        wait(act, tile_done, t)
                        act.activation(gate[:, :], b[3][:, :], ACT.Silu).then_inc(gated, 1)
                        act.wait_ge(steps, 6 * t + 6)
                        act.activation(ohi[:, 4 + t, :], acc[:, :], ACT.Copy).then_inc(hi_done, 1)
                        W.high(act, u0 + 4 * t + RING + 3)

                @block.vector
                def _(dve):
                    dve.memset(z[:, 0:1], 0.0).then_inc(padded, 1)
                    dve.memset(z[:, T + 1:T + 2], 0.0).then_inc(padded, 1)
                    dve.wait_ge(padded, 2)
                    n = 0

                    def step(ins):
                        nonlocal n
                        ins.then_inc(steps, 1)
                        n += 1
                        dve.wait_ge(steps, n)
                    for t in range(4):
                        b = S.ps[t % 2 * 4:t % 2 * 4 + 4]

                        def tap(k):
                            c = VEC["conv_w"] + 4 * k + t
                            return S.vec[:, c:c + 1]
                        c = VEC["conv_b"] + t
                        dve.wait_ge(c_kept, t + 1)
                        dve.wait_ge(W.used, u0 + 4 * t + 3)
                        step(dve.tensor_tensor(z[:, 1:T + 1], cc[:, :], b[1][:, :], ALU.mult))
                        step(dve.tensor_scalar(acc[:, :], z[:, 0:T], tap(0), S.vec[:, c:c + 1], ALU.mult, ALU.add))
                        for k in (1, 2):
                            step(dve.scalar_tensor_tensor(out=acc[:, :], in0=z[:, k:T + k], scalar=tap(k),
                                                          in1=acc[:, :], op0=ALU.mult, op1=ALU.add))
                        step(dve.tensor_tensor(acc[:, :], acc[:, :], b[2][:, :], ALU.mult))
                        dve.wait_ge(gated, t + 1)
                        step(dve.tensor_tensor(acc[:, :], acc[:, :], gate[:, :], ALU.mult))
                        dve.wait_ge(hi_done, t + 1)
                        dve.tensor_tensor(olo[:, 4 + t, :], acc[:, :], ohi[:, 4 + t, :].bitcast(F32),
                                          ALU.subtract).then_inc(tile_done, 1)
                        dve.wait_ge(tile_done, t + 1)
        u0 = W.first["gates"]
        silu = [sb(f"branch_gate{i}", [P, T]) for i in range(2)]
        silu_done, prod, hi2, lo2 = S.sem("gate_silu"), S.sem("gate_product"), S.sem("gate_hi"), S.sem("gate_lo")
        with nc.Block() as block:
            @block.sync
            def _(sp):
                W.load(sp, u0 + 2 * RING, u0 + 8 + 2 * RING)

            @block.gpsimd
            def _(pool):
                W.low(pool, u0 + RING, u0 + 8 + RING)

            @block.tensor
            def _(pe):
                for n in range(8):
                    pe.wait_ge(W.split_done, u0 + n + 1)
                    wait(pe, silu_done, n - 3)
                    products(pe, S.ps[n % 4][:, :], ((W.tile(u0 + n, k), (S.ahi[:, k, :], S.alo[:, k, :]))
                                                     for k in range(ND))).then_inc(W.used, 1)

            @block.scalar
            def _(act):
                for n in range(9):
                    if n < 8:
                        act.wait_ge(W.used, u0 + n + 1)
                        wait(act, prod, n - 1)
                        act.activation(silu[n % 2][:, :], S.ps[n % 4][:, :], ACT.Silu).then_inc(silu_done, 1)
                        W.high(act, u0 + n + RING)
                    if n >= 1:
                        o = o_attn if n <= 4 else o_mem
                        t = (n - 1) % 4
                        act.wait_ge(prod, n)
                        act.activation(ohi[:, (0 if n <= 4 else 8) + t, :], o[:, t, :], ACT.Copy).then_inc(hi2, 1)

            @block.vector
            def _(dve):
                for n in range(9):
                    if n < 8:
                        o, t = (o_attn if n < 4 else o_mem), n % 4
                        dve.wait_ge(silu_done, n + 1)
                        dve.tensor_tensor(o[:, t, :], o[:, t, :], silu[n % 2][:, :], ALU.mult).then_inc(prod, 1)
                    if n >= 1:
                        o, t = (o_attn if n <= 4 else o_mem), (n - 1) % 4
                        dve.wait_ge(hi2, n)
                        dve.wait_ge(prod, n)
                        c = (0 if n <= 4 else 8) + t
                        dve.tensor_tensor(olo[:, c, :], o[:, t, :], ohi[:, c, :].bitcast(F32),
                                          ALU.subtract).then_inc(lo2, 1)
        u0 = W.first["mix"]
        rt = [sb(f"mix_r{i}", [P, T]) for i in range(2)]
        tmp = sb("mix_term", [P, T])
        r_done, gated, summed = S.sem("mix_r_done"), S.sem("mix_gated"), S.sem("mix_summed")
        with nc.Block() as block:
            @block.sync
            def _(sp):
                W.load(sp, u0 + 2 * RING, u0 + 48 + 2 * RING)

            @block.gpsimd
            def _(pool):
                W.low(pool, u0 + RING, u0 + 48 + RING)

            @block.tensor
            def _(pe):
                for i in rounds(pe, 4):
                    for j in range(12):
                        m, kind = divmod(j, 6)
                        branch = kind // 2
                        pe.wait_ge(W.split_done, i * 12 + (u0 + j + 1))
                        if kind % 2 == 0:
                            wait(pe, r_done, i * 6 + (3 * m + branch - 2))
                            pairs = ((W.tile(u0 + j, k), (S.ahi[:, k, :], S.alo[:, k, :])) for k in range(ND))
                        else:
                            wait(pe, gated, i * 6 + (3 * m + branch - 2))
                            pairs = ((W.tile(u0 + j, k), (ohi[:, 4 * branch + k, :], olo[:, 4 * branch + k, :]))
                                     for k in range(4))
                        products(pe, S.ps[kind][:, :], pairs).then_inc(W.used, 1)

            @block.scalar
            def _(act):
                for i in rounds(act, 4):
                    for j in range(6):
                        m, b = divmod(j, 3)
                        act.wait_ge(W.used, i * 12 + (u0 + 2 * j + 1))
                        wait(act, gated, i * 6 + (j - 2))
                        c = VEC["b_gate"] + 8 * b + m
                        bias = S.vec[:, c:c + 1] if isinstance(i, int) else S.vec[:, bass.ds(i * 2 + c, 1)]
                        act.activation(S.mix_r[b][:, :], S.ps[2 * b][:, :], ACT.Sigmoid, bias=bias).then_inc(r_done, 1)
                        W.high(act, u0 + 2 * j + RING, i, 12)
                        W.high(act, u0 + 2 * j + 1 + RING, i, 12)

            @block.vector
            def _(dve):
                for i in rounds(dve, 8):
                    y = S.scratch[:, i, :] if isinstance(i, int) else \
                        S.scratch[:, bass.ds(i, 1), :].rearrange("p a t -> p (a t)")
                    for b in range(3):
                        dve.wait_ge(W.used, i * 6 + (u0 + 2 * b + 2))
                        dve.wait_ge(r_done, i * 3 + (b + 1))
                        wait(dve, summed, i * 2 + (b - 1))
                        dst = y if b == 0 else tmp[:, :]
                        dve.tensor_tensor(dst, S.mix_r[b][:, :], S.ps[2 * b + 1][:, :], ALU.mult).then_inc(gated, 1)
                        if b:
                            dve.wait_ge(gated, i * 3 + (b + 1))
                            dve.tensor_tensor(y, y, tmp[:, :], ALU.add).then_inc(summed, 1)
    return add_to_x(S, W.first["out"], S.ahi, S.alo, norm2, split=S.scratch)


def stick_breaking(S, norm, later):
    nc, W = S.nc, S.W
    with ExitStack() as scope:
        def sb(name, shape, dt=F32):
            return scope.enter_context(nc.sbuf_tensor(name, shape, dt))
        qkv = sb("sb_qkv", [P, 24, T])
        v_tok = sb("sb_v_tok", [P, NT, D])
        stay = [sb(f"sb_stay{i}", [P, T]) for i in range(2)]
        beta = [sb(f"sb_beta{i}", [P, T]) for i in range(2)]
        left = [sb(f"sb_left{i}", [P, T + 1]) for i in range(2)]
        zeros = sb("sb_zeros", [P, T])
        project_loop(S, W.first["qkv"], [(qkv, ACT.Copy, 24)], S.ahi, S.alo, norm)
        turned, kept, zeroed = S.sem("sb_v_turned"), S.sem("sb_v_kept"), S.sem("sb_zeroed")
        with nc.Block() as block:
            @block.gpsimd
            def _(pool):
                pool.memset(zeros[:, :], 0.0).then_inc(zeroed, 1)
                for l in left:
                    pool.memset(l[:, T:T + 1], 1.0).then_inc(zeroed, 1)

            @block.tensor
            def _(pe):
                for c in range(ND):
                    wait(pe, kept, c - 3)
                    for i in range(NT):
                        last = pe.transpose(S.ps[c % 4][:, i * P:(i + 1) * P], qkv[:, 16 + c, i * P:(i + 1) * P], S.eye)
                    last.then_inc(turned, 1)

            @block.scalar
            def _(act):
                for c in range(ND):
                    act.wait_ge(turned, c + 1)
                    act.activation(v_tok[:, :, c * P:(c + 1) * P], S.ps[c % 4][:, :].rearrange("p (i c) -> p i c", i=NT),
                                   ACT.Copy).then_inc(kept, 1)
        sq = S.scratch
        for name, first in (("sb_q", 0), ("sb_k", 8)):
            g = VEC[f"{name}_gain_2"]
            head_norm(S, f"{name}_norm", 8, SB_DIM, lambda t: qkv[:, first + t, :], P, sq,
                      lambda t: [(sq[:, t, :], S.const[:, K_HALVES:K_HALVES + 2])], S.vec[:, g:g + 1], halves=True,
                      square=lambda act, n: n.square(act, sq[:, :, :], qkv[:, first:first + 8, :]))
        items = [(h, i) for h in range(SB_HEADS) for i in range(NT)]
        pt = [S.scratch[:, 0:4, :], S.scratch[:, 4:8, :]]
        names = ("scored", "masked", "sigmoids", "scanned", "weighted", "turned2", "kept2", "summed", "out_hi", "out_lo")
        scored, masked, sig, scanned, weighted, turned2, kept2, summed, out_hi, out_lo = (S.sem(f"sb_{x}") for x in names)
        score_banks, turn_banks, out_banks = S.ps[0:3], S.ps[3:5], S.ps[5:7]
        scale = SB_DIM ** -0.5
        N = len(items)
        with nc.Block() as block:
            @block.tensor
            def _(pe):
                def score(n):
                    h, i = items[n]
                    r = slice(h % 2 * 64, h % 2 * 64 + 64)
                    wait(pe, sig, n - 2)
                    pe.matmul(score_banks[n % 3][:, 0:(i + 1) * P], qkv[r, h // 2, i * P:(i + 1) * P],
                              qkv[r, 8 + h // 2, 0:(i + 1) * P], start=True, stop=True).then_inc(scored, 1)

                def turn(n):
                    h, i = items[n]
                    wait(pe, kept2, n - 1)
                    pe.wait_ge(weighted, n + 1)
                    a = T - (i + 1) * P
                    for b in range(i + 1):
                        last = pe.transpose(turn_banks[n % 2][:, b * P:(b + 1) * P],
                                            beta[n % 2][:, a + b * P:a + (b + 1) * P], S.eye)
                    last.then_inc(turned2, 1)

                def weigh(h):
                    o = h // 2
                    wait(pe, out_lo, o - 1)
                    pe.wait_ge(kept2, NT * (h + 1))
                    r = h % 2 * 64
                    for b in range(NT):
                        last = pe.matmul(out_banks[o % 2][r:r + 64, b * P:T], v_tok[:, b, h * 64:(h + 1) * 64],
                                         pt[h % 2][:, b, b * P:T], start=b == 0, stop=b == NT - 1)
                    last.then_inc(summed, 1)
                score(0)
                score(1)
                for n in range(N):
                    if n + 2 < N:
                        score(n + 2)
                    turn(n)
                    if n >= 5 and (n - 5) % NT == 0:
                        weigh((n - 5) // NT)
                weigh(SB_HEADS - 1)

            @block.vector
            def _(dve):
                def mask(n):
                    h, i = items[n]
                    dve.wait_ge(scored, n + 1)
                    diag = score_banks[n % 3][:, i * P:(i + 1) * P]
                    dve.tensor_tensor(diag, diag, S.const[:, K_CAUSAL:K_CAUSAL + P], ALU.add).then_inc(masked, 1)

                def weigh(n):
                    h, i = items[n]
                    a = T - (i + 1) * P
                    dve.wait_ge(sig, n + 1)
                    wait(dve, weighted, n - 1)
                    rev = slice(None, None, -1)
                    dve.tensor_tensor_scan(left[n % 2][:, a:T][:, rev], stay[n % 2][:, a:T][:, rev], zeros[:, a:T],
                                           1.0, ALU.mult, ALU.add).then_inc(scanned, 1)
                    dve.wait_ge(scanned, n + 1)
                    dve.tensor_tensor(beta[n % 2][:, a:T], beta[n % 2][:, a:T], left[n % 2][:, a + 1:T + 1],
                                      ALU.mult).then_inc(weighted, 1)

                def lower(o):
                    dve.wait_ge(out_hi, o + 1)
                    dve.tensor_tensor(S.alo[:, o, :], out_banks[o % 2][:, :], S.ahi[:, o, :].bitcast(F32),
                                      ALU.subtract).then_inc(out_lo, 1)
                mask(0)
                for n in range(N):
                    if n + 1 < N:
                        mask(n + 1)
                    weigh(n)
                    if n >= 8 and (n - 8) % 8 == 7:
                        lower((n - 8) // 8)
                lower(SB_HEADS // 2 - 1)

            @block.scalar
            def _(act):
                def keep(n):
                    h, i = items[n]
                    act.wait_ge(turned2, n + 1)
                    wait(act, summed, h - 1)
                    act.activation(pt[h % 2][:, 0:i + 1, i * P:(i + 1) * P],
                                   turn_banks[n % 2][:, 0:(i + 1) * P].rearrange("p (b t) -> p b t", b=i + 1),
                                   ACT.Copy).then_inc(kept2, 1)

                def put(o):
                    act.wait_ge(summed, 2 * (o + 1))
                    act.activation(S.ahi[:, o, :], out_banks[o % 2][:, :], ACT.Copy).then_inc(out_hi, 1)
                for n in range(N):
                    h, i = items[n]
                    a = T - (i + 1) * P
                    src = score_banks[n % 3][:, 0:(i + 1) * P]
                    act.wait_ge(masked, n + 1)
                    wait(act, turned2, n - 1)
                    act.activation(stay[n % 2][:, a:T], src, ACT.Sigmoid, scale=-scale)
                    act.activation(beta[n % 2][:, a:T], src, ACT.Sigmoid, scale=scale).then_inc(sig, 1)
                    if n >= 1:
                        keep(n - 1)
                    if n >= 7 and (n - 7) % 8 == 7:
                        put((n - 7) // 8)
                keep(N - 1)
                put(SB_HEADS // 2 - 1)
        return add_to_x(S, W.first["sbo"], S.ahi, S.alo, later)


def mlp(S, layer, norm, make_norm):
    nc, W = S.nc, S.W
    later = make_norm() if make_norm else None
    with ExitStack() as scope:
        def sb(name, shape, dt=F32):
            return scope.enter_context(nc.sbuf_tensor(f"{name}{layer}", shape, dt))
        hhi = [sb(f"hidden_hi{i}_", [P, 4, T], F32R) for i in range(2)]
        hlo = [sb(f"hidden_lo{i}_", [P, 4, T], F32R) for i in range(2)]
        relu = [sb(f"hidden_relu{i}_", [P, T]) for i in range(4)]
        squ = [sb(f"hidden_square{i}_", [P, T]) for i in range(4)]
        names = ("relu_done", "hi_done", "square_done", "lo_done", "added")
        relu_done, hi_done, square_done, lo_done, added = (S.shared(f"mlp_{x}")[0] for x in names)
        tiles0, sums0 = 32 * layer, 64 * layer
        u0 = W.first[f"mlp{layer}head"]
        GROUPS = 8

        def order(eng, up, down):
            up(0, 0, u0, 0)
            for i in eng_rounds(eng, 3):
                b = u0 + 4
                up(i, 1, b, 1)
                down(i, 0, b + 4, 0)
                up(i, 2, b + 8, 0)
                down(i, 1, b + 12, 1)
            b = u0 + 52
            up(0, 7, b, 1)
            down(0, 6, b + 4, 0)
            down(0, 7, b + 8, 1)

        eng_rounds = rounds

        with nc.Block() as block:
            @block.sync
            def _(sp):
                W.load(sp, u0 + 2 * RING, u0 + 64 + 2 * RING)

            @block.gpsimd
            def _(pool):
                W.low(pool, u0 + RING, u0 + 64 + RING)

            @block.tensor
            def _(pe):
                def up(i, c, b, half):
                    for r in range(4):
                        pe.wait_ge(W.split_done, i * 16 + (b + r + 1))
                        wait(pe, relu_done, i * 8 + (tiles0 + 4 * c + r - 3))
                        first = isinstance(i, int) and c == 0 and r == 0
                        products(pe, S.ps[r][:, :], ((W.tile(b + r, k), (S.ahi[:, k, :], S.alo[:, k, :]))
                                                     for k in range(ND)), norm.ready(pe) if first else None
                                 ).then_inc(W.used, 1)

                def down(i, c, b, half):
                    wait(pe, lo_done, i * 8 + (tiles0 + 4 * c + 4))
                    for r in range(4):
                        pe.wait_ge(W.split_done, i * 16 + (b + r + 1))
                        wait(pe, added, i * 16 + (sums0 + 8 * c + 2 * r - 2))
                        for m in range(2):
                            last = products(pe, S.ps[4 + r % 2 * 2 + m][:, :],
                                            ((W.tile(b + r, k, m * P, P, 256), (hhi[half][:, k, :], hlo[half][:, k, :]))
                                             for k in range(4)))
                        last.then_inc(W.used, 1)
                        if later is not None and c == 7 and r >= 1:
                            later.sum_tile(pe, 2 * r - 2)
                            later.sum_tile(pe, 2 * r - 1)
                norm.pe_spread(pe)
                order(pe, up, down)
                if later is not None:
                    later.sum_tile(pe, ND - 2)
                    later.sum_tile(pe, ND - 1)

            @block.scalar
            def _(act):
                def up(i, c, b, half):
                    for r in range(4):
                        act.wait_ge(W.used, i * 16 + (b + r + 1))
                        wait(act, lo_done, i * 8 + (tiles0 + 4 * c + r - 3))
                        act.activation(relu[r][:, :], S.ps[r][:, :], ACT.Relu).then_inc(relu_done, 1)
                        act.wait_ge(relu_done, i * 8 + (tiles0 + 4 * c + r + 1))
                        act.activation(hhi[half][:, r, :], relu[r][:, :], ACT.Square).then_inc(hi_done, 1)
                        W.high(act, b + r + RING, i, 16)

                def down(i, c, b, half):
                    for r in range(4):
                        act.wait_ge(W.used, i * 16 + (b + r + 1))
                        W.high(act, b + r + RING, i, 16)
                        if later is not None and c == 7:
                            for t in (2 * r, 2 * r + 1):
                                act.wait_ge(added, sums0 + 8 * c + t + 1)
                                later.square_tile(act, t)
                norm.act_root(act)
                norm.act_high(act)
                order(act, up, down)

            @block.vector
            def _(dve):
                def up(i, c, b, half):
                    for r in range(4):
                        dve.wait_ge(relu_done, i * 8 + (tiles0 + 4 * c + r + 1))
                        wait(dve, lo_done, i * 8 + (tiles0 + 4 * c + r - 3))
                        dve.tensor_tensor(squ[r][:, :], relu[r][:, :], relu[r][:, :], ALU.mult).then_inc(square_done, 1)
                        dve.wait_ge(hi_done, i * 8 + (tiles0 + 4 * c + r + 1))
                        dve.wait_ge(square_done, i * 8 + (tiles0 + 4 * c + r + 1))
                        dve.tensor_tensor(hlo[half][:, r, :], squ[r][:, :], hhi[half][:, r, :].bitcast(F32),
                                          ALU.subtract).then_inc(lo_done, 1)

                def down(i, c, b, half):
                    for r in range(4):
                        dve.wait_ge(W.used, i * 16 + (b + r + 1))
                        for m in range(2):
                            t = 2 * r + m
                            wait(dve, added, i * 16 + (sums0 + 8 * c + t - 7))
                            dve.tensor_tensor(S.x[:, t, :], S.x[:, t, :], S.ps[4 + r % 2 * 2 + m][:, :],
                                              ALU.add).then_inc(added, 1)
                norm.dve_apply(dve)
                order(dve, up, down)
    return later


def hgrn(S, norm, later):
    nc, W = S.nc, S.W
    with ExitStack() as scope:
        def sb(name, shape, dt=F32):
            return scope.enter_context(nc.sbuf_tensor(name, shape, dt))
        qs, fs, vs, gs = (sb(f"hg_{x}", [P, ND, T]) for x in ("q", "f", "v", "g"))
        extra = sb("hg_factors", [P, 5, T])
        st = [sb(f"hg_scores{i}", [P, NT, P]) for i in range(2)]
        project_loop(S, W.first["hgin"], [(qs, ACT.Silu, 8), (fs, ACT.Sigmoid, 8), (vs, ACT.Copy, 8),
                                          (gs, ACT.Sigmoid, 8)], S.ahi, S.alo, norm)
        turned, kept, forget = S.sem("hg_v_turned"), S.sem("hg_v_kept"), S.sem("hg_forget")
        with nc.Block() as block:
            @block.vector
            def _(dve):
                dve.tensor_scalar(S.lb1[:, :], S.lb[:, :], -1.0, 1.0, ALU.mult, ALU.add).then_inc(forget, 1)
                dve.wait_ge(forget, 1)
                for h in range(HG_HEADS):
                    dve.tensor_scalar(fs[:, h, :], fs[:, h, :], S.lb1[:, h:h + 1], S.lb[:, h:h + 1], ALU.mult,
                                      ALU.add).then_inc(forget, 1)

            @block.tensor
            def _(pe):
                for h in range(HG_HEADS):
                    wait(pe, kept, h - 3)
                    for c in range(NT):
                        last = pe.transpose(S.ps[h % 4][:, c * P:(c + 1) * P], vs[:, h, c * P:(c + 1) * P], S.eye)
                    last.then_inc(turned, 1)

            @block.scalar
            def _(act):
                for h in range(HG_HEADS):
                    act.wait_ge(turned, h + 1)
                    act.activation(vs[:, h, :], S.ps[h % 4][:, :], ACT.Copy).then_inc(kept, 1)
        t = [S.scratch[:, n, :] for n in range(ND)] + [extra[:, n, :] for n in range(5)]
        pre, suf, ql, kl = t[0:2], t[2:4], (t[4:6], t[6:8]), (t[8:10], t[10:12])
        state = t[12][:, 0:3 * P].rearrange("p (c v) -> p c v", c=3)
        names = ("zeroed", "key", "suffix", "prefix", "q_ready", "k_ready", "scored", "picked", "k_turned", "k_kept",
                 "update", "totals", "stated", "out", "out_kept", "first")
        (zeroed, key, suffix, prefix, q_ready, k_ready, scored, picked, k_turned, k_kept, update, totalled, stated,
         out, out_kept, first) = (S.sem(f"hg_{x}") for x in names)
        totals = S.columns(HG_HEADS * NT)
        H = HG_HEADS
        LAST = LEVELS

        def done(h, n):
            return h // 2 * 16 + n * 2 + h % 2 + 1

        def halves(ap, level):
            v = ap.rearrange("p (b s h) -> p b s h", s=2, h=1 << level)
            return v[:, :, 0, :], v[:, :, 1, :]

        with nc.Block() as block:
            @block.gpsimd
            def _(pool):
                for b in (*kl[0], *kl[1]):
                    pool.memset(b, 0.0).then_inc(zeroed, 1)
                pool.wait_ge(zeroed, 4)
                for p in range(H // 2):
                    for n in range(LAST + 1):
                        for h in (2 * p, 2 * p + 1):
                            s = h % 2
                            pool.wait_ge(prefix, done(h, n))
                            if n >= 2:
                                pool.wait_ge(scored, done(h, n - 1))
                            elif p >= 1:
                                pool.wait_ge(out, h - 1)
                            q, k = ql[s][n % 2], kl[s][n % 2]
                            if n < LAST:
                                qr, pr = halves(qs[:, h, :], n)[1], halves(pre[s], n)[1]
                                kleft, ul = halves(fs[:, h, :], n)[0], halves(suf[s], n)[0]
                                q, k = halves(q, n)[1], halves(k, n)[0]
                            else:
                                qr, pr, kleft, ul = qs[:, h, :], pre[s], fs[:, h, :], suf[s]
                            pool.tensor_tensor(k, kleft, ul, ALU.mult).then_inc(k_ready, 1)
                            pool.tensor_tensor(q, qr, pr, ALU.mult).then_inc(q_ready, 1)

            @block.vector
            def _(dve):
                def start(h):
                    s = h % 2
                    if h >= 2:
                        dve.wait_ge(q_ready, done(h - 2, LAST))
                        dve.wait_ge(totalled, h - 1)
                    dve.memset(suf[s], 1.0).then_inc(suffix, 1)
                    dve.tensor_copy(pre[s], fs[:, h, :]).then_inc(first, 1)
                    dve.wait_ge(first, h + 1)
                    dve.tensor_scalar(fs[:, h, :], fs[:, h, :], -1.0, 1.0, ALU.mult, ALU.add).then_inc(key, 1)
                    dve.wait_ge(key, h + 1)
                    dve.wait_ge(suffix, done(h, 0))
                    dve.sem_inc(prefix, 1)

                def grow(h, level):
                    s, d = h % 2, 1 << level
                    dve.wait_ge(q_ready, done(h, level))
                    dve.wait_ge(prefix, done(h, level))
                    ul, _ = halves(suf[s], level)
                    pl, pr = halves(pre[s], level)
                    total = pr[:, :, d - 1:d].to_broadcast([P, T // (2 * d), d])
                    dve.tensor_tensor(ul, ul, total, ALU.mult).then_inc(suffix, 1)
                    dve.wait_ge(suffix, done(h, level + 1))
                    ltotal = pl[:, :, d - 1:d].to_broadcast([P, T // (2 * d), d])
                    dve.tensor_tensor(pr, pr, ltotal, ALU.mult).then_inc(prefix, 1)

                def total(h):
                    dve.wait_ge(prefix, done(h, LAST))
                    ends = pre[h % 2].rearrange("p (c t) -> p c t", c=NT)[:, :, P - 1]
                    dve.tensor_copy(totals[:, h * NT:(h + 1) * NT], ends).then_inc(totalled, 1)

                def pick(h, step):
                    dve.wait_ge(scored, done(h, step))
                    n = done(h, step) - 1
                    s = h % 2
                    if step == 0:
                        wait(dve, out, h - 1)
                        bank = S.ps[n % 3][:, :].rearrange("p (c t) -> p c t", c=NT)
                        m = S.const[:, K_EYE:K_EYE + P].unsqueeze(1).to_broadcast([P, NT, P])
                        dve.tensor_tensor(st[s][:, :, :], bank, m, ALU.mult).then_inc(picked, 1)
                    else:
                        level = step - 1
                        dve.wait_ge(picked, done(h, step - 1))
                        d, nb = 1 << level, 64 >> level
                        a = K_LEVEL + level * P
                        bank = S.ps[n % 3][:, 0:T // 2].rearrange("p (c b t) -> p c b t", c=NT, t=d)
                        m = S.const[:, a:a + P].bitcast(I32).rearrange("p (b s t) -> p b s t", s=2, t=d)[:, :, 1, :]
                        dst = st[s][:, :, :].rearrange("p c (b s t) -> p c b s t", s=2, t=d)[:, :, :, 1, :]
                        dve.copy_predicated(dst, m.unsqueeze(1).to_broadcast([P, NT, nb, d]),
                                            bank).then_inc(picked, 1)

                def states(h):
                    dve.wait_ge(update, h + 1)
                    wait(dve, out, h)
                    dve.wait_ge(totalled, h + 1)
                    dve.tensor_copy(state[:, 0, :], S.ps[3][:, 0:P]).then_inc(stated, 1)
                    for c in (1, 2):
                        dve.wait_ge(stated, 3 * h + c)
                        dve.scalar_tensor_tensor(out=state[:, c, :], in0=state[:, c - 1, :],
                                                 scalar=totals[:, h * NT + c:h * NT + c + 1],
                                                 in1=S.ps[3][:, c * P:(c + 1) * P], op0=ALU.mult,
                                                 op1=ALU.add).then_inc(stated, 1)
                start(0)
                start(1)
                for p in range(H // 2):
                    pair = (2 * p, 2 * p + 1)
                    for level in range(LEVELS):
                        for h in pair:
                            grow(h, level)
                        for h in pair:
                            pick(h, level)
                    for h in pair:
                        total(h)
                    for h in pair:
                        pick(h, LEVELS)
                    if p + 1 < H // 2:
                        start(2 * p + 2)
                        start(2 * p + 3)
                    for h in pair:
                        states(h)

            @block.tensor
            def _(pe):
                def score(h, step):
                    n, s = done(h, step) - 1, h % 2
                    wait(pe, picked, n - 2)
                    if step == 0:
                        pe.wait_ge(key, h + 1)
                        q, k = qs[:, h, :], fs[:, h, :]
                    else:
                        pe.wait_ge(k_ready, done(h, step - 1))
                        pe.wait_ge(q_ready, done(h, step - 1))
                        q, k = ql[s][(step - 1) % 2], kl[s][(step - 1) % 2]
                    for c in range(NT):
                        cols = slice(c * P, (c + 1) * P)
                        if step == 0:
                            to, src = S.ps[n % 3][:, cols], q[:, cols]
                        else:
                            d = 1 << (step - 1)
                            to = S.ps[n % 3][:, c * 64:(c + 1) * 64].rearrange("p (b t) -> p b t", t=d)
                            src = q[:, cols].rearrange("p (b s t) -> p b s t", s=2, t=d)[:, :, 1, :]
                        last = pe.matmul(to, k[:, cols], src, start=True, stop=True)
                    last.then_inc(scored, 1)

                for h in (0, 1):
                    score(h, 0)
                for p in range(H // 2):
                    pair = (2 * p, 2 * p + 1)
                    for step in range(1, LEVELS + 1):
                        for h in pair:
                            score(h, step)
                    for h in pair:
                        pe.wait_ge(k_ready, done(h, LAST))
                        for c in range(NT):
                            last = pe.transpose(S.ps[4 + h % 2][:, c * P:(c + 1) * P],
                                                kl[h % 2][LAST % 2][:, c * P:(c + 1) * P], S.eye)
                        last.then_inc(k_turned, 1)
                    if p + 1 < H // 2:
                        for h in (2 * p + 2, 2 * p + 3):
                            score(h, 0)
                    for h in pair:
                        pe.wait_ge(k_kept, h + 1)
                        wait(pe, stated, 3 * h)
                        for c in range(NT - 1):
                            last = pe.matmul(S.ps[3][:, c * P:(c + 1) * P], fs[:, h, c * P:(c + 1) * P],
                                             vs[:, h, c * P:(c + 1) * P], start=True, stop=True)
                        last.then_inc(update, 1)
                        wait(pe, out_kept, h - 1)
                        pe.wait_ge(picked, done(h, LEVELS))
                        pe.wait_ge(q_ready, done(h, LAST))
                        bank = S.ps[6 + h % 2]
                        for c in range(NT):
                            if c:
                                pe.wait_ge(stated, 3 * h + c)
                            cols = bank[:, c * P:(c + 1) * P]
                            last = pe.matmul(cols, vs[:, h, c * P:(c + 1) * P], st[h % 2][:, c, :], start=True,
                                             stop=c == 0)
                            if c:
                                last = pe.matmul(cols, state[:, c - 1, :], ql[h % 2][LAST % 2][:, c * P:(c + 1) * P],
                                                 start=False, stop=True)
                        last.then_inc(out, 1)

            @block.scalar
            def _(act):
                for p in range(H // 2):
                    for h in (2 * p, 2 * p + 1):
                        act.wait_ge(k_turned, h + 1)
                        act.activation(fs[:, h, :], S.ps[4 + h % 2][:, :], ACT.Copy).then_inc(k_kept, 1)
                    for h in (2 * p, 2 * p + 1):
                        act.wait_ge(out, h + 1)
                        act.activation(qs[:, h, :], S.ps[6 + h % 2][:, :], ACT.Copy).then_inc(out_kept, 1)
        sq = S.scratch
        head_norm(S, "hg_out_norm", ND, P, lambda g: qs[:, g, :], P, sq,
                  lambda g: [(sq[:, g, :], S.ones[:, 0:1])],
                  S.vec[:, VEC["hg_norm_gain_2"]:VEC["hg_norm_gain_2"] + 1],
                  square=lambda act, n: n.square(act, sq[:, :, :], qs[:, :, :]))
        prod, hi_done, lo_done = S.sem("hg_gated"), S.sem("hg_gated_hi"), S.sem("hg_gated_lo")
        with nc.Block() as block:
            @block.gpsimd
            def _(pool):
                for t in range(ND):
                    pool.tensor_tensor(qs[:, t, :], qs[:, t, :], gs[:, t, :], ALU.mult).then_inc(prod, 1)

            @block.scalar
            def _(act):
                for t in range(ND):
                    act.wait_ge(prod, t + 1)
                    act.activation(S.ahi[:, t, :], qs[:, t, :], ACT.Copy).then_inc(hi_done, 1)

            @block.vector
            def _(dve):
                for t in range(ND):
                    dve.wait_ge(hi_done, t + 1)
                    dve.tensor_tensor(S.alo[:, t, :], qs[:, t, :], S.ahi[:, t, :].bitcast(F32),
                                      ALU.subtract).then_inc(lo_done, 1)
        return add_to_x(S, W.first["hgo"], S.ahi, S.alo, later)


def store(S, out):
    nc = S.nc
    turned, copied, stored = S.sem("out_turned"), S.sem("out_copied"), S.sem("out_stored")
    with nc.Block() as block:
        tok = S.scratch[:, :, :].rearrange("p a t -> p (a t)").rearrange("p (i d) -> p i d", i=NT)

        @block.tensor
        def _(pe):
            for n in range(2 * NT):
                i, half = divmod(n, 2)
                wait(pe, copied, n - 3)
                for c in range(4):
                    last = pe.transpose(S.ps[n % 4][:, c * P:(c + 1) * P], S.x[:, half * 4 + c, i * P:(i + 1) * P], S.eye)
                last.then_inc(turned, 1)

        @block.scalar
        def _(act):
            for n in range(2 * NT):
                i, half = divmod(n, 2)
                act.wait_ge(turned, n + 1)
                act.activation(tok[:, i, half * T:(half + 1) * T], S.ps[n % 4][:, :], ACT.Copy).then_inc(copied, 1)

        @block.sync
        def _(sp):
            for i in range(NT):
                sp.wait_ge(copied, 2 * (i + 1))
                sp.dma_start(out[0, i * P:(i + 1) * P, :], tok[:, i, :]).then_inc(stored, 16)
            sp.wait_ge(stored, 16 * NT)


def build(nc, w, consts, out):
    with ExitStack() as ctx:
        S = State()
        S.nc = nc
        S.sb = lambda name, shape, dt: ctx.enter_context(nc.sbuf_tensor(name, shape, dt))
        S.sem = lambda name: ctx.enter_context(nc.semaphore(name))
        S.W = Weights(nc, S.sb, S.sem, w)
        S.ps = [ctx.enter_context(nc.psum_tensor(f"bank{i}", [P, T], F32)) for i in range(8)]
        S.x = S.sb("x_t", [P, ND, T], F32)
        S.ahi, S.alo = S.sb("a_hi", [P, ND, T], F32R), S.sb("a_lo", [P, ND, T], F32R)
        S.scratch = S.sb("scratch", [P, ND, T], F32)
        S.const = S.sb("const", [P, K_COLS], F32)
        S.vec = S.sb("vec", [P, P], F32)
        S.q_gain, S.mq_gain = S.sb("q_gain", [P, 1], F32), S.sb("mq_gain", [P, 1], F32)
        S.lb, S.lb1 = S.sb("lower_bound", [P, ND], F32), S.sb("one_less_bound", [P, ND], F32)
        S.cos, S.sin = S.sb("cos", [P, T], F32), S.sb("sin", [P, T], F32)
        S.kpe_sq = S.sb("kpe_sq", [P, T], F32)
        S.mix_r = [S.cos, S.sin, S.kpe_sq]
        S.eye, S.ones = S.const[:, K_EYE:K_EYE + P], S.const[:, K_ONE:K_ONE + P]
        shared = {}

        def share(name):
            if name not in shared:
                shared[name] = [S.sem(name), 0]
            return tuple(shared[name])

        def advance(name, n):
            shared[name][1] += n
        S.shared, S.advance = share, advance
        small = S.sb("small_columns", [P, 1100], F32)
        S.used_columns = 0

        def columns(n):
            S.used_columns += n
            assert S.used_columns <= 1100
            return small[:, S.used_columns - n:S.used_columns]
        S.columns = columns
        def x_norm(gain, sum_bank=7):
            return ModelNorm(S, S.x, gain, S.ahi, S.alo, sum_bank=sum_bank)
        g2 = VEC["norm_gains_2"]
        norm1 = x_norm(VEC["norm_g"])
        setup(S, w, consts, norm1)
        norm = first_block(S, w, norm1, lambda: x_norm(g2))
        norm = stick_breaking(S, norm, lambda: x_norm(g2 + 8))
        norm = mlp(S, 0, norm, lambda: x_norm(g2 + 16, sum_bank=0))
        norm = hgrn(S, norm, lambda: x_norm(g2 + 24))
        mlp(S, 1, norm, None)
        store(S, out)


_INS = ["x", "mem", "positions", "norm_g", "w_in", "b_gate", "q_norm_g", "w_uq", "kv_norm_g", "w_ukv", "q_head_g",
        "k_head_g", "conv_w", "conv_b", "mem_norm_g", "w_mkv", "mem_q_g", "mem_k_g", "w_br_attn", "w_br_conv",
        "w_br_mem", "w_out", "norm_gains_2", "sb_w_qkv_2", "sb_q_gain_2", "sb_k_gain_2", "sb_w_o_2", "hg_w_in_2",
        "hg_lb_logits_2", "hg_norm_gain_2", "hg_w_o_2", "mlp_w1_2", "mlp_w2_2"]


def kernel(**inputs):
    import numpy as _np
    import concourse.bacc as _bacc
    from concourse import mybir as _mybir
    from concourse.bass_utils import run_bass_kernel_spmd as _run

    nc = _bacc.Bacc("TRN2", target_bir_lowering=False, num_devices=1)
    arrays, w = {}, {}
    for name in _INS:
        a = _np.ascontiguousarray(inputs[name])
        arrays[f"in_{name}"] = a
        w[name] = nc.dram_tensor(f"in_{name}", a.shape, _mybir.dt.from_np(a.dtype), kind="ExternalInput").ap()
    c = shape_constants()
    arrays["in_consts"] = c
    consts = nc.dram_tensor("in_consts", c.shape, _mybir.dt.float32, kind="ExternalInput").ap()
    out = nc.dram_tensor("out_0", (1, T, D), _mybir.dt.float32, kind="ExternalOutput").ap()
    build(nc, w, consts, out)
    r = _run(nc, [arrays], core_ids=[0])
    return r.results[0]["out_0"]
```

```python
from contextlib import ExitStack
from math import lcm

import concourse.bass as bass
import numpy as np
from concourse import mybir

ALU = mybir.AluOpType
ACT = mybir.ActivationFunctionType
F32 = mybir.dt.float32
F32R = mybir.dt.float32r
I32 = mybir.dt.int32
AX = mybir.AxisListType

P = 128
T = 512
NT = T // P
D = 1024
ND = D // P
M = 256
NM = M // P
EPS = 1e-6
HEADS, NOPE, ROPE, QK, DV = 8, 64, 32, 96, 64
Q_RANK, KV_RANK = 384, 256
CONV = 512
MEM_HEADS = 4
SB_HEADS, SB_DIM = 16, 64
HG_HEADS = 8
D_FF = 4096

C_QLAT, C_KVLAT, C_KPE = 0, 384, 640
C_B, C_C, C_U = 672, 1184, 1696
C_QMEM, C_GATTN, C_GCONV, C_GMEM, C_R = 2208, 2720, 3232, 3744, 4256

K_EYE, K_ONE, K_CAUSAL = 0, 128, 256
K_PICK, K_PICK_HALVES = K_ONE + 8, K_ONE + 32
K_HALVES = 384
K_INVF, K_SIGN, K_EPS = 386, 387, 388
K_LEVEL = 392
LEVELS = 7
K_DIAG = K_EYE
K_COLS = K_LEVEL + LEVELS * P

VEC_ROWS = [("norm_g", 8), ("b_gate", 24), ("q_norm_g", 3), ("kv_norm_g", 2), ("conv_w", 12),
            ("conv_b", 4), ("mem_norm_g", 8), ("mem_q_g", 1), ("mem_k_g", 1), ("norm_gains_2", 32),
            ("hg_lb_logits_2", 8), ("hg_norm_gain_2", 1),
            ("q_head_g", 1), ("k_head_g", 1), ("sb_q_gain_2", 1), ("sb_k_gain_2", 1)]
VEC = {}
_at = 0
for _name, _n in VEC_ROWS:
    VEC[_name] = _at
    _at += _n
VEC_N = _at


def shape_constants():
    c = np.zeros((P, K_COLS), np.float32)
    c[:, K_EYE:K_EYE + P] = np.eye(P)
    c[:, K_ONE:K_ONE + 8] = 1.0
    c[:, K_PICK + 7] = 1.0
    c[:64, K_PICK_HALVES + 14] = 1.0
    c[64:, K_PICK_HALVES + 15] = 1.0
    q = np.arange(P)[:, None]
    s = np.arange(P)[None, :]
    c[:, K_CAUSAL:K_CAUSAL + P] = np.where(s < q, 0.0, -1e30)
    c[:64, K_HALVES] = 1.0
    c[64:, K_HALVES + 1] = 1.0
    freq = np.float32(10000.0) ** (-np.arange(0, ROPE, 2, dtype=np.float32) / np.float32(ROPE))
    c[NOPE:QK, K_INVF] = np.concatenate([freq, freq])
    c[NOPE:QK, K_SIGN] = np.concatenate([-np.ones(16), np.ones(16)])
    c[:, K_EPS] = EPS
    src, dst = np.arange(P)[:, None], np.arange(P)[None, :]
    for level in range(LEVELS):
        h = 1 << level
        same = src // (2 * h) == dst // (2 * h)
        c[:, K_LEVEL + level * P:K_LEVEL + (level + 1) * P] = same & (src // h % 2 == 0) & (dst // h % 2 == 1)
    return c


def wait(eng, sem, value):
    if isinstance(value, int) and value <= 0:
        return
    eng.wait_ge(sem, value)


def rounds(eng, n):
    yield 0
    if n > 1:
        with eng.Fori(1, n) as i:
            yield i


def at(i, size):
    return bass.ds(i * size, size) if not isinstance(i, int) else slice(i * size, (i + 1) * size)


RING = 4
UNIT = ND * P


LAG = 2


class Weights:

    def __init__(self, nc, sb, sem, w):
        self.stage = [sb(f"weight_stage{i}", [P, UNIT], F32) for i in range(RING)]
        self.hi = [sb(f"weight_hi{i}", [P, UNIT], F32R) for i in range(RING)]
        self.lo = [sb(f"weight_lo{i}", [P, UNIT], F32R) for i in range(RING)]
        self.loaded = [sem(f"weight_loaded{i}") for i in range(RING)]
        self.hi_done = sem("weight_hi_done")
        self.split_done = sem("weight_split_done")
        self.used = sem("weight_used")
        self.runs, self.n = [], 0
        self.first = {}

        def cols(name, lead, base):
            def view(f):
                full = w[name][lead].rearrange("(k p) n -> p k n", p=P)
                return full[:, :, bass.ds(f * P + base, P) if not isinstance(f, int) else slice(base + f * P, base + f * P + P)]
            return view

        def add(name, count, period, load, size=lambda r: UNIT):
            self.first[name] = self.n
            self.runs.append((self.n, count, period, load, size))
            self.n += count

        win = [cols("w_in", 0, c) for c in (C_QLAT,)][0]
        add("latent", 5, 1, lambda f, r: win(f))
        add("kpe", 1, 1, lambda f, r: w["w_in"][0].rearrange("(k p) n -> p k n", p=P)[:, :, C_KPE - 64:C_KPE + ROPE],
            lambda r: ND * QK)
        add("uq", 3, 1, lambda f, r: w["w_uq"][0, f * P:(f + 1) * P, :].rearrange("p (k n) -> p k n", k=1),
            lambda r: HEADS * QK)
        add("ukv", 2, 1, lambda f, r: w["w_ukv"][0, f * P:(f + 1) * P, :].rearrange("p (k n) -> p k n", k=1))
        qmem = cols("w_in", 0, C_QMEM)
        add("qmem", 4, 1, lambda f, r: qmem(f))
        mkv = cols("w_mkv", 0, 0)
        add("mkv", 8, 1, lambda f, r: mkv(f))
        conv = [cols("w_in", 0, c) for c in (C_C, C_U, C_B, C_GCONV)]
        add("conv", 16, 4, lambda f, r: conv[r](f))
        gates = [cols("w_in", 0, c) for c in (C_GATTN, C_GMEM)]
        add("gates", 8, 8, lambda f, r: gates[r // 4](r % 4))
        mix = [cols("w_in", 0, C_R), cols("w_br_attn", 0, 0), cols("w_in", 0, C_R + D), cols("w_br_conv", 0, 0),
               cols("w_in", 0, C_R + 2 * D), cols("w_br_mem", 0, 0)]
        add("mix", 48, 6, lambda f, r: mix[r](f), lambda r: UNIT // 2 if r % 2 else UNIT)
        for name, source, count in (("out", "w_out", 8), ("qkv", "sb_w_qkv_2", 24), ("sbo", "sb_w_o_2", 8)):
            add(name, count, 1, lambda f, r, v=cols(source, 0, 0): v(f))
        self.mlp_runs(add, w, 0, cols)
        for name, source, count in (("hgin", "hg_w_in_2", 32), ("hgo", "hg_w_o_2", 8)):
            add(name, count, 1, lambda f, r, v=cols(source, 0, 0): v(f))
        self.mlp_runs(add, w, 1, cols)

    def mlp_runs(self, add, w, layer, cols):
        one = cols("mlp_w1_2", layer, 0)
        w2 = w["mlp_w2_2"][layer].rearrange("(g k p) n -> g p k n", k=4, p=P)

        def two(g, r):
            group = w2[g] if isinstance(g, int) else w2[bass.ds(g, 1)].rearrange("a p k n -> p (a k) n")
            return group[:, :, r * 256:(r + 1) * 256]

        def body(f, r):
            which, r = divmod(r, 4)
            if which % 2 == 0:
                return one(f * 8 + (4 if which == 0 else 8) + r)
            return two(f * 2 + (0 if which == 1 else 1), r)

        def tail(f, r):
            return one(28 + r) if r < 4 else two(6 if r < 8 else 7, r % 4)

        add(f"mlp{layer}head", 4, 1, lambda f, r: one(f))
        add(f"mlp{layer}", 48, 16, body)
        add(f"mlp{layer}tail", 12, 12, tail)

    def steps(self, eng, lo, hi, straight=()):
        for start, count, period, load, size in self.runs:
            a, b = max(lo, start), min(hi, start + count)
            if a >= b:
                continue
            body = lcm(RING, period)
            times = (b - a) // body if b - a >= 2 * body and start not in straight else 0

            def one(i, j):
                q, r = divmod(a - start + j, period)
                return (i * body + a + j, (a + j) % RING, i * (body // RING) + (a + j) // RING + 1,
                        lambda: load(i * (body // period) + q, r), size(r))
            if times:
                with eng.Fori(0, times) as i:
                    for j in range(body):
                        yield one(i, j)
            for j in range(times * body, b - a):
                yield one(0, j)

    def behind(self, lo, hi):
        return max(lo - LAG, 0), min(hi - LAG, self.n)

    def load(self, sp, lo, hi):
        for u, slot, fills, source, size in self.steps(sp, *self.behind(lo, hi),
                                                       (self.first["mix"],)):
            wait(sp, self.split_done, u - RING + 1)
            src = source()
            k = src.shape[1]
            sp.dma_start(self.stage[slot][:, 0:size].rearrange("p (k n) -> p k n", k=k),
                         src).then_inc(self.loaded[slot], 16)

    def high(self, act, c, i=0, per=0):
        if c >= self.n:
            return
        slot = c % RING
        act.wait_ge(self.loaded[slot], i * (16 * per // RING) + 16 * (c // RING + 1))
        wait(act, self.used, i * per + (c - RING + 1))
        act.activation(self.hi[slot][:, :], self.stage[slot][:, :], ACT.Copy).then_inc(self.hi_done, 1)

    def low(self, pool, lo, hi):
        for u, slot, fills, _, size in self.steps(pool, *self.behind(lo, hi)):
            pool.wait_ge(self.hi_done, u + 1)
            pool.tensor_tensor(self.lo[slot][:, :], self.stage[slot][:, :], self.hi[slot][:, :].bitcast(F32),
                               ALU.subtract).then_inc(self.split_done, 1)

    def tile(self, u, k, a=0, n=P, width=P):
        s = u % RING
        return self.hi[s][:, k * width + a:k * width + a + n], self.lo[s][:, k * width + a:k * width + a + n]


def products(pe, out, pairs, before=None):
    pairs = list(pairs)
    n = 0
    for k, ((whi, wlo), (ahi, alo)) in enumerate(pairs):
        if before is not None:
            before(k)
        for l, r in ((wlo, ahi), (whi, alo), (whi, ahi)):
            last = pe.matmul(out, l, r, start=n == 0, stop=n == 3 * len(pairs) - 1)
            n += 1
    return last


class Norm:

    def __init__(self, S, name, groups, width, tokens=NT, squares=1, summed=1, columns=True):
        self.S, self.groups, self.width, self.tokens = S, groups, width, tokens
        self.signals = {}
        counts = {"squared": squares, "summed": summed, "rooted": 1, "inverted": 1, "spread": groups,
                  "applied": max(groups, squares)}
        self.counts = counts
        for event, n in counts.items():
            self.signals[event] = S.shared(f"norm_{event}")
            S.advance(f"norm_{event}", n)
        if columns:
            self.cols = groups * tokens
            self.root, self.rstd = S.columns(self.cols), S.columns(self.cols)

    def sem(self, event):
        return self.signals[event][0]

    def wait(self, eng, event, n):
        if n > 0:
            sem, before = self.signals[event]
            eng.wait_ge(sem, before + n)

    def square(self, act, out, src):
        act.activation(out, src, ACT.Square).then_inc(self.sem("squared"), 1)

    def roots(self, act, bank):
        self.wait(act, "summed", self.counts["summed"])
        act.activation(self.root, bank[:, 0:self.cols], ACT.Sqrt, bias=self.S.const[:, K_EPS:K_EPS + 1],
                       scale=1.0 / self.width).then_inc(self.sem("rooted"), 1)

    def invert(self, dve):
        self.wait(dve, "rooted", 1)
        dve.reciprocal(self.rstd, self.root).then_inc(self.sem("inverted"), 1)

    def spread(self, pe, bank):
        self.wait(pe, "inverted", 1)
        for i in range(self.tokens):
            last = pe.matmul(bank[:, i * P:(i + 1) * P], self.rstd[:, i:i + 1].to_broadcast([P, P]), self.S.eye,
                             start=True, stop=True)
        last.then_inc(self.sem("spread"), 1)


class State:
    pass


class ModelNorm(Norm):

    def __init__(self, S, src, gain, hi, lo, tokens=NT, width=D, sum_bank=7, spread_bank=7, work=0):
        self.tiles = width // P
        super().__init__(S, "model", 1, width, tokens, self.tiles)
        self.src, self.gain, self.hi, self.lo, self.tk = src, gain, hi, lo, tokens * P
        self.scratch = S.scratch[:, work:, :]
        self.sum_bank, self.spread_bank = S.ps[sum_bank], S.ps[spread_bank]
        self.hi_done, self.hi0 = S.shared("split_hi")
        self.lo_done, self.lo0 = S.shared("split_lo")
        S.advance("split_hi", self.tiles)
        S.advance("split_lo", self.tiles)

    def square_tile(self, act, t):
        self.square(act, self.scratch[:, t, 0:self.tk], self.src[:, t, 0:self.tk])

    def sum_tile(self, pe, t):
        self.wait(pe, "squared", t + 1)
        for i in range(self.tokens):
            last = pe.matmul(self.sum_bank[:, i:i + 1], self.scratch[:, t, i * P:(i + 1) * P], self.S.ones[:, 0:1],
                             start=t == 0 and i == 0, stop=t == self.tiles - 1, skip_group_check=True)
        if t == self.tiles - 1:
            last.then_inc(self.sem("summed"), 1)

    def act_root(self, act):
        self.roots(act, self.sum_bank)

    def act_high(self, act):
        for t in range(self.tiles):
            self.wait(act, "applied", t + 1)
            act.activation(self.hi[:, t, 0:self.tk], self.scratch[:, t, 0:self.tk],
                           ACT.Copy).then_inc(self.hi_done, 1)

    def pe_spread(self, pe):
        self.spread(pe, self.spread_bank)

    def dve_apply(self, dve):
        self.invert(dve)
        self.wait(dve, "spread", 1)

        def low(t):
            dve.wait_ge(self.hi_done, self.hi0 + t + 1)
            dve.tensor_tensor(self.lo[:, t, 0:self.tk], self.scratch[:, t, 0:self.tk],
                              self.hi[:, t, 0:self.tk].bitcast(F32), ALU.subtract).then_inc(self.lo_done, 1)
        for t in range(self.tiles):
            dve.scalar_tensor_tensor(out=self.scratch[:, t, 0:self.tk], in0=self.src[:, t, 0:self.tk],
                                     scalar=self.S.vec[:, self.gain + t:self.gain + t + 1],
                                     in1=self.spread_bank[:, 0:self.tk], op0=ALU.mult,
                                     op1=ALU.mult).then_inc(self.sem("applied"), 1)
            if t >= 2:
                low(t - 2)
        low(self.tiles - 2)
        low(self.tiles - 1)

    def ready(self, pe):
        return lambda k: pe.wait_ge(self.lo_done, self.lo0 + k + 1)


def setup(S, w, consts, norm):
    nc, W = S.nc, S.W
    loaded, vec_loaded, zeroed = S.sem("setup_loaded"), S.sem("vec_loaded"), S.sem("rows_zeroed")
    turned, copied = S.sem("x_turned"), S.sem("x_copied")
    vec_turned, vec_copied = S.sem("vec_turned"), S.sem("vec_copied")
    pos_f, spread = S.sem("pos_float"), S.sem("pos_spread")
    x_loaded = S.sem("x_loaded")
    with ExitStack() as scope:
        def sb(name, shape, dt):
            return scope.enter_context(nc.sbuf_tensor(name, shape, dt))
        x_tok = sb("x_tok", [P, NT, D], F32)
        rows = sb("vec_rows", [P, P], F32)
        pos_i = sb("pos_i", [1, T], I32)
        pos = sb("pos", [1, T], F32)
        block = scope.enter_context(nc.Block())

        @block.sync
        def _(sp):
            sp.dma_start(x_tok[:, :, :], w["x"][0].rearrange("(i p) d -> p i d", p=P)).then_inc(x_loaded, 16)
            sp.dma_start(S.const[:, :], consts).then_inc(loaded, 16)
            sp.dma_start(pos_i[:, :], w["positions"]).then_inc(loaded, 16)
            sp.wait_ge(zeroed, 1)
            n = 0
            for name, k in VEC_ROWS:
                r, src = VEC[name], w[name]
                if name == "conv_w":
                    views = [(rows[r:r + k, :], src[0].rearrange("t (c p) -> (t c) p", p=P))]
                elif name == "norm_gains_2":
                    views = [(rows[r:r + k, :], src.rearrange("l s (c p) -> (l s c) p", p=P))]
                elif name in ("sb_q_gain_2", "sb_k_gain_2"):
                    views = [(rows[r:r + 1, 0:64], src), (rows[r:r + 1, 64:128], src)]
                elif name in ("q_head_g", "k_head_g"):
                    views = [(rows[r:r + 1, 0:QK], src)]
                else:
                    views = [(rows[r:r + k, :], src[0].rearrange("(c p) -> c p", p=P))]
                for dst, view in views:
                    sp.dma_start(dst, view).then_inc(vec_loaded, 16)
                    n += 1
            S.n_vec = n
            W.load(sp, 0, 2 * RING)

        @block.gpsimd
        def _(pool):
            pool.memset(rows[:, :], 0.0).then_inc(zeroed, 1)
            W.low(pool, 0, RING)

        @block.tensor
        def _(pe):
            pe.wait_ge(loaded, 32)
            pe.wait_ge(x_loaded, 16)
            for c in range(ND):
                if c >= 4:
                    pe.wait_ge(copied, c - 3)
                for i in range(NT):
                    last = pe.transpose(S.ps[c % 4][:, i * P:(i + 1) * P], x_tok[:, i, c * P:(c + 1) * P], S.eye)
                last.then_inc(turned, 1)
                if c >= 2:
                    norm.sum_tile(pe, c - 2)
            norm.sum_tile(pe, ND - 2)
            norm.sum_tile(pe, ND - 1)
            pe.wait_ge(vec_loaded, 16 * S.n_vec)
            pe.transpose(S.ps[4][:, 0:P], rows[:, :], S.eye).then_inc(vec_turned, 1)
            pe.wait_ge(pos_f, 1)
            pe.matmul(S.ps[5][0:QK, :], S.ones[0:1, 0:1].to_broadcast([1, QK]), pos[:, :], start=True, stop=True).then_inc(spread, 1)

        @block.scalar
        def _(act):
            for c in range(ND):
                act.wait_ge(turned, c + 1)
                act.activation(S.x[:, c, :], S.ps[c % 4][:, :], ACT.Copy).then_inc(copied, 1)
                act.wait_ge(copied, c + 1)
                norm.square_tile(act, c)
            for u in range(RING):
                W.high(act, u)
        @block.vector
        def _(dve):
            dve.wait_ge(loaded, 32)
            dve.tensor_copy(pos[:, :], pos_i[:, :]).then_inc(pos_f, 1)
            dve.tensor_copy(S.eye_r[:, :], S.eye[0:ND, 0:ND]).then_inc(vec_copied, 1)
            dve.wait_ge(vec_turned, 1)
            dve.tensor_copy(S.vec[:, :], S.ps[4][:, 0:P]).then_inc(vec_copied, 1)
            dve.wait_ge(vec_copied, 2)
            dve.tensor_scalar(S.q_gain[:, :], S.vec[:, VEC["q_head_g"]:VEC["q_head_g"] + 1], QK ** -0.5, None,
                              ALU.mult).then_inc(vec_copied, 1)
            dve.tensor_scalar(S.mq_gain[:, :], S.vec[:, VEC["mem_q_g"]:VEC["mem_q_g"] + 1], P ** -0.5, None,
                              ALU.mult).then_inc(vec_copied, 1)
            lg = S.vec[:, VEC["hg_lb_logits_2"]:VEC["hg_lb_logits_2"] + 8]
            dve.tensor_tensor(S.lb[:, :], lg, lg, ALU.subtract).then_inc(vec_copied, 1)
            dve.wait_ge(spread, 1)
            r = slice(NOPE, QK)
            dve.tensor_scalar(S.cos[r, :], S.ps[5][r, :], S.const[r, K_INVF:K_INVF + 1], None,
                              ALU.mult).then_inc(vec_copied, 1)


def angles(S, ang):
    r = slice(NOPE, QK)
    angle = S.sem("angle_steps")
    whole = ang[r, 5, :].bitcast(I32)

    def reduce(dve):
        steps = 0

        def step(ins):
            nonlocal steps
            ins.then_inc(angle, 1)
            steps += 1
            dve.wait_ge(angle, steps)
        for quarter, dst in ((0.25, 4), (0.0, 3)):
            step(dve.tensor_scalar(ang[r, 1, :], S.cos[r, :], 1.0 / (2 * np.pi), quarter, ALU.mult, ALU.add))
            step(dve.tensor_copy(whole, ang[r, 1, :]))
            step(dve.tensor_copy(ang[r, 2, :], whole))
            for k, part in enumerate(TWO_PI):
                step(dve.scalar_tensor_tensor(out=ang[r, dst, :], in0=ang[r, 2, :], scalar=-part,
                                              in1=S.cos[r, :] if k == 0 else ang[r, dst, :], op0=ALU.mult,
                                              op1=ALU.add))
            if quarter:
                step(dve.tensor_scalar(ang[r, dst, :], ang[r, dst, :], float(np.pi / 2), None, ALU.add))
        assert steps == 13
        dve.tensor_scalar(ang[r, 3:5, :], ang[r, 3:5, :], PI_DOWN, -PI_DOWN, ALU.min, ALU.max).then_inc(angle, 1)
        dve.wait_ge(angle, 16)
        dve.tensor_scalar(S.sin[r, :], ang[r, 1, :], S.const[r, K_SIGN:K_SIGN + 1], None, ALU.mult)

    def sines(act):
        act.wait_ge(angle, 14)
        act.activation(S.cos[r, :], ang[r, 4, :], ACT.Sin).then_inc(angle, 1)
        act.activation(ang[r, 1, :], ang[r, 3, :], ACT.Sin).then_inc(angle, 1)

    return reduce, sines


PI_DOWN = 3.1415925
_A = 6.28125
_B = float(np.float32(np.floor((2 * np.pi - _A) * 2 ** 21) / 2 ** 21))
TWO_PI = (_A, _B, 2 * np.pi - _A - _B)
SWAP = [(i + 16) % 32 for i in range(32)]


def project(S, dests, u0, act_side, norm=None, after=(), pe_second=None, act_second=None, sp_first=None,
            dve_last=None, act_last=None):
    nc, W = S.nc, S.W
    out_done, before = S.shared("projected")
    ahi, alo, tokens = act_side
    n_units = len(dests)
    with nc.Block() as block:
        @block.sync
        def _(sp):
            if sp_first is not None:
                sp_first(sp)
            W.load(sp, u0 + 2 * RING, u0 + n_units + 2 * RING)

        @block.gpsimd
        def _(pool):
            W.low(pool, u0 + RING, u0 + n_units + RING)

        @block.tensor
        def _(pe):
            if norm is not None:
                norm.pe_spread(pe)
            for n, (dst, rows, _) in enumerate(dests):
                u = u0 + n
                pe.wait_ge(W.split_done, u + 1)
                if n >= 4:
                    pe.wait_ge(out_done, before + n - 3)
                products(pe, S.ps[n % 4][0:rows, 0:tokens],
                         ((W.tile(u, k, 0, rows, rows), (ahi[:, k, 0:tokens], alo[:, k, 0:tokens]))
                          for k in range(ND)), norm.ready(pe) if norm is not None and n == 0 else None
                         ).then_inc(W.used, 1)
                if n == 0 and pe_second is not None:
                    pe_second(pe)
                for later, t, unit in after:
                    if unit == n - 1:
                        later.sum_tile(pe, t)
            for later, t, unit in after:
                if unit == n_units - 1:
                    later.sum_tile(pe, t)

        @block.scalar
        def _(act):
            if norm is not None:
                norm.act_root(act)
                norm.act_high(act)
            for n, (dst, rows, func) in enumerate(dests):
                act.wait_ge(W.used, u0 + n + 1)
                act.activation(dst, S.ps[n % 4][0:rows, 0:tokens], func).then_inc(out_done, 1)
                W.high(act, u0 + n + RING)
                if n == 0 and act_second is not None:
                    act_second(act)
                for later, t, unit in after:
                    if unit == n:
                        act.wait_ge(out_done, before + n + 1)
                        later.square_tile(act, t)
            if act_last is not None:
                act_last(act)

        if norm is not None:
            @block.vector
            def _(dve):
                norm.dve_apply(dve)
                if dve_last is not None:
                    dve_last(dve)
    S.advance("projected", n_units)


def project_loop(S, u0, groups, ahi, alo, norm):
    nc, W = S.nc, S.W
    out_done, before = S.shared("projected")
    total = sum(n for _, _, n in groups)
    with nc.Block() as block:
        @block.sync
        def _(sp):
            W.load(sp, u0 + 2 * RING, u0 + total + 2 * RING)

        @block.gpsimd
        def _(pool):
            W.low(pool, u0 + RING, u0 + total + RING)

        @block.tensor
        def _(pe):
            norm.pe_spread(pe)
            for i in rounds(pe, total // 4):
                for j in range(4):
                    pe.wait_ge(W.split_done, i * 4 + (u0 + j + 1))
                    if not isinstance(i, int):
                        pe.wait_ge(out_done, i * 4 + (before + j - 3))
                    first = isinstance(i, int) and j == 0
                    products(pe, S.ps[j][:, :], ((W.tile(u0 + j, k), (ahi[:, k, :], alo[:, k, :]))
                                                 for k in range(ND)), norm.ready(pe) if first else None
                             ).then_inc(W.used, 1)

        @block.scalar
        def _(act):
            norm.act_root(act)
            norm.act_high(act)
            base = 0
            for dst, func, n in groups:
                with act.Fori(0, n // 4) as i:
                    for j in range(4):
                        act.wait_ge(W.used, i * 4 + (u0 + base + j + 1))
                        act.activation(dst[:, bass.ds(i * 4 + j, 1), :].rearrange("p a t -> p (a t)"),
                                       S.ps[j][:, :], func).then_inc(out_done, 1)
                        W.high(act, u0 + base + j + RING, i, 4)
                base += n

        @block.vector
        def _(dve):
            norm.dve_apply(dve)
    S.advance("projected", total)


def add_to_x(S, u0, ahi, alo, make_norm, split=None):
    nc, W = S.nc, S.W
    added, before = S.shared("x_added")
    (hi_done, hi0), (lo_done, lo0) = S.shared("split_hi"), S.shared("split_lo")
    if split is not None:
        S.advance("split_hi", ND)
        S.advance("split_lo", ND)
    later = make_norm()
    with nc.Block() as block:
        @block.sync
        def _(sp):
            W.load(sp, u0 + 2 * RING, u0 + ND + 2 * RING)

        @block.gpsimd
        def _(pool):
            W.low(pool, u0 + RING, u0 + ND + RING)

        @block.tensor
        def _(pe):
            for n in range(ND):
                pe.wait_ge(W.split_done, u0 + n + 1)
                if n >= 4:
                    pe.wait_ge(added, before + n - 3)
                ready = (lambda k: pe.wait_ge(lo_done, lo0 + k + 1)) if split is not None and n == 0 else None
                products(pe, S.ps[n % 4][:, :], ((W.tile(u0 + n, k), (ahi[:, k, :], alo[:, k, :]))
                                                 for k in range(ND)), ready).then_inc(W.used, 1)
                if n >= 1:
                    later.sum_tile(pe, n - 1)
            later.sum_tile(pe, ND - 1)

        @block.scalar
        def _(act):
            if split is not None:
                for t in range(ND):
                    act.activation(ahi[:, t, :], split[:, t, :], ACT.Copy).then_inc(hi_done, 1)
                act.wait_ge(lo_done, lo0 + ND)
            for n in range(ND):
                act.wait_ge(W.used, u0 + n + 1)
                if n < ND - 1:
                    W.high(act, u0 + n + RING)
                act.wait_ge(added, before + n + 1)
                later.square_tile(act, n)
            W.high(act, u0 + ND - 1 + RING)

        @block.vector
        def _(dve):
            if split is not None:
                for t in range(ND):
                    dve.wait_ge(hi_done, hi0 + t + 1)
                    dve.tensor_tensor(alo[:, t, :], split[:, t, :], ahi[:, t, :].bitcast(F32),
                                      ALU.subtract).then_inc(lo_done, 1)
            for n in range(ND):
                dve.wait_ge(W.used, u0 + n + 1)
                dve.tensor_tensor(S.x[:, n, :], S.x[:, n, :], S.ps[n % 4][:, :], ALU.add).then_inc(added, 1)
    S.advance("x_added", ND)
    return later


def softmax_attention(S, name, heads, q, k, v, key_tiles, dv, out, pt, prob):
    nc = S.nc
    keys = key_tiles * P
    per = P // dv
    scored, maxed, exped = S.sem(f"{name}_scored"), S.sem(f"{name}_maxed"), S.sem(f"{name}_exped")
    inverted, scaled = S.sem(f"{name}_inverted"), S.sem(f"{name}_scaled")
    turned, kept = S.sem(f"{name}_turned"), S.sem(f"{name}_kept")
    summed, out_done = S.sem(f"{name}_summed"), S.sem(f"{name}_out_done")
    items = [(h, i) for h in range(heads) for i in range(NT)]
    nmax = S.columns(len(items))
    total = S.columns(len(items))
    inv = S.columns(len(items))
    score_banks, turn_banks, out_banks = S.ps[0:3], S.ps[3:5], S.ps[5:7]
    with nc.Block() as block:
        @block.tensor
        def _(pe):
            def score(n):
                h, i = items[n]
                wait(pe, exped, n - 2)
                pe.matmul(score_banks[n % 3][:, 0:keys], q(h)[:, i * P:(i + 1) * P], k(h), start=True,
                          stop=True).then_inc(scored, 1)

            def turn(n):
                wait(pe, kept, n - 1)
                pe.wait_ge(scaled, n + 1)
                for b in range(key_tiles):
                    last = pe.transpose(turn_banks[n % 2][:, b * P:(b + 1) * P],
                                        prob[n % 3][:, b * P:(b + 1) * P], S.eye)
                last.then_inc(turned, 1)

            def weigh(h):
                o = h // per
                wait(pe, out_done, o - 1)
                pe.wait_ge(kept, NT * (h + 1))
                r = h % per * dv
                for b in range(key_tiles):
                    last = pe.matmul(out_banks[o % 2][r:r + dv, :], v(h, b), pt[h % 2][:, b, :],
                                     start=b == 0, stop=b == key_tiles - 1)
                last.then_inc(summed, 1)

            for n in range(len(items) + 2):
                if n == 0:
                    score(0)
                    score(1)
                if n + 2 < len(items):
                    score(n + 2)
                if n < len(items):
                    turn(n)
                if n >= 5 and (n - 5) % NT == 0:
                    weigh((n - 5) // NT)

        @block.vector
        def _(dve):
            def normalise(n):
                dve.wait_ge(exped, n + 1)
                dve.reciprocal(inv[:, n:n + 1], total[:, n:n + 1]).then_inc(inverted, 1)
                dve.wait_ge(inverted, n + 1)
                dve.tensor_scalar(prob[n % 3][:, 0:keys], prob[n % 3][:, 0:keys], inv[:, n:n + 1], None,
                                  ALU.mult).then_inc(scaled, 1)
            for n in range(len(items)):
                dve.wait_ge(scored, n + 1)
                dve.tensor_reduce(nmax[:, n:n + 1], score_banks[n % 3][:, 0:keys], AX.X, ALU.max,
                                  negate=True).then_inc(maxed, 1)
                if n >= 1:
                    normalise(n - 1)
            normalise(len(items) - 1)

        @block.scalar
        def _(act):
            def keep(n):
                h, i = items[n]
                act.wait_ge(turned, n + 1)
                wait(act, summed, h - 1)
                act.activation(pt[h % 2][:, 0:key_tiles, i * P:(i + 1) * P],
                               turn_banks[n % 2][:, 0:keys].rearrange("p (b t) -> p b t", b=key_tiles),
                               ACT.Copy).then_inc(kept, 1)

            def put(o):
                act.wait_ge(summed, per * (o + 1))
                act.activation(out[:, o, :], out_banks[o % 2][:, :], ACT.Copy).then_inc(out_done, 1)
            for n in range(len(items)):
                act.wait_ge(maxed, n + 1)
                wait(act, turned, n - 2)
                act.activation(prob[n % 3][:, 0:keys], score_banks[n % 3][:, 0:keys], ACT.Exp,
                               bias=nmax[:, n:n + 1], accum_out=total[:, n:n + 1]).then_inc(exped, 1)
                if n >= 2:
                    keep(n - 2)
                if n >= 8 and (n - 8) % (NT * per) == NT * per - 1:
                    put((n - 8) // (NT * per))
            keep(len(items) - 2)
            keep(len(items) - 1)
            done = len([n for n in range(8, len(items)) if (n - 8) % (NT * per) == NT * per - 1])
            for o in range(done, heads // per):
                put(o)


class HeadNorm(Norm):

    def __init__(self, S, name, groups, width, src, rows, gain, bank, factors, tokens=NT, halves=None, work=0,
                 more=None, extra=None, rotate=None):
        super().__init__(S, name, groups, width, tokens, squares=groups, summed=groups, columns=False)
        self.src, self.rows, self.gain, self.work, self.halves = src, rows, gain, work, halves
        self.bank, self.more, self.extra, self.rotate = S.ps[bank], more, extra, rotate
        self.tk = tokens * P
        self.n = groups * (2 if halves else 1)
        self.sums = self.bank[0:self.n, 0:self.tk]
        self.factors, self.high, self.low = (f[0:self.n, 0:self.tk] for f in factors)
        self.split = S.shared("norm_split")
        S.advance("norm_split", 2)

    def squares_of(self, g):
        return self.S.scratch[0:self.src(g).shape[0], self.work + g, 0:self.tk]

    def square_group(self, act, g):
        self.square(act, self.squares_of(g), self.src(g))

    def sum_group(self, pe, g):
        self.wait(pe, "squared", g + 1)
        if g == 0 and self.more is not None:
            squares, ones = self.more
            pe.matmul(self.sums, ones[:, 0:self.n], squares, start=True, stop=False)
        sq = self.squares_of(g)
        c = K_PICK_HALVES + 14 - 2 * g if self.halves else K_PICK + 7 - g
        pe.matmul(self.sums, self.S.const[0:sq.shape[0], c:c + self.n], sq, start=g == 0 and self.more is None,
                  stop=g == self.groups - 1).then_inc(self.sem("summed"), 1)

    def root_all(self, act):
        self.wait(act, "summed", self.groups)
        act.activation(self.sums, self.sums, ACT.Sqrt, bias=self.S.const[0:self.n, K_EPS:K_EPS + 1],
                       scale=1.0 / self.width).then_inc(self.sem("rooted"), 1)

    def invert_all(self, dve):
        self.wait(dve, "rooted", 1)
        dve.reciprocal(self.factors, self.sums).then_inc(self.sem("inverted"), 1)

    def split_high(self, act):
        self.wait(act, "inverted", 1)
        act.activation(self.high, self.factors, ACT.Copy).then_inc(self.split[0], 1)

    def split_low(self, dve):
        dve.wait_ge(self.split[0], self.split[1] + 1)
        dve.tensor_tensor(self.low, self.factors, self.high.bitcast(F32), ALU.subtract).then_inc(self.split[0], 1)

    def spread_group(self, pe, bank, g, free_at=None):
        if g == 0:
            pe.wait_ge(self.split[0], self.split[1] + 2)
        if free_at is not None:
            sem, before = self.signals["applied"]
            pe.wait_ge(sem, before + free_at)
        lhs = self.halves(g) if self.halves else self.S.eye_r[0:self.n, g:g + 1].to_broadcast([self.n, self.rows])
        pe.matmul(bank[0:self.rows, 0:self.tk], lhs, self.high, start=True, stop=False)
        pe.matmul(bank[0:self.rows, 0:self.tk], lhs, self.low, start=False,
                  stop=True).then_inc(self.sem("spread"), 1)

    def apply_group(self, dve, g, bank):
        self.wait(dve, "spread", g + 1)
        if self.extra is not None:
            self.extra(dve, g, bank)
        s = self.src(g)
        r = s.shape[0]
        dve.scalar_tensor_tensor(out=s, in0=s, scalar=self.gain[0:r, :], in1=bank[0:r, 0:self.tk],
                                 op0=ALU.mult, op1=ALU.mult).then_inc(self.sem("applied"), 1)
        if self.rotate is not None:
            self.rotate(dve, g)


def head_norms(S, jobs, turn=None, keep=None, act_first=None, act_last=None, dve_first=None, pe_last=None,
               pool_side=None):
    groups = jobs[0].groups
    with S.nc.Block() as block:
        @block.scalar
        def _(act):
            if act_first is not None:
                act_first(act)
            for g in range(groups):
                jobs[0].square_group(act, g)
            jobs[0].root_all(act)
            for g in range(groups):
                if keep is not None:
                    keep(act, g)
                if g == groups // 2:
                    jobs[0].split_high(act)
                if len(jobs) > 1:
                    jobs[0].wait(act, "summed", g + 1)
                    jobs[1].square_group(act, g)
            if len(jobs) > 1:
                jobs[1].root_all(act)
                jobs[1].split_high(act)
            if act_last is not None:
                act_last(act)

        @block.tensor
        def _(pe):
            for g in range(groups):
                jobs[0].sum_group(pe, g)
            if turn is not None:
                for g in range(groups):
                    turn(pe, g)
            if pe_last is not None:
                pe_last(pe)
            for j, job in enumerate(jobs):
                for g in range(groups):
                    n = j * groups + g
                    job.spread_group(pe, S.ps[2 + n % 3], g, free_at=g - 2 if n >= 3 else None)
                    if j + 1 < len(jobs):
                        jobs[j + 1].sum_group(pe, g)

        @block.vector
        def _(dve):
            if dve_first is not None:
                dve_first(dve)
            for j, job in enumerate(jobs):
                job.invert_all(dve)
                job.split_low(dve)
                for g in range(groups):
                    job.apply_group(dve, g, S.ps[2 + (j * groups + g) % 3])

        if pool_side is not None:
            @block.gpsimd
            def _(pool):
                pool_side(pool)


def first_block(S, w, norm, norm2):
    nc, W = S.nc, S.W
    f = W.first
    outer = ExitStack()
    with outer:
        def sbo(name, shape, dt=F32):
            return outer.enter_context(nc.sbuf_tensor(name, shape, dt))
        o_attn = sbo("o_attn", [P, 4, T])
        with ExitStack() as mla:
            def sb(name, shape, dt=F32):
                return mla.enter_context(nc.sbuf_tensor(name, shape, dt))
            qh = sb("q_heads", [QK, HEADS, T])
            kv = sb("kv_heads", [P, HEADS, T])
            v_tok = sb("v_tok", [P, NT, HEADS, DV])
            kpe = sb("k_rope", [QK, 3, T])
            lat = kv
            with ExitStack() as lat_scope:
                lhi = lat_scope.enter_context(nc.sbuf_tensor("latent_hi", [P, 5, T], F32R))
                llo = lat_scope.enter_context(nc.sbuf_tensor("latent_lo", [P, 5, T], F32R))
                q_norm = ModelNorm(S, lat, VEC["q_norm_g"], lhi, llo, width=Q_RANK, sum_bank=6, spread_bank=6)
                kv_norm = ModelNorm(S, lat[:, 3:5, :], VEC["kv_norm_g"], lhi[:, 3:5, :], llo[:, 3:5, :],
                                    width=KV_RANK, sum_bank=5, spread_bank=5, work=3)
                reduce, sines = angles(S, qh)
                project(S, [(lat[:, n, :], P, ACT.Copy) for n in range(5)] + [(kpe[:, 0, :], QK, ACT.Copy)],
                        f["latent"], (S.ahi, S.alo, T), norm,
                        [(q_norm, t, t) for t in range(3)] + [(kv_norm, t, 3 + t) for t in range(2)],
                        dve_last=reduce, act_last=sines)
                up_project(S, qh, kv, lhi, llo, q_norm, kv_norm)
            with nc.sbuf_tensor("attn_factor_parts", [HEADS, 4, T], F32R) as parts:
                turn_values_and_rope(S, qh, kv, v_tok, kpe, parts)
            p_scope = ExitStack()
            with p_scope:
                prob = [p_scope.enter_context(nc.sbuf_tensor(f"attn_prob{i}", [P, T], F32)) for i in range(3)]
                pt = [S.scratch[:, 0:4, :], S.scratch[:, 4:8, :]]
                softmax_attention(S, "mla", HEADS, lambda h: qh[:, h, :], lambda h: kv[0:QK, h, :],
                                  lambda h, b: v_tok[:, b, h, :], NT, DV, o_attn, pt, prob)
        o_mem = sbo("o_mem", [P, 4, T])
        memory_branch(S, w, o_mem)
        return mix_branches(S, w, o_attn, o_mem, norm2)


def up_project(S, qh, kv, lhi, llo, q_norm, kv_norm):
    nc, W = S.nc, S.W
    out_done, head_done = S.sem("up_out_done"), S.sem("up_head_done")
    uq, ukv = W.first["uq"], W.first["ukv"]
    n_units = 5
    with nc.Block() as block:
        @block.sync
        def _(sp):
            W.load(sp, uq + 2 * RING, uq + n_units + 2 * RING)

        @block.gpsimd
        def _(pool):
            W.low(pool, uq + RING, uq + n_units + RING)

        @block.tensor
        def _(pe):
            q_norm.pe_spread(pe)
            kv_norm.pe_spread(pe)
            pe.wait_ge(W.split_done, uq + 3)
            for h in range(HEADS):
                wait(pe, out_done, h - 3)
                last = products(pe, S.ps[h % 4][0:QK, :], ((W.tile(uq + k, 0, h * QK, QK), (lhi[:, k, :], llo[:, k, :]))
                                                          for k in range(3)), q_norm.ready(pe) if h == 0 else None)
                last.then_inc(head_done, 1)
            pe.wait_ge(head_done, HEADS)
            pe.sem_inc(W.used, 3)
            pe.wait_ge(W.split_done, ukv + 2)
            for h in range(HEADS):
                wait(pe, out_done, HEADS + h - 3)
                products(pe, S.ps[h % 4][:, :], ((W.tile(ukv + k, 0, h * P, P), (lhi[:, 3 + k, :], llo[:, 3 + k, :]))
                                                 for k in range(2)),
                         kv_norm.ready(pe) if h == 0 else None).then_inc(head_done, 1)
            pe.wait_ge(head_done, 2 * HEADS)
            pe.sem_inc(W.used, 2)

        @block.scalar
        def _(act):
            q_norm.act_root(act)
            kv_norm.act_root(act)
            q_norm.act_high(act)
            kv_norm.act_high(act)
            for n in range(2 * HEADS):
                act.wait_ge(head_done, n + 1)
                h = n % HEADS
                dst, rows = (qh[:, h, :], QK) if n < HEADS else (kv[:, h, :], P)
                act.activation(dst, S.ps[n % 4][0:rows, :], ACT.Copy).then_inc(out_done, 1)
                if n == HEADS - 1:
                    for k in range(3):
                        W.high(act, uq + RING + k)
            for k in range(3, n_units):
                W.high(act, uq + RING + k)

        @block.vector
        def _(dve):
            q_norm.dve_apply(dve)
            kv_norm.dve_apply(dve)


def turn_values_and_rope(S, qh, kv, v_tok, kpe, parts):
    turned, kept = S.sem("v_turned"), S.sem("v_kept")
    kpe_squared, kpe_steps = S.sem("k_rope_squared"), S.sem("k_rope_steps")
    swapped_done, cos_done, sin_done, rotated = (S.sem(f"q_rope_{x}") for x in ("swapped", "cos", "sin", "added"))
    kg = S.vec[:, VEC["k_head_g"]:VEC["k_head_g"] + 1]
    r = slice(NOPE, QK)

    def turn(pe, h):
        wait(pe, kept, h - 2)
        for i in range(NT):
            last = pe.transpose(S.ps[5 + h % 3][:, i * P:(i + 1) * P], kv[:, h, i * P:(i + 1) * P], S.eye)
        last.then_inc(turned, 1)

    def keep(act, h):
        act.wait_ge(turned, h + 1)
        act.activation(v_tok[:, :, h, :], S.ps[5 + h % 3][:, :].rearrange("p (i c) -> p i c", i=NT)[:, :, NOPE:P],
                       ACT.Copy).then_inc(kept, 1)

    def square_kpe(act):
        act.activation(S.kpe_sq[r, :], kpe[r, 0, :], ACT.Square).then_inc(kpe_squared, 1)

    def rotate_kpe(dve):
        dve.wait_ge(kpe_squared, 1)
        done = 0

        def step(ins):
            nonlocal done
            ins.then_inc(kpe_steps, 1)
            done += 1
            dve.wait_ge(kpe_steps, done)
        step(dve.tensor_scalar(kpe[r, 0, :], kpe[r, 0, :], kg[r, :], None, ALU.mult))
        step(dve.stream_shuffle(kpe[r, 1, :], kpe[r, 0, :], SWAP))
        step(dve.tensor_tensor(kpe[r, 0, :], kpe[r, 0, :], S.cos[r, :], ALU.mult))
        step(dve.tensor_tensor(kpe[r, 1, :], kpe[r, 1, :], S.sin[r, :], ALU.mult))
        step(dve.tensor_tensor(kpe[r, 2, :], kpe[r, 0, :], kpe[r, 1, :], ALU.add))

    def key_rope(dve, g, bank):
        dve.wait_ge(turned, g + 1)
        dve.tensor_tensor(kv[r, g, :], kpe[r, 2, :], bank[r, :], ALU.mult)

    def query_cos(dve, g):
        dve.wait_ge(swapped_done, g + 1)
        dve.tensor_tensor(qh[r, g, :], qh[r, g, :], S.cos[r, :], ALU.mult).then_inc(cos_done, 1)

    def query_rotate(dve, g):
        q_job.wait(dve, "applied", g + 1)
        dve.stream_shuffle(S.scratch[r, g, :], qh[r, g, :], SWAP).then_inc(swapped_done, 1)
        if g > 0:
            query_cos(dve, g - 1)
        if g == HEADS - 1:
            query_cos(dve, g)

    def query_sum(pool):
        for g in range(HEADS):
            pool.wait_ge(swapped_done, g + 1)
            pool.tensor_tensor(S.scratch[r, g, :], S.scratch[r, g, :], S.sin[r, :], ALU.mult).then_inc(sin_done, 1)
            pool.wait_ge(sin_done, g + 1)
            pool.wait_ge(cos_done, g + 1)
            pool.tensor_tensor(qh[r, g, :], qh[r, g, :], S.scratch[r, g, :], ALU.add).then_inc(rotated, 1)

    q_job = HeadNorm(S, "q_head", HEADS, QK, lambda g: qh[:, g, :], QK, S.q_gain[:, 0:1], 0,
                     (kpe[:, 1, :], parts[:, 0, :], parts[:, 1, :]), rotate=query_rotate)
    k_job = HeadNorm(S, "k_head", HEADS, QK, lambda g: kv[0:NOPE, g, :], QK, kg, 1, (kpe[:, 2, :], parts[:, 2, :], parts[:, 3, :]),
                     more=(S.kpe_sq[r, :], S.ones[r, :]), extra=key_rope)
    head_norms(S, [q_job, k_job], turn, keep, act_first=square_kpe, dve_first=rotate_kpe,
               pool_side=query_sum)


def memory_branch(S, w, o_mem):
    nc, W = S.nc, S.W
    with ExitStack() as scope:
        def sb(name, shape, dt=F32):
            return scope.enter_context(nc.sbuf_tensor(name, shape, dt))
        qm = sb("mem_q", [P, MEM_HEADS, T])
        memT = sb("mem_t", [P, ND, M])
        mkv = sb("mem_kv", [P, 2 * MEM_HEADS, M])
        mv = sb("mem_v", [P, NM, MEM_HEADS, P])
        mhi, mlo = sb("mem_hi", [P, ND, M], F32R), sb("mem_lo", [P, ND, M], F32R)
        prob = [sb(f"mem_prob{i}", [P, M]) for i in range(3)]
        parts = sb("mem_factor_parts", [MEM_HEADS, 4, T], F32R)
        mem_loaded, turned, copied = S.sem("memory_loaded"), S.sem("memory_turned"), S.sem("memory_copied")
        tok = mkv[:, :, :].rearrange("p a t -> p (a t)").rearrange("p (i d) -> p i d", i=NM)

        def load_memory(sp):
            sp.dma_start(tok, w["mem"][0].rearrange("(i p) d -> p i d", p=P)).then_inc(mem_loaded, 16)

        def turn_memory(pe):
            pe.wait_ge(mem_loaded, 16)
            for c in range(ND):
                wait(pe, copied, c - 2)
                for i in range(NM):
                    last = pe.transpose(S.ps[4 + c % 3][:, i * P:(i + 1) * P], tok[:, i, c * P:(c + 1) * P], S.eye)
                last.then_inc(turned, 1)

        def keep_memory(act):
            for c in range(ND):
                act.wait_ge(turned, c + 1)
                act.activation(memT[:, c, :], S.ps[4 + c % 3][:, 0:M], ACT.Copy).then_inc(copied, 1)
        mem_norm = ModelNorm(S, memT, VEC["mem_norm_g"], mhi, mlo, tokens=NM)
        project(S, [(qm[:, n, :], P, ACT.Copy) for n in range(MEM_HEADS)], W.first["qmem"],
                (S.ahi, S.alo, T), None, [(mem_norm, t, 1 + t // 3) for t in range(ND)], pe_second=turn_memory,
                act_second=keep_memory, sp_first=load_memory)
        project(S, [(mkv[:, n, :], P, ACT.Copy) for n in range(2 * MEM_HEADS)], W.first["mkv"],
                (mhi, mlo, M), mem_norm)
        v_turned = S.sem("mem_v_turned")

        def turn(pe, h):
            for i in range(NM):
                last = pe.transpose(S.ps[5 + h // 2][:, (h % 2 * NM + i) * P:(h % 2 * NM + i + 1) * P],
                                    mkv[:, 2 * h + 1, i * P:(i + 1) * P], S.eye)
            if h % 2 == 1:
                last.then_inc(v_turned, 1)

        def keep(act, h):
            if h % 2 == 1:
                act.wait_ge(v_turned, h // 2 + 1)
                for a in range(2):
                    act.activation(mv[:, :, h - 1 + a, :], S.ps[5 + h // 2][:, a * M:(a + 1) * M].rearrange(
                        "p (i c) -> p i c", i=NM), ACT.Copy)

        head_norms(S, [
            HeadNorm(S, "mem_q_norm", MEM_HEADS, P, lambda g: qm[:, g, :], P, S.mq_gain[:, 0:1], 0,
                     (o_mem[:, 0, :], parts[:, 0, :], parts[:, 1, :])),
            HeadNorm(S, "mem_k_norm", MEM_HEADS, P, lambda g: mkv[:, 2 * g, :], P,
                     S.vec[:, VEC["mem_k_g"]:VEC["mem_k_g"] + 1], 1, (o_mem[:, 1, :], parts[:, 2, :], parts[:, 3, :]), tokens=NM,
                     work=MEM_HEADS)], turn, keep)
        softmax_attention(S, "mem", MEM_HEADS, lambda h: qm[:, h, :], lambda h: mkv[:, 2 * h, :],
                          lambda h, b: mv[:, b, h, :], NM, P, o_mem,
                          [S.scratch[:, 0:4, :], S.scratch[:, 4:8, :]], prob)


def mix_branches(S, w, o_attn, o_mem, norm2):
    nc, W = S.nc, S.W
    with ExitStack() as scope:
        def sb(name, shape, dt=F32):
            return scope.enter_context(nc.sbuf_tensor(name, shape, dt))
        ohi, olo = sb("o_hi", [P, 12, T], F32R), sb("o_lo", [P, 12, T], F32R)
        with ExitStack() as conv_scope:
            def sbc(name, shape, dt=F32):
                return conv_scope.enter_context(nc.sbuf_tensor(name, shape, dt))
            cc, z = sbc("conv_c", [P, T]), sbc("conv_z", [P, T + 2])
            gate, acc = sbc("conv_gate", [P, T]), sbc("conv_acc", [P, T])
            c_kept, gated, hi_done = S.sem("conv_c_kept"), S.sem("conv_gate_done"), S.sem("conv_hi_done")
            steps, tile_done, padded = S.sem("conv_steps"), S.sem("conv_tile_done"), S.sem("conv_padded")
            u0 = W.first["conv"]
            with nc.Block() as block:
                @block.sync
                def _(sp):
                    W.load(sp, u0 + 2 * RING, u0 + 16 + 2 * RING)

                @block.gpsimd
                def _(pool):
                    W.low(pool, u0 + RING, u0 + 16 + RING)

                @block.tensor
                def _(pe):
                    for t in range(4):
                        wait(pe, tile_done, t - 1)
                        for j in range(4):
                            u = u0 + 4 * t + j
                            pe.wait_ge(W.split_done, u + 1)
                            products(pe, S.ps[t % 2 * 4 + j][:, :], ((W.tile(u, k), (S.ahi[:, k, :], S.alo[:, k, :]))
                                                                     for k in range(ND))).then_inc(W.used, 1)

                @block.scalar
                def _(act):
                    for t in range(4):
                        b = S.ps[t % 2 * 4:t % 2 * 4 + 4]
                        act.wait_ge(W.used, u0 + 4 * t + 1)
                        wait(act, steps, 6 * (t - 1) + 1)
                        act.activation(cc[:, :], b[0][:, :], ACT.Copy).then_inc(c_kept, 1)
                        for j in range(3):
                            W.high(act, u0 + 4 * t + RING + j)
                        act.wait_ge(W.used, u0 + 4 * t + 4)
                        wait(act, tile_done, t)
                        act.activation(gate[:, :], b[3][:, :], ACT.Silu).then_inc(gated, 1)
                        act.wait_ge(steps, 6 * t + 6)
                        act.activation(ohi[:, 4 + t, :], acc[:, :], ACT.Copy).then_inc(hi_done, 1)
                        W.high(act, u0 + 4 * t + RING + 3)

                @block.vector
                def _(dve):
                    dve.memset(z[:, 0:1], 0.0).then_inc(padded, 1)
                    dve.memset(z[:, T + 1:T + 2], 0.0).then_inc(padded, 1)
                    dve.wait_ge(padded, 2)
                    n = 0

                    def step(ins):
                        nonlocal n
                        ins.then_inc(steps, 1)
                        n += 1
                        dve.wait_ge(steps, n)
                    for t in range(4):
                        b = S.ps[t % 2 * 4:t % 2 * 4 + 4]

                        def tap(k):
                            c = VEC["conv_w"] + 4 * k + t
                            return S.vec[:, c:c + 1]
                        c = VEC["conv_b"] + t
                        dve.wait_ge(c_kept, t + 1)
                        dve.wait_ge(W.used, u0 + 4 * t + 3)
                        step(dve.tensor_tensor(z[:, 1:T + 1], cc[:, :], b[1][:, :], ALU.mult))
                        step(dve.tensor_scalar(acc[:, :], z[:, 0:T], tap(0), S.vec[:, c:c + 1], ALU.mult, ALU.add))
                        for k in (1, 2):
                            step(dve.scalar_tensor_tensor(out=acc[:, :], in0=z[:, k:T + k], scalar=tap(k),
                                                          in1=acc[:, :], op0=ALU.mult, op1=ALU.add))
                        step(dve.tensor_tensor(acc[:, :], acc[:, :], b[2][:, :], ALU.mult))
                        dve.wait_ge(gated, t + 1)
                        step(dve.tensor_tensor(acc[:, :], acc[:, :], gate[:, :], ALU.mult))
                        dve.wait_ge(hi_done, t + 1)
                        dve.tensor_tensor(olo[:, 4 + t, :], acc[:, :], ohi[:, 4 + t, :].bitcast(F32),
                                          ALU.subtract).then_inc(tile_done, 1)
                        dve.wait_ge(tile_done, t + 1)
        u0 = W.first["gates"]
        silu = [sb(f"branch_gate{i}", [P, T]) for i in range(2)]
        silu_done, prod, hi2, lo2 = S.sem("gate_silu"), S.sem("gate_product"), S.sem("gate_hi"), S.sem("gate_lo")
        with nc.Block() as block:
            @block.sync
            def _(sp):
                W.load(sp, u0 + 2 * RING, u0 + 8 + 2 * RING)

            @block.gpsimd
            def _(pool):
                W.low(pool, u0 + RING, u0 + 8 + RING)

            @block.tensor
            def _(pe):
                for n in range(8):
                    pe.wait_ge(W.split_done, u0 + n + 1)
                    wait(pe, silu_done, n - 3)
                    products(pe, S.ps[n % 4][:, :], ((W.tile(u0 + n, k), (S.ahi[:, k, :], S.alo[:, k, :]))
                                                     for k in range(ND))).then_inc(W.used, 1)

            @block.scalar
            def _(act):
                for n in range(9):
                    if n < 8:
                        act.wait_ge(W.used, u0 + n + 1)
                        wait(act, prod, n - 1)
                        act.activation(silu[n % 2][:, :], S.ps[n % 4][:, :], ACT.Silu).then_inc(silu_done, 1)
                        W.high(act, u0 + n + RING)
                    if n >= 1:
                        o = o_attn if n <= 4 else o_mem
                        t = (n - 1) % 4
                        act.wait_ge(prod, n)
                        act.activation(ohi[:, (0 if n <= 4 else 8) + t, :], o[:, t, :], ACT.Copy).then_inc(hi2, 1)

            @block.vector
            def _(dve):
                for n in range(9):
                    if n < 8:
                        o, t = (o_attn if n < 4 else o_mem), n % 4
                        dve.wait_ge(silu_done, n + 1)
                        dve.tensor_tensor(o[:, t, :], o[:, t, :], silu[n % 2][:, :], ALU.mult).then_inc(prod, 1)
                    if n >= 1:
                        o, t = (o_attn if n <= 4 else o_mem), (n - 1) % 4
                        dve.wait_ge(hi2, n)
                        dve.wait_ge(prod, n)
                        c = (0 if n <= 4 else 8) + t
                        dve.tensor_tensor(olo[:, c, :], o[:, t, :], ohi[:, c, :].bitcast(F32),
                                          ALU.subtract).then_inc(lo2, 1)
        u0 = W.first["mix"]
        rt = [sb(f"mix_r{i}", [P, T]) for i in range(2)]
        tmp = sb("mix_term", [P, T])
        r_done, gated, summed = S.sem("mix_r_done"), S.sem("mix_gated"), S.sem("mix_summed")
        with nc.Block() as block:
            @block.sync
            def _(sp):
                W.load(sp, u0 + 2 * RING, u0 + 48 + 2 * RING)

            @block.gpsimd
            def _(pool):
                W.low(pool, u0 + RING, u0 + 48 + RING)

            @block.tensor
            def _(pe):
                for i in rounds(pe, 4):
                    for j in range(12):
                        m, kind = divmod(j, 6)
                        branch = kind // 2
                        pe.wait_ge(W.split_done, i * 12 + (u0 + j + 1))
                        if kind % 2 == 0:
                            wait(pe, r_done, i * 6 + (3 * m + branch - 2))
                            pairs = ((W.tile(u0 + j, k), (S.ahi[:, k, :], S.alo[:, k, :])) for k in range(ND))
                        else:
                            wait(pe, gated, i * 6 + (3 * m + branch - 2))
                            pairs = ((W.tile(u0 + j, k), (ohi[:, 4 * branch + k, :], olo[:, 4 * branch + k, :]))
                                     for k in range(4))
                        products(pe, S.ps[kind][:, :], pairs).then_inc(W.used, 1)

            @block.scalar
            def _(act):
                for i in rounds(act, 4):
                    for j in range(6):
                        m, b = divmod(j, 3)
                        act.wait_ge(W.used, i * 12 + (u0 + 2 * j + 1))
                        wait(act, gated, i * 6 + (j - 2))
                        c = VEC["b_gate"] + 8 * b + m
                        bias = S.vec[:, c:c + 1] if isinstance(i, int) else S.vec[:, bass.ds(i * 2 + c, 1)]
                        act.activation(S.mix_r[b][:, :], S.ps[2 * b][:, :], ACT.Sigmoid, bias=bias).then_inc(r_done, 1)
                        W.high(act, u0 + 2 * j + RING, i, 12)
                        W.high(act, u0 + 2 * j + 1 + RING, i, 12)

            @block.vector
            def _(dve):
                for i in rounds(dve, 8):
                    y = S.scratch[:, i, :] if isinstance(i, int) else \
                        S.scratch[:, bass.ds(i, 1), :].rearrange("p a t -> p (a t)")
                    for b in range(3):
                        dve.wait_ge(W.used, i * 6 + (u0 + 2 * b + 2))
                        dve.wait_ge(r_done, i * 3 + (b + 1))
                        wait(dve, summed, i * 2 + (b - 1))
                        dst = y if b == 0 else tmp[:, :]
                        dve.tensor_tensor(dst, S.mix_r[b][:, :], S.ps[2 * b + 1][:, :], ALU.mult).then_inc(gated, 1)
                        if b:
                            dve.wait_ge(gated, i * 3 + (b + 1))
                            dve.tensor_tensor(y, y, tmp[:, :], ALU.add).then_inc(summed, 1)
    return add_to_x(S, W.first["out"], S.ahi, S.alo, norm2, split=S.scratch)


def stick_breaking(S, norm, later):
    nc, W = S.nc, S.W
    with ExitStack() as scope:
        def sb(name, shape, dt=F32):
            return scope.enter_context(nc.sbuf_tensor(name, shape, dt))
        qkv = sb("sb_qkv", [P, 24, T])
        v_tok = sb("sb_v_tok", [P, NT, D])
        stay = [sb(f"sb_stay{i}", [P, T]) for i in range(2)]
        beta = [sb(f"sb_beta{i}", [P, T]) for i in range(2)]
        left = [sb(f"sb_left{i}", [P, T + 1]) for i in range(2)]
        zeros = sb("sb_zeros", [P, T])
        project_loop(S, W.first["qkv"], [(qkv, ACT.Copy, 24)], S.ahi, S.alo, norm)
        turned, kept, zeroed = S.sem("sb_v_turned"), S.sem("sb_v_kept"), S.sem("sb_zeroed")

        def set_constants(pool):
            pool.memset(zeros[:, :], 0.0).then_inc(zeroed, 1)
            for l in left:
                pool.memset(l[:, T:T + 1], 1.0).then_inc(zeroed, 1)

        def turn_v(pe, c):
            wait(pe, kept, c - 2)
            for i in range(NT):
                last = pe.transpose(S.ps[5 + c % 3][:, i * P:(i + 1) * P], qkv[:, 16 + c, i * P:(i + 1) * P], S.eye)
            last.then_inc(turned, 1)

        def keep_v(act, c):
            act.wait_ge(turned, c + 1)
            act.activation(v_tok[:, :, c * P:(c + 1) * P], S.ps[5 + c % 3][:, :].rearrange("p (i c) -> p i c", i=NT),
                           ACT.Copy).then_inc(kept, 1)

        pick_done = S.sem("sb_pick_done")
        n_rows = 2 * ND

        def pick(dve):
            for c in range(2):
                eye = S.eye[0:n_rows, c * 8:c * 8 + 8].unsqueeze(2).to_broadcast([n_rows, 8, 64])
                dve.tensor_copy(S.ahi[0:n_rows, 2 + c, :].rearrange("p (a t) -> p a t", t=64), eye).then_inc(pick_done, 1)

        def job(name, first, bank):
            g = VEC[f"{name}_gain_2"]
            return HeadNorm(S, f"{name}_norm", ND, SB_DIM, lambda t: qkv[:, first + t, :], P, S.vec[:, g:g + 1], bank,
                            (beta[bank], S.ahi[:, bank, :], S.alo[:, bank, :]), halves=lambda t: S.ahi[0:n_rows, 2 + t // 4, t % 4 * P:(t % 4 + 1) * P])
        head_norms(S, [job("sb_q", 0, 0), job("sb_k", ND, 1)], turn_v, keep_v, dve_first=pick,
                   pe_last=lambda pe: pe.wait_ge(pick_done, 2), pool_side=set_constants)
        items = [(h, i) for h in range(SB_HEADS) for i in range(NT)]
        pt = [S.scratch[:, 0:4, :], S.scratch[:, 4:8, :]]
        names = ("scored", "masked", "sigmoids", "scanned", "weighted", "turned2", "kept2", "summed", "out_hi", "out_lo")
        scored, masked, sig, scanned, weighted, turned2, kept2, summed, out_hi, out_lo = (S.sem(f"sb_{x}") for x in names)
        score_banks, turn_banks, out_banks = S.ps[0:3], S.ps[3:5], S.ps[5:7]
        scale = SB_DIM ** -0.5
        N = len(items)
        with nc.Block() as block:
            @block.tensor
            def _(pe):
                def score(n):
                    h, i = items[n]
                    r = slice(h % 2 * 64, h % 2 * 64 + 64)
                    wait(pe, sig, 2 * (n - 2))
                    pe.matmul(score_banks[n % 3][:, 0:(i + 1) * P], qkv[r, h // 2, i * P:(i + 1) * P],
                              qkv[r, 8 + h // 2, 0:(i + 1) * P], start=True, stop=True).then_inc(scored, 1)

                def turn(n):
                    h, i = items[n]
                    wait(pe, kept2, n - 1)
                    pe.wait_ge(weighted, n + 1)
                    a = T - (i + 1) * P
                    for b in range(i + 1):
                        last = pe.transpose(turn_banks[n % 2][:, b * P:(b + 1) * P],
                                            beta[n % 2][:, a + b * P:a + (b + 1) * P], S.eye)
                    last.then_inc(turned2, 1)

                def weigh(h):
                    o = h // 2
                    wait(pe, out_lo, o - 1)
                    pe.wait_ge(kept2, NT * (h + 1))
                    r = h % 2 * 64
                    for b in range(NT):
                        last = pe.matmul(out_banks[o % 2][r:r + 64, b * P:T], v_tok[:, b, h * 64:(h + 1) * 64],
                                         pt[h % 2][:, b, b * P:T], start=b == 0, stop=b == NT - 1)
                    last.then_inc(summed, 1)
                score(0)
                score(1)
                for n in range(N):
                    if n + 2 < N:
                        score(n + 2)
                    turn(n)
                    if n >= 5 and (n - 5) % NT == 0:
                        weigh((n - 5) // NT)
                weigh(SB_HEADS - 1)

            @block.vector
            def _(dve):
                def mask(n):
                    h, i = items[n]
                    dve.wait_ge(scored, n + 1)
                    diag = score_banks[n % 3][:, i * P:(i + 1) * P]
                    dve.tensor_tensor(diag, diag, S.const[:, K_CAUSAL:K_CAUSAL + P], ALU.add).then_inc(masked, 1)

                def weigh(n):
                    h, i = items[n]
                    a = T - (i + 1) * P
                    dve.wait_ge(sig, 2 * n + 1)
                    wait(dve, weighted, n - 1)
                    rev = slice(None, None, -1)
                    dve.tensor_tensor_scan(left[n % 2][:, a:T][:, rev], stay[n % 2][:, a:T][:, rev], zeros[:, a:T],
                                           1.0, ALU.mult, ALU.add).then_inc(scanned, 1)
                    dve.wait_ge(scanned, n + 1)
                    dve.wait_ge(sig, 2 * n + 2)
                    dve.tensor_tensor(beta[n % 2][:, a:T], beta[n % 2][:, a:T], left[n % 2][:, a + 1:T + 1],
                                      ALU.mult).then_inc(weighted, 1)

                def lower(o):
                    dve.wait_ge(out_hi, o + 1)
                    dve.tensor_tensor(S.alo[:, o, :], out_banks[o % 2][:, :], S.ahi[:, o, :].bitcast(F32),
                                      ALU.subtract).then_inc(out_lo, 1)
                mask(0)
                for n in range(N):
                    if n + 1 < N:
                        mask(n + 1)
                    weigh(n)
                    if n >= 8 and (n - 8) % 8 == 7:
                        lower((n - 8) // 8)
                lower(SB_HEADS // 2 - 1)

            @block.scalar
            def _(act):
                def keep(n):
                    h, i = items[n]
                    act.wait_ge(turned2, n + 1)
                    wait(act, summed, h - 1)
                    act.activation(pt[h % 2][:, 0:i + 1, i * P:(i + 1) * P],
                                   turn_banks[n % 2][:, 0:(i + 1) * P].rearrange("p (b t) -> p b t", b=i + 1),
                                   ACT.Copy).then_inc(kept2, 1)

                def put(o):
                    act.wait_ge(summed, 2 * (o + 1))
                    act.activation(S.ahi[:, o, :], out_banks[o % 2][:, :], ACT.Copy).then_inc(out_hi, 1)
                for n in range(N):
                    h, i = items[n]
                    a = T - (i + 1) * P
                    src = score_banks[n % 3][:, 0:(i + 1) * P]
                    act.wait_ge(masked, n + 1)
                    wait(act, turned2, n - 1)
                    act.activation(stay[n % 2][:, a:T], src, ACT.Sigmoid, scale=-scale).then_inc(sig, 1)
                    act.activation(beta[n % 2][:, a:T], src, ACT.Sigmoid, scale=scale).then_inc(sig, 1)
                    if n >= 2:
                        keep(n - 2)
                    if n >= 7 and (n - 7) % 8 == 7:
                        put((n - 7) // 8)
                keep(N - 2)
                keep(N - 1)
                put(SB_HEADS // 2 - 1)
        return add_to_x(S, W.first["sbo"], S.ahi, S.alo, later)


def mlp(S, layer, norm, make_norm):
    nc, W = S.nc, S.W
    later = make_norm() if make_norm else None
    with ExitStack() as scope:
        def sb(name, shape, dt=F32):
            return scope.enter_context(nc.sbuf_tensor(f"{name}{layer}", shape, dt))
        hhi = [sb(f"hidden_hi{i}_", [P, 4, T], F32R) for i in range(2)]
        hlo = [sb(f"hidden_lo{i}_", [P, 4, T], F32R) for i in range(2)]
        relu = [sb(f"hidden_relu{i}_", [P, T]) for i in range(4)]
        squ = [sb(f"hidden_square{i}_", [P, T]) for i in range(4)]
        names = ("relu_done", "hi_done", "square_done", "lo_done", "added")
        relu_done, hi_done, square_done, lo_done, added = (S.shared(f"mlp_{x}")[0] for x in names)
        tiles0, sums0 = 32 * layer, 64 * layer
        u0 = W.first[f"mlp{layer}head"]
        GROUPS = 8

        def order(eng, up, down):
            up(0, 0, u0, 0)
            for i in eng_rounds(eng, 3):
                b = u0 + 4
                up(i, 1, b, 1)
                down(i, 0, b + 4, 0)
                up(i, 2, b + 8, 0)
                down(i, 1, b + 12, 1)
            b = u0 + 52
            up(0, 7, b, 1)
            down(0, 6, b + 4, 0)
            down(0, 7, b + 8, 1)

        eng_rounds = rounds

        with nc.Block() as block:
            @block.sync
            def _(sp):
                W.load(sp, u0 + 2 * RING, u0 + 64 + 2 * RING)

            @block.gpsimd
            def _(pool):
                W.low(pool, u0 + RING, u0 + 64 + RING)

            @block.tensor
            def _(pe):
                def up(i, c, b, half):
                    for r in range(4):
                        pe.wait_ge(W.split_done, i * 16 + (b + r + 1))
                        wait(pe, relu_done, i * 8 + (tiles0 + 4 * c + r - 3))
                        first = isinstance(i, int) and c == 0 and r == 0
                        products(pe, S.ps[r][:, :], ((W.tile(b + r, k), (S.ahi[:, k, :], S.alo[:, k, :]))
                                                     for k in range(ND)), norm.ready(pe) if first else None
                                 ).then_inc(W.used, 1)

                def down(i, c, b, half):
                    wait(pe, lo_done, i * 8 + (tiles0 + 4 * c + 4))
                    for r in range(4):
                        pe.wait_ge(W.split_done, i * 16 + (b + r + 1))
                        wait(pe, added, i * 16 + (sums0 + 8 * c + 2 * r - 2))
                        for m in range(2):
                            last = products(pe, S.ps[4 + r % 2 * 2 + m][:, :],
                                            ((W.tile(b + r, k, m * P, P, 256), (hhi[half][:, k, :], hlo[half][:, k, :]))
                                             for k in range(4)))
                        last.then_inc(W.used, 1)
                        if later is not None and c == 7 and r >= 1:
                            later.sum_tile(pe, 2 * r - 2)
                            later.sum_tile(pe, 2 * r - 1)
                norm.pe_spread(pe)
                order(pe, up, down)
                if later is not None:
                    later.sum_tile(pe, ND - 2)
                    later.sum_tile(pe, ND - 1)

            @block.scalar
            def _(act):
                def up(i, c, b, half):
                    for r in range(4):
                        act.wait_ge(W.used, i * 16 + (b + r + 1))
                        wait(act, lo_done, i * 8 + (tiles0 + 4 * c + r - 3))
                        act.activation(relu[r][:, :], S.ps[r][:, :], ACT.Relu).then_inc(relu_done, 1)
                        act.wait_ge(relu_done, i * 8 + (tiles0 + 4 * c + r + 1))
                        act.activation(hhi[half][:, r, :], relu[r][:, :], ACT.Square).then_inc(hi_done, 1)
                        W.high(act, b + r + RING, i, 16)

                def down(i, c, b, half):
                    for r in range(4):
                        act.wait_ge(W.used, i * 16 + (b + r + 1))
                        W.high(act, b + r + RING, i, 16)
                        if later is not None and c == 7:
                            for t in (2 * r, 2 * r + 1):
                                act.wait_ge(added, sums0 + 8 * c + t + 1)
                                later.square_tile(act, t)
                norm.act_root(act)
                norm.act_high(act)
                order(act, up, down)

            @block.vector
            def _(dve):
                def up(i, c, b, half):
                    for r in range(4):
                        dve.wait_ge(relu_done, i * 8 + (tiles0 + 4 * c + r + 1))
                        wait(dve, lo_done, i * 8 + (tiles0 + 4 * c + r - 3))
                        dve.tensor_tensor(squ[r][:, :], relu[r][:, :], relu[r][:, :], ALU.mult).then_inc(square_done, 1)
                        dve.wait_ge(hi_done, i * 8 + (tiles0 + 4 * c + r + 1))
                        dve.wait_ge(square_done, i * 8 + (tiles0 + 4 * c + r + 1))
                        dve.tensor_tensor(hlo[half][:, r, :], squ[r][:, :], hhi[half][:, r, :].bitcast(F32),
                                          ALU.subtract).then_inc(lo_done, 1)

                def down(i, c, b, half):
                    for r in range(4):
                        dve.wait_ge(W.used, i * 16 + (b + r + 1))
                        for m in range(2):
                            t = 2 * r + m
                            wait(dve, added, i * 16 + (sums0 + 8 * c + t - 7))
                            dve.tensor_tensor(S.x[:, t, :], S.x[:, t, :], S.ps[4 + r % 2 * 2 + m][:, :],
                                              ALU.add).then_inc(added, 1)
                norm.dve_apply(dve)
                order(dve, up, down)
    return later


def hgrn(S, norm, later):
    nc, W = S.nc, S.W
    with ExitStack() as scope:
        def sb(name, shape, dt=F32):
            return scope.enter_context(nc.sbuf_tensor(name, shape, dt))
        qs, fs, vs, gs = (sb(f"hg_{x}", [P, ND, T]) for x in ("q", "f", "v", "g"))
        extra = sb("hg_factors", [P, 5, T])
        st = [sb(f"hg_scores{i}", [P, NT, P]) for i in range(2)]
        project_loop(S, W.first["hgin"], [(qs, ACT.Silu, 8), (fs, ACT.Sigmoid, 8), (vs, ACT.Copy, 8),
                                          (gs, ACT.Sigmoid, 8)], S.ahi, S.alo, norm)
        turned, kept, forget = S.sem("hg_v_turned"), S.sem("hg_v_kept"), S.sem("hg_forget")
        with nc.Block() as block:
            @block.vector
            def _(dve):
                dve.tensor_scalar(S.lb1[:, :], S.lb[:, :], -1.0, 1.0, ALU.mult, ALU.add).then_inc(forget, 1)
                dve.wait_ge(forget, 1)
                for h in range(HG_HEADS):
                    dve.tensor_scalar(fs[:, h, :], fs[:, h, :], S.lb1[:, h:h + 1], S.lb[:, h:h + 1], ALU.mult,
                                      ALU.add).then_inc(forget, 1)

            @block.tensor
            def _(pe):
                for h in range(HG_HEADS):
                    wait(pe, kept, h - 3)
                    for c in range(NT):
                        last = pe.transpose(S.ps[h % 4][:, c * P:(c + 1) * P], vs[:, h, c * P:(c + 1) * P], S.eye)
                    last.then_inc(turned, 1)

            @block.scalar
            def _(act):
                for h in range(HG_HEADS):
                    act.wait_ge(turned, h + 1)
                    act.activation(vs[:, h, :], S.ps[h % 4][:, :], ACT.Copy).then_inc(kept, 1)
        t = [S.scratch[:, n, :] for n in range(ND)] + [extra[:, n, :] for n in range(5)]
        pre, suf, ql, kl = t[0:2], t[2:4], (t[4:6], t[6:8]), (t[8:10], t[10:12])
        state = t[12][:, 0:3 * P].rearrange("p (c v) -> p c v", c=3)
        names = ("zeroed", "key", "suffix", "prefix", "q_ready", "k_ready", "scored", "picked", "k_turned", "k_kept",
                 "update", "totals", "stated", "out", "out_kept", "first")
        (zeroed, key, suffix, prefix, q_ready, k_ready, scored, picked, k_turned, k_kept, update, totalled, stated,
         out, out_kept, first) = (S.sem(f"hg_{x}") for x in names)
        totals = S.columns(HG_HEADS * NT)
        H = HG_HEADS
        LAST = LEVELS

        def done(h, n):
            return h // 2 * 16 + n * 2 + h % 2 + 1

        def halves(ap, level):
            v = ap.rearrange("p (b s h) -> p b s h", s=2, h=1 << level)
            return v[:, :, 0, :], v[:, :, 1, :]

        with nc.Block() as block:
            @block.gpsimd
            def _(pool):
                for b in (*kl[0], *kl[1]):
                    pool.memset(b, 0.0).then_inc(zeroed, 1)
                pool.wait_ge(zeroed, 4)
                for p in range(H // 2):
                    for n in range(LAST + 1):
                        for h in (2 * p, 2 * p + 1):
                            s = h % 2
                            pool.wait_ge(prefix, done(h, n))
                            if n >= 2:
                                pool.wait_ge(scored, done(h, n - 1))
                            elif p >= 1:
                                pool.wait_ge(out, h - 1)
                            q, k = ql[s][n % 2], kl[s][n % 2]
                            if n < LAST:
                                qr, pr = halves(qs[:, h, :], n)[1], halves(pre[s], n)[1]
                                kleft, ul = halves(fs[:, h, :], n)[0], halves(suf[s], n)[0]
                                q, k = halves(q, n)[1], halves(k, n)[0]
                            else:
                                qr, pr, kleft, ul = qs[:, h, :], pre[s], fs[:, h, :], suf[s]
                            pool.tensor_tensor(k, kleft, ul, ALU.mult).then_inc(k_ready, 1)
                            pool.tensor_tensor(q, qr, pr, ALU.mult).then_inc(q_ready, 1)

            @block.vector
            def _(dve):
                def start(h):
                    s = h % 2
                    if h >= 2:
                        dve.wait_ge(q_ready, done(h - 2, LAST))
                        dve.wait_ge(totalled, h - 1)
                    dve.memset(suf[s], 1.0).then_inc(suffix, 1)
                    dve.tensor_copy(pre[s], fs[:, h, :]).then_inc(first, 1)
                    dve.wait_ge(first, h + 1)
                    dve.tensor_scalar(fs[:, h, :], fs[:, h, :], -1.0, 1.0, ALU.mult, ALU.add).then_inc(key, 1)
                    dve.wait_ge(key, h + 1)
                    dve.wait_ge(suffix, done(h, 0))
                    dve.sem_inc(prefix, 1)

                def grow(h, level):
                    s, d = h % 2, 1 << level
                    dve.wait_ge(q_ready, done(h, level))
                    dve.wait_ge(prefix, done(h, level))
                    ul, _ = halves(suf[s], level)
                    pl, pr = halves(pre[s], level)
                    total = pr[:, :, d - 1:d].to_broadcast([P, T // (2 * d), d])
                    dve.tensor_tensor(ul, ul, total, ALU.mult).then_inc(suffix, 1)
                    dve.wait_ge(suffix, done(h, level + 1))
                    ltotal = pl[:, :, d - 1:d].to_broadcast([P, T // (2 * d), d])
                    dve.tensor_tensor(pr, pr, ltotal, ALU.mult).then_inc(prefix, 1)

                def total(h):
                    dve.wait_ge(prefix, done(h, LAST))
                    ends = pre[h % 2].rearrange("p (c t) -> p c t", c=NT)[:, :, P - 1]
                    dve.tensor_copy(totals[:, h * NT:(h + 1) * NT], ends).then_inc(totalled, 1)

                def pick(h, step):
                    dve.wait_ge(scored, done(h, step))
                    n = done(h, step) - 1
                    s = h % 2
                    if step == 0:
                        wait(dve, out, h - 1)
                        bank = S.ps[n % 3][:, :].rearrange("p (c t) -> p c t", c=NT)
                        m = S.const[:, K_EYE:K_EYE + P].unsqueeze(1).to_broadcast([P, NT, P])
                        dve.tensor_tensor(st[s][:, :, :], bank, m, ALU.mult).then_inc(picked, 1)
                    else:
                        level = step - 1
                        dve.wait_ge(picked, done(h, step - 1))
                        d, nb = 1 << level, 64 >> level
                        a = K_LEVEL + level * P
                        bank = S.ps[n % 3][:, 0:T // 2].rearrange("p (c b t) -> p c b t", c=NT, t=d)
                        m = S.const[:, a:a + P].bitcast(I32).rearrange("p (b s t) -> p b s t", s=2, t=d)[:, :, 1, :]
                        dst = st[s][:, :, :].rearrange("p c (b s t) -> p c b s t", s=2, t=d)[:, :, :, 1, :]
                        dve.copy_predicated(dst, m.unsqueeze(1).to_broadcast([P, NT, nb, d]),
                                            bank).then_inc(picked, 1)

                def states(h):
                    dve.wait_ge(update, h + 1)
                    wait(dve, out, h)
                    dve.wait_ge(totalled, h + 1)
                    dve.tensor_copy(state[:, 0, :], S.ps[3][:, 0:P]).then_inc(stated, 1)
                    for c in (1, 2):
                        dve.wait_ge(stated, 3 * h + c)
                        dve.scalar_tensor_tensor(out=state[:, c, :], in0=state[:, c - 1, :],
                                                 scalar=totals[:, h * NT + c:h * NT + c + 1],
                                                 in1=S.ps[3][:, c * P:(c + 1) * P], op0=ALU.mult,
                                                 op1=ALU.add).then_inc(stated, 1)
                start(0)
                start(1)
                for p in range(H // 2):
                    pair = (2 * p, 2 * p + 1)
                    for level in range(LEVELS):
                        for h in pair:
                            grow(h, level)
                        for h in pair:
                            pick(h, level)
                    for h in pair:
                        total(h)
                    for h in pair:
                        pick(h, LEVELS)
                    if p + 1 < H // 2:
                        start(2 * p + 2)
                        start(2 * p + 3)
                    for h in pair:
                        states(h)

            @block.tensor
            def _(pe):
                def score(h, step):
                    n, s = done(h, step) - 1, h % 2
                    wait(pe, picked, n - 2)
                    if step == 0:
                        pe.wait_ge(key, h + 1)
                        q, k = qs[:, h, :], fs[:, h, :]
                    else:
                        pe.wait_ge(k_ready, done(h, step - 1))
                        pe.wait_ge(q_ready, done(h, step - 1))
                        q, k = ql[s][(step - 1) % 2], kl[s][(step - 1) % 2]
                    for c in range(NT):
                        cols = slice(c * P, (c + 1) * P)
                        if step == 0:
                            to, src = S.ps[n % 3][:, cols], q[:, cols]
                        else:
                            d = 1 << (step - 1)
                            to = S.ps[n % 3][:, c * 64:(c + 1) * 64].rearrange("p (b t) -> p b t", t=d)
                            src = q[:, cols].rearrange("p (b s t) -> p b s t", s=2, t=d)[:, :, 1, :]
                        last = pe.matmul(to, k[:, cols], src, start=True, stop=True)
                    last.then_inc(scored, 1)

                for h in (0, 1):
                    score(h, 0)
                for p in range(H // 2):
                    pair = (2 * p, 2 * p + 1)
                    for step in range(1, LEVELS + 1):
                        for h in pair:
                            score(h, step)
                    for h in pair:
                        pe.wait_ge(k_ready, done(h, LAST))
                        for c in range(NT):
                            last = pe.transpose(S.ps[4 + h % 2][:, c * P:(c + 1) * P],
                                                kl[h % 2][LAST % 2][:, c * P:(c + 1) * P], S.eye)
                        last.then_inc(k_turned, 1)
                    if p + 1 < H // 2:
                        for h in (2 * p + 2, 2 * p + 3):
                            score(h, 0)
                    for h in pair:
                        pe.wait_ge(k_kept, h + 1)
                        wait(pe, stated, 3 * h)
                        for c in range(NT - 1):
                            last = pe.matmul(S.ps[3][:, c * P:(c + 1) * P], fs[:, h, c * P:(c + 1) * P],
                                             vs[:, h, c * P:(c + 1) * P], start=True, stop=True)
                        last.then_inc(update, 1)
                        wait(pe, out_kept, h - 1)
                        pe.wait_ge(picked, done(h, LEVELS))
                        pe.wait_ge(q_ready, done(h, LAST))
                        bank = S.ps[6 + h % 2]
                        for c in range(NT):
                            if c:
                                pe.wait_ge(stated, 3 * h + c)
                            cols = bank[:, c * P:(c + 1) * P]
                            last = pe.matmul(cols, vs[:, h, c * P:(c + 1) * P], st[h % 2][:, c, :], start=True,
                                             stop=c == 0)
                            if c:
                                last = pe.matmul(cols, state[:, c - 1, :], ql[h % 2][LAST % 2][:, c * P:(c + 1) * P],
                                                 start=False, stop=True)
                        last.then_inc(out, 1)

            @block.scalar
            def _(act):
                for p in range(H // 2):
                    for h in (2 * p, 2 * p + 1):
                        act.wait_ge(k_turned, h + 1)
                        act.activation(fs[:, h, :], S.ps[4 + h % 2][:, :], ACT.Copy).then_inc(k_kept, 1)
                    for h in (2 * p, 2 * p + 1):
                        act.wait_ge(out, h + 1)
                        act.activation(qs[:, h, :], S.ps[6 + h % 2][:, :], ACT.Copy).then_inc(out_kept, 1)
        prod, hi_done, lo_done = S.sem("hg_gated"), S.sem("hg_gated_hi"), S.sem("hg_gated_lo")

        def gate(dve, g):
            job.wait(dve, "applied", g + 1)
            dve.tensor_tensor(qs[:, g, :], qs[:, g, :], gs[:, g, :], ALU.mult).then_inc(prod, 1)

        def high(act):
            for t in range(ND):
                act.wait_ge(prod, t + 1)
                act.activation(S.ahi[:, t, :], qs[:, t, :], ACT.Copy).then_inc(hi_done, 1)

        def low(pool):
            for t in range(ND):
                pool.wait_ge(prod, t + 1)
                pool.wait_ge(hi_done, t + 1)
                pool.tensor_tensor(S.alo[:, t, :], qs[:, t, :], S.ahi[:, t, :].bitcast(F32),
                                   ALU.subtract).then_inc(lo_done, 1)
        g = VEC["hg_norm_gain_2"]
        job = HeadNorm(S, "hg_out_norm", ND, P, lambda t: qs[:, t, :], P, S.vec[:, g:g + 1], 0, (extra[:, 0, :], S.ahi[:, ND - 1, :], S.alo[:, ND - 1, :]),
                       rotate=gate)
        head_norms(S, [job], act_last=high, pool_side=low)
        return add_to_x(S, W.first["hgo"], S.ahi, S.alo, later)


def store(S, out):
    nc = S.nc
    turned, copied, stored = S.sem("out_turned"), S.sem("out_copied"), S.sem("out_stored")
    with nc.Block() as block:
        tok = S.scratch[:, :, :].rearrange("p a t -> p (a t)").rearrange("p (i d) -> p i d", i=NT)

        @block.tensor
        def _(pe):
            for n in range(2 * NT):
                i, half = divmod(n, 2)
                wait(pe, copied, n - 3)
                for c in range(4):
                    last = pe.transpose(S.ps[n % 4][:, c * P:(c + 1) * P], S.x[:, half * 4 + c, i * P:(i + 1) * P], S.eye)
                last.then_inc(turned, 1)

        @block.scalar
        def _(act):
            for n in range(2 * NT):
                i, half = divmod(n, 2)
                act.wait_ge(turned, n + 1)
                act.activation(tok[:, i, half * T:(half + 1) * T], S.ps[n % 4][:, :], ACT.Copy).then_inc(copied, 1)

        @block.sync
        def _(sp):
            for i in range(NT):
                sp.wait_ge(copied, 2 * (i + 1))
                sp.dma_start(out[0, i * P:(i + 1) * P, :], tok[:, i, :]).then_inc(stored, 16)
            sp.wait_ge(stored, 16 * NT)


def build(nc, w, consts, out):
    with ExitStack() as ctx:
        S = State()
        S.nc = nc
        S.sb = lambda name, shape, dt: ctx.enter_context(nc.sbuf_tensor(name, shape, dt))
        S.sem = lambda name: ctx.enter_context(nc.semaphore(name))
        S.W = Weights(nc, S.sb, S.sem, w)
        S.ps = [ctx.enter_context(nc.psum_tensor(f"bank{i}", [P, T], F32)) for i in range(8)]
        S.x = S.sb("x_t", [P, ND, T], F32)
        S.ahi, S.alo = S.sb("a_hi", [P, ND, T], F32R), S.sb("a_lo", [P, ND, T], F32R)
        S.scratch = S.sb("scratch", [P, ND, T], F32)
        S.const = S.sb("const", [P, K_COLS], F32)
        S.vec = S.sb("vec", [P, P], F32)
        S.q_gain, S.mq_gain = S.sb("q_gain", [P, 1], F32), S.sb("mq_gain", [P, 1], F32)
        S.eye_r = S.sb("eye_r", [ND, ND], F32R)
        S.lb, S.lb1 = S.sb("lower_bound", [P, ND], F32), S.sb("one_less_bound", [P, ND], F32)
        S.cos, S.sin = S.sb("cos", [P, T], F32), S.sb("sin", [P, T], F32)
        S.kpe_sq = S.sb("kpe_sq", [P, T], F32)
        S.mix_r = [S.cos, S.sin, S.kpe_sq]
        S.eye, S.ones = S.const[:, K_EYE:K_EYE + P], S.const[:, K_ONE:K_ONE + P]
        shared = {}

        def share(name):
            if name not in shared:
                shared[name] = [S.sem(name), 0]
            return tuple(shared[name])

        def advance(name, n):
            shared[name][1] += n
        S.shared, S.advance = share, advance
        small = S.sb("small_columns", [P, 1100], F32)
        S.used_columns = 0

        def columns(n):
            S.used_columns += n
            assert S.used_columns <= 1100
            return small[:, S.used_columns - n:S.used_columns]
        S.columns = columns
        def x_norm(gain, sum_bank=7):
            return ModelNorm(S, S.x, gain, S.ahi, S.alo, sum_bank=sum_bank)
        g2 = VEC["norm_gains_2"]
        norm1 = x_norm(VEC["norm_g"])
        setup(S, w, consts, norm1)
        norm = first_block(S, w, norm1, lambda: x_norm(g2))
        norm = stick_breaking(S, norm, lambda: x_norm(g2 + 8))
        norm = mlp(S, 0, norm, lambda: x_norm(g2 + 16, sum_bank=0))
        norm = hgrn(S, norm, lambda: x_norm(g2 + 24))
        mlp(S, 1, norm, None)
        store(S, out)


_INS = ["x", "mem", "positions", "norm_g", "w_in", "b_gate", "q_norm_g", "w_uq", "kv_norm_g", "w_ukv", "q_head_g",
        "k_head_g", "conv_w", "conv_b", "mem_norm_g", "w_mkv", "mem_q_g", "mem_k_g", "w_br_attn", "w_br_conv",
        "w_br_mem", "w_out", "norm_gains_2", "sb_w_qkv_2", "sb_q_gain_2", "sb_k_gain_2", "sb_w_o_2", "hg_w_in_2",
        "hg_lb_logits_2", "hg_norm_gain_2", "hg_w_o_2", "mlp_w1_2", "mlp_w2_2"]


def kernel(**inputs):
    import numpy as _np
    import concourse.bacc as _bacc
    from concourse import mybir as _mybir
    from concourse.bass_utils import run_bass_kernel_spmd as _run

    nc = _bacc.Bacc("TRN2", target_bir_lowering=False, num_devices=1)
    arrays, w = {}, {}
    for name in _INS:
        a = _np.ascontiguousarray(inputs[name])
        arrays[f"in_{name}"] = a
        w[name] = nc.dram_tensor(f"in_{name}", a.shape, _mybir.dt.from_np(a.dtype), kind="ExternalInput").ap()
    c = shape_constants()
    arrays["in_consts"] = c
    consts = nc.dram_tensor("in_consts", c.shape, _mybir.dt.float32, kind="ExternalInput").ap()
    out = nc.dram_tensor("out_0", (1, T, D), _mybir.dt.float32, kind="ExternalOutput").ap()
    build(nc, w, consts, out)
    r = _run(nc, [arrays], core_ids=[0])
    return r.results[0]["out_0"]
```
